# Optimizing a Trainium2 kernel written in Bass

```python
import jax, jax.numpy as jnp
from jax import lax
import numpy as np
import jax
import jax.numpy as jnp

D_MODEL = 1024
BATCH = 1
SEQ = 256
DEPTH = 2

N_MIXERS = 2
CONV_WIDTH = 3
ATTN_GROUPS = ((128, 1), (512, 4), (2048, 16))
N_GROUPS = len(ATTN_GROUPS)
HEADS_PER_GROUP = 5
HEAD_DIM = 64
ATTN_WIDTH = N_GROUPS * HEADS_PER_GROUP * HEAD_DIM
ROPE_THETA = 10000.0
D_FF = 2816
N_EXPERTS = 8
TOP_K = 2
D_FF_EXPERT = 2816
RMS_EPS = 1e-6
N_EVEN = (DEPTH + 1) // 2
N_ODD = DEPTH // 2


def rms_norm(x, g):
    xf = x.astype(jnp.float32)
    y = xf * lax.rsqrt(jnp.mean(xf * xf, axis=-1, keepdims=True) + RMS_EPS)
    return (y * g.astype(jnp.float32)).astype(x.dtype)

def ada_params(c, w, b):
    mod = jax.nn.silu(c) @ w + b
    shift, scale, gate = jnp.split(mod, 3, axis=-1)
    return shift[:, None, :], scale[:, None, :], gate[:, None, :]

def modulated_residual(x, c, g, w_mod, b_mod, fn):
    shift, scale, gate = ada_params(c, w_mod, b_mod)
    h = rms_norm(x, g) * (1 + scale) + shift
    return x + gate * fn(h)

def rope(x, positions):
    inv_freq = ROPE_THETA ** (-jnp.arange(0, HEAD_DIM, 2, dtype=jnp.float32) / HEAD_DIM)
    ang = positions.astype(jnp.float32)[..., None] * inv_freq
    cos, sin = jnp.cos(ang)[:, :, None, :], jnp.sin(ang)[:, :, None, :]
    xf = x.astype(jnp.float32)
    x1, x2 = jnp.split(xf, 2, axis=-1)
    return jnp.concatenate([x1 * cos - x2 * sin, x2 * cos + x1 * sin], axis=-1).astype(x.dtype)

def short_conv_mixer(h, w_in, conv_w, w_out):
    b_gate, c_gate, u = jnp.split(h @ w_in, 3, axis=-1)
    v = c_gate * u
    conv = lax.conv_general_dilated(
        v, conv_w.astype(v.dtype)[:, None, :], window_strides=(1,),
        padding=[(CONV_WIDTH - 1, 0)], dimension_numbers=('NWC', 'WIO', 'NWC'),
        feature_group_count=v.shape[-1])
    return (b_gate * conv) @ w_out

def dilated_group_attention(q, k, v, dilation, steps):
    b, s, nh, dh = q.shape
    chunk = dilation * steps
    sp = -(-s // chunk) * chunk
    nb = sp // chunk
    pad = [(0, 0), (0, sp - s), (0, 0), (0, 0)]

    def to_blocks(t):
        return jnp.pad(t, pad).reshape(b, nb, steps, dilation, nh, dh)

    def with_prev(t):
        prev = jnp.pad(t[:, :-1], [(0, 0), (1, 0), (0, 0), (0, 0), (0, 0), (0, 0)])
        return jnp.concatenate([prev, t], axis=2)

    qb = to_blocks(q)
    kk = with_prev(to_blocks(k))
    vv = with_prev(to_blocks(v))
    scores = jnp.einsum('bnqrhd,bnkrhd->bnrhqk', qb, kk,
                        preferred_element_type=jnp.float32) * (dh ** -0.5)
    a = jnp.arange(steps)[:, None]
    j = jnp.arange(2 * steps)[None, :]
    band = (j >= a) & (j <= a + steps)
    not_first = jnp.arange(nb)[:, None, None] > 0
    valid = band[None] & (not_first | (j >= steps)[None])
    scores = jnp.where(valid[None, :, None, None], scores, -jnp.inf)
    lse = jax.nn.logsumexp(scores, axis=-1)
    p = jnp.exp(scores - lse[..., None])
    o = jnp.einsum('bnrhqk,bnkrhd->bnqrhd', p.astype(v.dtype), vv)
    o = o.reshape(b, sp, nh, dh)[:, :s]
    lse = lse.transpose(0, 1, 4, 2, 3).reshape(b, sp, nh)[:, :s]
    return o, lse

def dilated_attention_mixer(h, positions, w_qkv, w_o):
    b, s, _ = h.shape
    nh = N_GROUPS * HEADS_PER_GROUP
    qkv = (h @ w_qkv).reshape(b, s, 3, nh, HEAD_DIM)
    q = rope(qkv[:, :, 0], positions).reshape(b, s, N_GROUPS, HEADS_PER_GROUP, HEAD_DIM)
    k = rope(qkv[:, :, 1], positions).reshape(b, s, N_GROUPS, HEADS_PER_GROUP, HEAD_DIM)
    v = qkv[:, :, 2].reshape(b, s, N_GROUPS, HEADS_PER_GROUP, HEAD_DIM)
    outs, lses = [], []
    for g, (window, dil) in enumerate(ATTN_GROUPS):
        o, l = dilated_group_attention(q[:, :, g], k[:, :, g], v[:, :, g], dil, window // dil)
        outs.append(o)
        lses.append(l)
    alpha = jax.nn.softmax(jnp.stack(lses, axis=2), axis=2)
    o = jnp.stack(outs, axis=2) * alpha[..., None].astype(h.dtype)
    return o.reshape(b, s, ATTN_WIDTH) @ w_o

def swiglu(h, w_gate, w_up, w_down):
    return (jax.nn.silu(h @ w_gate) * (h @ w_up)) @ w_down

def moe_swiglu(h, w_router, w_gate, w_up, w_down):
    logits = jnp.einsum('bsd,de->bse', h, w_router, preferred_element_type=jnp.float32)
    top_val, top_idx = lax.top_k(logits, TOP_K)
    top_w = jax.nn.softmax(top_val, axis=-1)
    gates = jnp.sum(jax.nn.one_hot(top_idx, N_EXPERTS, dtype=jnp.float32) * top_w[..., None],
                    axis=-2).astype(h.dtype)
    out = jnp.zeros_like(h)
    for e in range(N_EXPERTS):
        out = out + gates[..., e:e + 1] * swiglu(h, w_gate[e], w_up[e], w_down[e])
    return out

def first_inputs(seed: int = 0) -> dict:
    key = jax.random.key(seed)
    ks = jax.random.split(key, 20)
    D, F, FE, E = D_MODEL, D_FF, D_FF_EXPERT, N_EXPERTS

    def w(k, shape, fan_in, scale=1.0):
        return jax.random.normal(k, shape, jnp.float32) * (scale * fan_in ** -0.5)

    offsets = jax.random.randint(ks[2], (BATCH, 1), 0, 1024, dtype=jnp.int32)
    return {
        "x": jax.random.normal(ks[0], (BATCH, SEQ, D), jnp.float32),
        "c": jax.random.normal(ks[1], (BATCH, D), jnp.float32),
        "positions": offsets + jnp.arange(SEQ, dtype=jnp.int32)[None, :],
        "mod_w": w(ks[3], (DEPTH, 2, D, 3 * D), D, 0.5),
        "mod_b": 0.02 * jax.random.normal(ks[4], (DEPTH, 2, 3 * D), jnp.float32),
        "norm_g": 1.0 + 0.05 * jax.random.normal(ks[5], (DEPTH, 2, D), jnp.float32),
        "conv_w_in": w(ks[6], (N_EVEN, D, 3 * D), D),
        "conv_w": w(ks[7], (N_EVEN, CONV_WIDTH, D), CONV_WIDTH),
        "conv_w_out": w(ks[8], (N_EVEN, D, D), D),
        "ffn_w_gate": w(ks[9], (N_EVEN, D, F), D),
        "ffn_w_up": w(ks[10], (N_EVEN, D, F), D),
        "ffn_w_down": w(ks[11], (N_EVEN, F, D), F),
        "attn_w_qkv": w(ks[12], (N_ODD, D, 3 * ATTN_WIDTH), D),
        "attn_w_o": w(ks[13], (N_ODD, ATTN_WIDTH, D), ATTN_WIDTH),
        "router_w": w(ks[14], (N_ODD, D, E), D),
        "moe_w_gate": w(ks[15], (N_ODD, E, D, FE), D),
        "moe_w_up": w(ks[16], (N_ODD, E, D, FE), D),
        "moe_w_down": w(ks[17], (N_ODD, E, FE, D), FE),
        "final_g": 1.0 + 0.05 * jax.random.normal(ks[18], (D,), jnp.float32),
    }

def first_block(x, c, positions, mod_w, mod_b, norm_g, conv_w_in, conv_w, conv_w_out,
              ffn_w_gate, ffn_w_up, ffn_w_down, attn_w_qkv, attn_w_o, router_w,
              moe_w_gate, moe_w_up, moe_w_down, final_g):
    c = c.astype(x.dtype)
    for i in range(DEPTH):
        j = i // N_MIXERS
        if i % N_MIXERS == 0:
            mixer = lambda h, j=j: short_conv_mixer(h, conv_w_in[j], conv_w[j], conv_w_out[j])
            channel = lambda h, j=j: swiglu(h, ffn_w_gate[j], ffn_w_up[j], ffn_w_down[j])
        else:
            mixer = lambda h, j=j: dilated_attention_mixer(h, positions, attn_w_qkv[j], attn_w_o[j])
            channel = lambda h, j=j: moe_swiglu(h, router_w[j], moe_w_gate[j], moe_w_up[j],
                                                moe_w_down[j])
        x = modulated_residual(x, c, norm_g[i, 0], mod_w[i, 0], mod_b[i, 0], mixer)
        x = modulated_residual(x, c, norm_g[i, 1], mod_w[i, 1], mod_b[i, 1], channel)
    return rms_norm(x, final_g)


CTX_LEN = 256
GRID_W = 64
N_EVEN_2 = (DEPTH + 1) // 2
N_ODD_2 = DEPTH // 2
EPS = 1e-6

ML_HEADS = 4
ML_DQK = 128
ML_DV = 128
ML_CHUNK = 64
ML_QK_W = ML_HEADS * ML_DQK
ML_W = ML_HEADS * ML_DV
ML_GATES = 4 * ML_HEADS

GLA_HEADS = 4
GLA_DK = 64
GLA_DV = 128
GLA_LR = 16
GLA_TAU = 16.0
GLA_CHUNK = 32
GLA_QK_W = GLA_HEADS * GLA_DK
GLA_W = GLA_HEADS * GLA_DV

MIX_W = ML_W + GLA_W
IN_SIZES = (ML_QK_W, ML_QK_W, ML_W, ML_W, ML_GATES, GLA_QK_W, GLA_QK_W, GLA_W, GLA_W, 2 * GLA_LR)
IN_WIDTH = sum(IN_SIZES)

RW_HEAD = 64
RW_HEADS = D_MODEL // RW_HEAD
RW_DECAY_LR = 64
RW_A_LR = 64
RW_G_LR = 128
RW_LN_EPS = 64e-5


def split_points(sizes):
    pts, acc = [], 0
    for s in sizes[:-1]:
        acc += s
        pts.append(acc)
    return pts

def rmsnorm(x, g):
    xf = x.astype(jnp.float32)
    y = xf * lax.rsqrt(jnp.mean(xf * xf, axis=-1, keepdims=True) + EPS)
    return (y * g.astype(jnp.float32)).astype(x.dtype)

def head_rmsnorm(y, g, n_heads):
    bn, L, W = y.shape
    d = W // n_heads
    return rmsnorm(y.reshape(bn, L, n_heads, d), g.reshape(n_heads, d)).reshape(bn, L, W)

def head_layernorm(y, w, b, n_heads, out_dtype):
    bn, L, W = y.shape
    yf = y.astype(jnp.float32).reshape(bn, L, n_heads, W // n_heads)
    mu = jnp.mean(yf, axis=-1, keepdims=True)
    var = jnp.mean(jnp.square(yf - mu), axis=-1, keepdims=True)
    yn = ((yf - mu) * lax.rsqrt(var + RW_LN_EPS)).reshape(bn, L, W)
    return (yn * w.astype(jnp.float32) + b.astype(jnp.float32)).astype(out_dtype)

def modulate(h, shift, scale):
    return h * (1 + scale) + shift

def to_heads(t, n_heads):
    bn, L, W = t.shape
    return t.reshape(bn, L, n_heads, W // n_heads).transpose(0, 2, 1, 3)

def from_heads(t):
    bn, H, L, d = t.shape
    return t.transpose(0, 2, 1, 3).reshape(bn, L, H * d)

def to_chunks(t, chunk):
    bn, H, L = t.shape[:3]
    t = t.reshape((bn, H, L // chunk, chunk) + t.shape[3:])
    return jnp.moveaxis(t, 2, 0)

def from_chunks(t):
    t = jnp.moveaxis(t, 0, 2)
    return t.reshape(t.shape[:2] + (-1,) + t.shape[4:])

def short_conv(x, w, b):
    xp = jnp.pad(x, ((0, 0), (1, 1), (0, 0)))
    return xp[:, :-2] * w[0] + xp[:, 1:-1] * w[1] + xp[:, 2:] * w[2] + b

def dwconv_grid(h, w, b, grid):
    rows, width = grid
    bn, L, F = h.shape
    img = h.reshape(bn, rows, width, F)
    out = lax.conv_general_dilated(img, w[:, :, None, :].astype(h.dtype), window_strides=(1, 1), padding="SAME",
                                   dimension_numbers=("NHWC", "HWIO", "NHWC"), feature_group_count=F)
    return out.reshape(bn, L, F) + b

def grid_shift(x, grid):
    rows, width = grid
    bn, L, D = x.shape
    q = D // 4
    p = jnp.pad(x.reshape(bn, rows, width, D), ((0, 0), (1, 1), (1, 1), (0, 0)))
    out = jnp.concatenate([p[:, 1:-1, :-2, :q], p[:, 1:-1, 2:, q:2 * q],
                           p[:, :-2, 1:-1, 2 * q:3 * q], p[:, 2:, 1:-1, 3 * q:]], axis=-1)
    return out.reshape(bn, L, D)

def seq_shift(x):
    D = x.shape[-1]
    q = D // 4
    p = jnp.pad(x, ((0, 0), (1, 1), (0, 0)))
    prv, nxt = p[:, :-2], p[:, 2:]
    return jnp.concatenate([prv[..., :q], nxt[..., q:2 * q], prv[..., 2 * q:3 * q], nxt[..., 3 * q:]], axis=-1)

def bidir_scan(scan_fn, init, ctx_fwd, ctx_bwd, lat_fwd, lat_bwd):
    flip = lambda args: tuple(jnp.flip(a, axis=2) for a in args)
    y_cf, s_f = scan_fn(*ctx_fwd, init)
    y_cb, s_b = scan_fn(*flip(ctx_bwd), init)
    y_lf, _ = scan_fn(*lat_fwd, s_f)
    y_lb, _ = scan_fn(*flip(lat_bwd), s_b)
    return y_cf + jnp.flip(y_cb, axis=2), y_lf + jnp.flip(y_lb, axis=2)

def mlstm_scan(q, k, v, logi, logf, state):
    q, k, v, logi, logf = (t.astype(jnp.float32) for t in (q, k, v, logi, logf))
    mask = jnp.tril(jnp.ones((ML_CHUNK, ML_CHUNK), dtype=bool))

    def step(carry, blk):
        C, n, m = carry
        qc, kc, vc, ic, fc = blk
        b = jnp.cumsum(fc, axis=-1)
        inter = b + m[..., None]
        d = jnp.where(mask, b[..., :, None] - b[..., None, :] + ic[..., None, :], -jnp.inf)
        mt = jnp.maximum(inter, jnp.max(d, axis=-1))
        s = jnp.einsum("bhtd,bhsd->bhts", qc, kc) * jnp.exp(d - mt[..., None])
        wi = jnp.exp(inter - mt)
        num = jnp.einsum("bhts,bhsv->bhtv", s, vc) + wi[..., None] * jnp.einsum("bhtd,bhdv->bhtv", qc, C)
        den = jnp.sum(s, axis=-1) + wi * jnp.einsum("bhtd,bhd->bht", qc, n)
        h = num / jnp.maximum(jnp.abs(den), jnp.exp(-mt))[..., None]
        bl = b[..., -1]
        g = bl[..., None] - b + ic
        m_new = jnp.maximum(bl + m, jnp.max(g, axis=-1))
        ws = jnp.exp(g - m_new[..., None])
        wp = jnp.exp(bl + m - m_new)
        C = wp[..., None, None] * C + jnp.einsum("bhs,bhsd,bhsv->bhdv", ws, kc, vc)
        n = wp[..., None] * n + jnp.einsum("bhs,bhsd->bhd", ws, kc)
        return (C, n, m_new), h

    state, hs = lax.scan(step, state, tuple(to_chunks(t, ML_CHUNK) for t in (q, k, v, logi, logf)))
    return from_chunks(hs), state

def gla_scan(q, k, v, la, S):
    q, k, v, la = (t.astype(jnp.float32) for t in (q, k, v, la))
    mask = jnp.tril(jnp.ones((GLA_CHUNK, GLA_CHUNK), dtype=bool))[:, :, None]

    def step(S, blk):
        qc, kc, vc, ac = blk
        b = jnp.cumsum(ac, axis=2)
        decay = jnp.exp(jnp.where(mask, b[:, :, :, None, :] - b[:, :, None, :, :], -jnp.inf))
        A = jnp.einsum("bhtd,bhsd,bhtsd->bhts", qc, kc, decay)
        o = jnp.einsum("bhts,bhsv->bhtv", A, vc) + jnp.einsum("bhtd,bhdv->bhtv", qc * jnp.exp(b), S)
        bl = b[:, :, -1:, :]
        S = jnp.exp(bl[:, :, 0, :])[..., None] * S + jnp.einsum("bhsd,bhsv->bhdv", kc * jnp.exp(bl - b), vc)
        return S, o

    S, os_ = lax.scan(step, S, tuple(to_chunks(t, GLA_CHUNK) for t in (q, k, v, la)))
    return from_chunks(os_), S

def rwkv7_scan(r, w, k, v, kk, a, S):
    xs = tuple(jnp.moveaxis(t.astype(jnp.float32), 2, 0) for t in (r, w, k, v, kk, a))

    def step(S, inp):
        rt, wt, kt, vt, kkt, at = inp
        sa = jnp.einsum("bhvk,bhk->bhv", S, -kkt)
        S = S * wt[:, :, None, :] + sa[..., None] * (kkt * at)[:, :, None, :] + vt[..., None] * kt[:, :, None, :]
        return S, jnp.einsum("bhvk,bhk->bhv", S, rt)

    S, ys = lax.scan(step, S, xs)
    return jnp.moveaxis(ys, 0, 2), S

def even_project(h, w_in, b_gates, conv_w, conv_b, gla_w2, gla_b):
    bn, L, _ = h.shape
    z = h @ w_in
    mq, mk, mv, mo, mg, gq, gk, gv, gg, glr = jnp.split(z, split_points(IN_SIZES), axis=-1)
    qk = jax.nn.silu(short_conv(jnp.concatenate([mq, mk], axis=-1), conv_w, conv_b))
    mq, mk = jnp.split(qk, 2, axis=-1)
    mg = (mg + b_gates).astype(jnp.float32).reshape(bn, L, 4, ML_HEADS).transpose(2, 0, 3, 1)
    glr = glr.reshape(bn, L, 2, GLA_LR)
    la = jax.nn.log_sigmoid((jnp.einsum("blzr,zrc->zblc", glr, gla_w2) + gla_b[:, None, None, :]).astype(jnp.float32)) / GLA_TAU
    return {
        "mq": to_heads(mq * ML_DQK ** -0.5, ML_HEADS), "mk": to_heads(mk, ML_HEADS), "mv": to_heads(mv, ML_HEADS),
        "i_f": mg[0], "f_f": jax.nn.log_sigmoid(mg[1]), "i_b": mg[2], "f_b": jax.nn.log_sigmoid(mg[3]),
        "gq": to_heads(gq * GLA_DK ** -0.5, GLA_HEADS), "gk": to_heads(gk, GLA_HEADS), "gv": to_heads(gv, GLA_HEADS),
        "la_f": to_heads(la[0], GLA_HEADS), "la_b": to_heads(la[1], GLA_HEADS),
        "mo": mo, "gg": gg,
    }

def even_out(ml_y, gla_y, p, head_g, w_out):
    dt = p["mo"].dtype
    m = head_rmsnorm(from_heads(ml_y).astype(dt), head_g[:ML_W], ML_HEADS) * jax.nn.sigmoid(p["mo"])
    g = head_rmsnorm(from_heads(gla_y).astype(dt), head_g[ML_W:], GLA_HEADS) * jax.nn.silu(p["gg"])
    return jnp.concatenate([m, g], axis=-1) @ w_out

def even_mixer(hc, hl, w_in, b_gates, conv_w, conv_b, gla_w2, gla_b, head_g, w_out, need_ctx):
    pc = even_project(hc, w_in, b_gates, conv_w, conv_b, gla_w2, gla_b)
    pl = even_project(hl, w_in, b_gates, conv_w, conv_b, gla_w2, gla_b)
    bn = hl.shape[0]
    f32 = jnp.float32
    ml_init = (jnp.zeros((bn, ML_HEADS, ML_DQK, ML_DV), f32), jnp.zeros((bn, ML_HEADS, ML_DQK), f32),
               jnp.zeros((bn, ML_HEADS), f32))
    gla_init = jnp.zeros((bn, GLA_HEADS, GLA_DK, GLA_DV), f32)
    ml_args = lambda p: ((p["mq"], p["mk"], p["mv"], p["i_f"], p["f_f"]), (p["mq"], p["mk"], p["mv"], p["i_b"], p["f_b"]))
    gla_args = lambda p: ((p["gq"], p["gk"], p["gv"], p["la_f"]), (p["gq"], p["gk"], p["gv"], p["la_b"]))
    ml_c, ml_l = bidir_scan(mlstm_scan, ml_init, *ml_args(pc), *ml_args(pl))
    gla_c, gla_l = bidir_scan(gla_scan, gla_init, *gla_args(pc), *gla_args(pl))
    y_lat = even_out(ml_l, gla_l, pl, head_g, w_out)
    y_ctx = even_out(ml_c, gla_c, pc, head_g, w_out) if need_ctx else None
    return y_ctx, y_lat

def rwkv_project(h, shifted, mu, w_rkv, w0, w1, w2, a0, a1, a2, g1, g2, kvec):
    xx = shifted - h
    xr, xw, xk, xv, xa, xg = (h + xx * mu[i] for i in range(6))
    r = xr @ w_rkv[0]
    k = xk @ w_rkv[1]
    v = xv @ w_rkv[2]
    lw = jnp.einsum("zblr,zrd->zbld", jnp.tanh(jnp.einsum("bld,zdr->zblr", xw, w1)), w2) + w0[:, None, None, :]
    decay = jnp.exp(-jnp.exp(-jax.nn.softplus(-lw.astype(jnp.float32)) - 0.5))
    a = jax.nn.sigmoid(a0 + (xa @ a1) @ a2)
    g = jax.nn.sigmoid(xg @ g1) @ g2
    kk = to_heads(k * kvec[0], RW_HEADS).astype(jnp.float32)
    kk = kk / jnp.maximum(jnp.sqrt(jnp.sum(kk * kk, axis=-1, keepdims=True)), 1e-12)
    k = k * (1 + (a - 1) * kvec[1])
    return {"r": r, "k": k, "v": v, "a": a, "g": g, "decay": decay, "kk": kk}

def rwkv_out(y, p, kvec, lnx, w_o):
    r, k, v, g = p["r"], p["k"], p["v"], p["g"]
    bn, L, D = r.shape
    y = head_layernorm(from_heads(y), lnx[0], lnx[1], RW_HEADS, r.dtype)
    bonus = jnp.sum((r * k * kvec[2]).reshape(bn, L, RW_HEADS, RW_HEAD), axis=-1, keepdims=True) * v.reshape(bn, L, RW_HEADS, RW_HEAD)
    return ((y + bonus.reshape(bn, L, D)) * g) @ w_o

def rwkv_mixer(hc, hl, lat_grid, mu, w_rkv, w_o, w0, w1, w2, a0, a1, a2, g1, g2, kvec, lnx, need_ctx):
    pc = rwkv_project(hc, seq_shift(hc), mu, w_rkv, w0, w1, w2, a0, a1, a2, g1, g2, kvec)
    pl = rwkv_project(hl, grid_shift(hl, lat_grid), mu, w_rkv, w0, w1, w2, a0, a1, a2, g1, g2, kvec)
    init = jnp.zeros((hl.shape[0], RW_HEADS, RW_HEAD, RW_HEAD), jnp.float32)

    def scan_args(p):
        r, k, v, a = (to_heads(p[n], RW_HEADS) for n in ("r", "k", "v", "a"))
        return ((r, to_heads(p["decay"][0], RW_HEADS), k, v, p["kk"], a),
                (r, to_heads(p["decay"][1], RW_HEADS), k, v, p["kk"], a))

    y_c, y_l = bidir_scan(rwkv7_scan, init, *scan_args(pc), *scan_args(pl))
    out_l = rwkv_out(y_l, pl, kvec, lnx, w_o)
    out_c = rwkv_out(y_c, pc, kvec, lnx, w_o) if need_ctx else None
    return out_c, out_l

def conv_ffn(h, w_up, conv_w, conv_b, w_down, grid):
    gate, up = jnp.split(h @ w_up, 2, axis=-1)
    gate = dwconv_grid(gate, conv_w, conv_b, grid)
    return (jax.nn.gelu(gate, approximate=True) * up) @ w_down

def second_inputs(seed: int = 0) -> dict:
    key = jax.random.key(seed)
    keys = iter(jax.random.split(key, 48))

    def nrm(shape, scale):
        return jax.random.normal(next(keys), shape, jnp.float32) * scale

    def unif(shape, lo, hi):
        return jax.random.uniform(next(keys), shape, jnp.float32, lo, hi)

    D = D_MODEL
    gate_i = nrm((N_EVEN_2, 2, 1, ML_HEADS), 0.1)
    gate_f = jnp.linspace(3.0, 6.0, ML_HEADS, dtype=jnp.float32) + nrm((N_EVEN_2, 2, 1, ML_HEADS), 0.1)
    return {
        "x": nrm((BATCH, SEQ, D), 1.0),
        "c": nrm((BATCH, D), 1.0),
        "ctx": nrm((BATCH, CTX_LEN, D), 1.0),
        "c_ctx": nrm((D,), 1.0),
        "w_mod": nrm((DEPTH, D, 6 * D), 0.5 * D ** -0.5),
        "b_mod": nrm((DEPTH, 6 * D), 0.02),
        "norm_g": 1.0 + nrm((DEPTH, 4, D), 0.02),
        "ffn_w_up": nrm((DEPTH, D, 2 * D_FF), D ** -0.5),
        "ffn_conv_w": nrm((DEPTH, 3, 3, D_FF), 1.0 / 3.0),
        "ffn_conv_b": nrm((DEPTH, D_FF), 0.02),
        "ffn_w_down": nrm((DEPTH, D_FF, D), D_FF ** -0.5),
        "ev_w_in": nrm((N_EVEN_2, D, IN_WIDTH), D ** -0.5),
        "ev_b_gates": jnp.concatenate([gate_i, gate_f], axis=2).reshape(N_EVEN_2, ML_GATES),
        "ev_conv_w": nrm((N_EVEN_2, 3, 2 * ML_QK_W), 3 ** -0.5),
        "ev_conv_b": nrm((N_EVEN_2, 2 * ML_QK_W), 0.02),
        "ev_gla_w2": nrm((N_EVEN_2, 2, GLA_LR, GLA_QK_W), GLA_LR ** -0.5),
        "ev_gla_b": nrm((N_EVEN_2, 2, GLA_QK_W), 0.1),
        "ev_head_g": 1.0 + nrm((N_EVEN_2, MIX_W), 0.02),
        "ev_w_out": nrm((N_EVEN_2, MIX_W, D), MIX_W ** -0.5),
        "rw_mu": unif((N_ODD_2, 6, D), 0.0, 1.0),
        "rw_w_rkv": nrm((N_ODD_2, 3, D, D), D ** -0.5),
        "rw_w_o": nrm((N_ODD_2, D, D), D ** -0.5),
        "rw_w0": unif((N_ODD_2, 2, D), -6.0, 1.0),
        "rw_w1": nrm((N_ODD_2, 2, D, RW_DECAY_LR), D ** -0.5),
        "rw_w2": nrm((N_ODD_2, 2, RW_DECAY_LR, D), 0.1 * RW_DECAY_LR ** -0.5),
        "rw_a0": nrm((N_ODD_2, D), 0.1),
        "rw_a1": nrm((N_ODD_2, D, RW_A_LR), D ** -0.5),
        "rw_a2": nrm((N_ODD_2, RW_A_LR, D), 0.1 * RW_A_LR ** -0.5),
        "rw_g1": nrm((N_ODD_2, D, RW_G_LR), D ** -0.5),
        "rw_g2": nrm((N_ODD_2, RW_G_LR, D), RW_G_LR ** -0.5),
        "rw_kvec": jnp.stack([0.85 + nrm((N_ODD_2, D), 0.02), 1.0 + nrm((N_ODD_2, D), 0.02), nrm((N_ODD_2, D), 0.1)], axis=1),
        "rw_lnx": jnp.stack([1.0 + nrm((N_ODD_2, D), 0.02), nrm((N_ODD_2, D), 0.02)], axis=1),
    }

def second_block(x, c, ctx, c_ctx, w_mod, b_mod, norm_g, ffn_w_up, ffn_conv_w, ffn_conv_b, ffn_w_down,
              ev_w_in, ev_b_gates, ev_conv_w, ev_conv_b, ev_gla_w2, ev_gla_b, ev_head_g, ev_w_out,
              rw_mu, rw_w_rkv, rw_w_o, rw_w0, rw_w1, rw_w2, rw_a0, rw_a1, rw_a2, rw_g1, rw_g2, rw_kvec, rw_lnx):
    rows = x.shape[1] // GRID_W
    lat_grid = (rows, GRID_W)
    ctx_grid = (1, ctx.shape[1])
    xl, xc = x, ctx
    for layer in range(DEPTH):
        last = layer == DEPTH - 1
        j = layer // 2
        mod_l = jnp.split((jax.nn.silu(c) @ w_mod[layer] + b_mod[layer])[:, None, :], 6, axis=-1)
        mod_c = jnp.split((jax.nn.silu(c_ctx) @ w_mod[layer] + b_mod[layer])[None, None, :], 6, axis=-1)
        hl = modulate(rmsnorm(xl, norm_g[layer, 0]), mod_l[0], mod_l[1])
        hc = modulate(rmsnorm(xc, norm_g[layer, 0]), mod_c[0], mod_c[1])
        if layer % 2 == 0:
            yc, yl = even_mixer(hc, hl, ev_w_in[j], ev_b_gates[j], ev_conv_w[j], ev_conv_b[j], ev_gla_w2[j],
                                ev_gla_b[j], ev_head_g[j], ev_w_out[j], not last)
        else:
            yc, yl = rwkv_mixer(hc, hl, lat_grid, rw_mu[j], rw_w_rkv[j], rw_w_o[j], rw_w0[j], rw_w1[j], rw_w2[j],
                                rw_a0[j], rw_a1[j], rw_a2[j], rw_g1[j], rw_g2[j], rw_kvec[j], rw_lnx[j], not last)
        xl = xl + mod_l[2] * rmsnorm(yl, norm_g[layer, 1])
        hl = modulate(rmsnorm(xl, norm_g[layer, 2]), mod_l[3], mod_l[4])
        xl = xl + mod_l[5] * rmsnorm(conv_ffn(hl, ffn_w_up[layer], ffn_conv_w[layer], ffn_conv_b[layer],
                                              ffn_w_down[layer], lat_grid), norm_g[layer, 3])
        if not last:
            xc = xc + mod_c[2] * rmsnorm(yc, norm_g[layer, 1])
            hc = modulate(rmsnorm(xc, norm_g[layer, 2]), mod_c[3], mod_c[4])
            xc = xc + mod_c[5] * rmsnorm(conv_ffn(hc, ffn_w_up[layer], ffn_conv_w[layer], ffn_conv_b[layer],
                                                  ffn_w_down[layer], ctx_grid), norm_g[layer, 3])
    return xl


def setup_inputs(seed=0):
    out = dict(first_inputs(seed))
    for name, value in second_inputs(seed + 1).items():
        if name != "x":
            out[name + "_2"] = value
    return out


def reference(
    x, c, positions, mod_w, mod_b, norm_g, conv_w_in, conv_w, conv_w_out, ffn_w_gate, ffn_w_up,
    ffn_w_down, attn_w_qkv, attn_w_o, router_w, moe_w_gate, moe_w_up, moe_w_down, final_g, c_2,
    ctx_2, c_ctx_2, w_mod_2, b_mod_2, norm_g_2, ffn_w_up_2, ffn_conv_w_2, ffn_conv_b_2,
    ffn_w_down_2, ev_w_in_2, ev_b_gates_2, ev_conv_w_2, ev_conv_b_2, ev_gla_w2_2, ev_gla_b_2,
    ev_head_g_2, ev_w_out_2, rw_mu_2, rw_w_rkv_2, rw_w_o_2, rw_w0_2, rw_w1_2, rw_w2_2, rw_a0_2,
    rw_a1_2, rw_a2_2, rw_g1_2, rw_g2_2, rw_kvec_2, rw_lnx_2,
):
    x = first_block(
        x, c, positions, mod_w, mod_b, norm_g, conv_w_in, conv_w, conv_w_out, ffn_w_gate,
        ffn_w_up, ffn_w_down, attn_w_qkv, attn_w_o, router_w, moe_w_gate, moe_w_up, moe_w_down,
        final_g,
    )
    return second_block(
        x, c_2, ctx_2, c_ctx_2, w_mod_2, b_mod_2, norm_g_2, ffn_w_up_2, ffn_conv_w_2,
        ffn_conv_b_2, ffn_w_down_2, ev_w_in_2, ev_b_gates_2, ev_conv_w_2, ev_conv_b_2,
        ev_gla_w2_2, ev_gla_b_2, ev_head_g_2, ev_w_out_2, rw_mu_2, rw_w_rkv_2, rw_w_o_2,
        rw_w0_2, rw_w1_2, rw_w2_2, rw_a0_2, rw_a1_2, rw_a2_2, rw_g1_2, rw_g2_2, rw_kvec_2,
        rw_lnx_2,
    )


_drawn_inputs = setup_inputs


def setup_inputs(seed=0):
    import zlib

    import numpy as np

    out = dict(_drawn_inputs(seed))
    spreads = {}
    factors = {'ffn_conv_b_2': 6.811,
     'ev_conv_b_2': 33.261,
     'ev_gla_b_2': 4.989,
     'ev_head_g_2': 64.0,
     'rw_w1_2': 8.0,
     'rw_w2_2': 8.0,
     'rw_a0_2': 4.938,
     'rw_a1_2': 5.036,
     'rw_a2_2': 4.935}
    for name, (base, spread) in spreads.items():
        noise = np.random.default_rng([zlib.crc32(name.encode()), seed]).standard_normal(out[name].shape)
        drawn = base * np.exp(spread * noise) if base else spread * noise
        out[name] = jnp.asarray(drawn.astype(out[name].dtype))
    for name, factor in factors.items():
        out[name] = (out[name] * factor).astype(out[name].dtype)
    return out
```

```python
import numpy as np
import concourse.bass as bass
from concourse import mybir

F32 = mybir.dt.float32
I32 = mybir.dt.int32
U32 = mybir.dt.uint32
ALU = mybir.AluOpType
ACT = mybir.ActivationFunctionType
AX = mybir.AxisListType

P = 128
D = 1024
KD = D // P
S = 256
T = 2 * S
F = 2816
KF = F // P
NE = 8
NHEAD = 15
GROUPS = ((128, 1), (512, 4), (2048, 16))
EPS = 1e-6
RW_LINKS = 127
RING = 11
UT = 16
EXPERT_UNITS = (2 * KF * KD + KF * KD) // UT
LAT = slice(S, T)
CTX = slice(0, S)
GRID_W = 64
CH = 64
NB = T // P


def vec_layout():
    sizes = [("c", 8), ("c2", 16), ("norm_g", 32), ("mod_b", 96), ("final_g", 8), ("conv_w", 24),
             ("router", 64), ("hmask", 2), ("invf", 1),
             ("mod_b2", 96), ("norm_g2", 64), ("fcw", 2 * 9 * KF), ("fcb", 2 * KF),
             ("ecw", 24), ("ecb", 8), ("ebg", 2), ("glab", 4), ("headg", 8),
             ("mu", 48), ("lnx", 16)]
    at, out = 0, {}
    for name, n in sizes:
        out[name] = slice(at, at + n)
        at += n
    return out, at


VEC, NVEC = vec_layout()
U_ADA1 = 12
U_CONV_IN, U_SQ = 12, 4
U_UP, U_DOWN = 22, 11
U_ADA2 = 24
U_EV = 12
NCONST = 3 * P + 14 * P + P


class Signal:

    def __init__(self, nc, name):
        self.sem = nc.alloc_semaphore(name)
        self.base = 0

    def at(self, n):
        return self.base + n


class Link:

    def __init__(self, signal, eng):
        self.s, self.eng, self.n, self.turn, self.per = signal, eng, 0, None, 0

    def loop(self, turn, per):
        self.turn, self.per, self.start = turn, per, self.n

    def value(self):
        if self.turn is None:
            return self.s.base + self.n
        return self.turn * self.per + (self.s.base + self.n)

    def __call__(self, ins):
        self.mark(ins)
        self.eng.wait_ge(self.s.sem, self.value())

    def mark(self, ins):
        ins.then_inc(self.s.sem, 1)
        self.n += 1

    def wait(self):
        self.eng.wait_ge(self.s.sem, self.value())

    def end_loop(self, turns):
        assert self.n - self.start == self.per, f"{self.s.sem}: {self.n - self.start} a turn, not {self.per}"
        self.n = self.start + self.per * turns
        self.turn = None

    def close(self):
        self.s.base += self.n


class Kernel:

    def __init__(self, nc, aps):
        self.nc, self.a = nc, aps
        sb = lambda name, shape, dt=F32: nc.alloc_sbuf_tensor(name, shape, dt)
        self.ring = sb("ring", [P, RING, UT * P])
        self.X = sb("X", [P, KD, T])
        self.H = sb("H", [P, KD, T])
        self.W = sb("W", [P, 16384])
        self.vec = sb("vec", [P, NVEC])
        self.const = sb("const", [P, NCONST])
        self.mod1 = sb("mod1", [P, 4, 24])
        self.mod2 = sb("mod2", [P, 2, 48, 2])
        self.cs = sb("cs", [P, 24])
        self.sm = sb("sm", [P, 512])
        self.ps = nc.alloc_psum_tensor("ps", [P, 8, 512], F32)
        c = lambda i, n=1: self.const[:, i * P:(i + n) * P]
        self.ident, self.ones, self.prot = c(0), c(1), c(2)
        self.level = [c(3, 7), c(10, 7)]
        self.hblock = c(17)
        self.hat = sb("hat", [P, 4, P])
        self.cmask = sb("cmask", [P, 4 * P])
        self.stored = [nc.alloc_semaphore(f"stored_{i}") for i in range(4)]
        self.w_in = [nc.alloc_semaphore(f"weights_in_{i}") for i in range(RING)]
        self.unit = 0
        sig = lambda n: Signal(nc, n)
        self.mm = sig("matmul_done")
        self.act = sig("act_done")
        self.dve = sig("dve_done")
        self.pool = sig("pool_done")
        self.dma = sig("dma_done")
        self.pel = sig("tensor_order")
        self.actl = sig("act_order")
        self.dvel = sig("dve_order")
        self.pooll = sig("pool_order")

    def v(self, name, i=0, n=1):
        s = VEC[name].start + i
        return self.vec[:, s:s + n]

    def slot(self, u):
        return (self.unit + u) % RING

    def landed(self, u):
        return 16 * ((self.unit + u) // RING + 1)


def plan(owner):
    unit_done, out_done, signals, n = {}, {}, set(), 0
    for i, o in enumerate(owner):
        ends_unit = i % UT == UT - 1 or i == len(owner) - 1
        ends_out = i == len(owner) - 1 or owner[i + 1] != o
        if ends_unit or ends_out:
            n += 1
            signals.add(i)
        if ends_unit:
            unit_done[i // UT] = n
        if ends_out:
            out_done[o] = n
    return unit_done, out_done, signals, n


def refill(k, sp, unit_done, n_units, turn=None, per=0, total_units=None):
    for u in range(n_units):
        if turn is None:
            if k.unit + u + RING >= k.a["weights"].shape[0]:
                break
            sp.wait_ge(k.mm.sem, k.mm.at(unit_done[u]))
            src = k.a["weights"][k.unit + u + RING]
        else:
            sp.wait_ge(k.mm.sem, turn * per + k.mm.at(unit_done[u]))
            src = k.a["weights"][bass.ds(turn * n_units + (k.unit + u + RING), 1)].squeeze(0)
        sp.dma_start(k.ring[:, k.slot(u), :], src).then_inc(k.w_in[k.slot(u)], 16)


def gemm(k, pe, n_out, kt, rhs, out, before, signals, first=0, turn=None, rounds=0):
    for i in range(first, first + n_out * kt):
        o, kk = divmod(i - first, kt)
        u, p = divmod(i, UT)
        if p == 0 or i == first:
            need = k.landed(u)
            pe.wait_ge(k.w_in[k.slot(u)], need if turn is None else turn * (16 * rounds) + need)
        if kk == 0:
            before(o)
        mm = pe.matmul(out(o), lhsT=k.ring[:, k.slot(u), p * P:(p + 1) * P], rhs=rhs(kk),
                       start=kk == 0, stop=kk == kt - 1)
        if i in signals:
            mm.then_inc(k.mm.sem, 1)


def stage_load(k):
    nc = k.nc
    with nc.Block() as block:
        @block.sync
        def _(sp):
            sp.dma_start(k.vec[:, :], k.a["vectors"]).then_inc(k.dma.sem, 16)
            sp.dma_start(k.X[:, :, :], k.a["tokens"]).then_inc(k.dma.sem, 16)
            sp.dma_start(k.const[:, :], k.a["constants"]).then_inc(k.dma.sem, 16)
            for u in range(RING):
                sp.dma_start(k.ring[:, u, :], k.a["weights"][u]).then_inc(k.w_in[u], 16)
            sp.wait_ge(k.dma.sem, 48)

        @block.scalar
        def _(act):
            act.wait_ge(k.dma.sem, 48)
            act.activation(k.cs[:, :], k.vec[:, VEC["c"].start:VEC["c2"].stop], ACT.Silu).then_inc(k.act.sem, 1)
    k.dma.base += 48
    k.act.base += 1


def stage_ada1(k, first, count):
    nc = k.nc
    unit_done, out_done, signals, total = plan([i // KD for i in range(count * 24 * KD)])
    with nc.Block() as block:
        @block.sync
        def _(sp):
            refill(k, sp, unit_done, count * U_ADA1)

        @block.tensor
        def _(pe):
            gemm(k, pe, count * 24, KD, lambda kk: k.cs[:, kk:kk + 1],
                 lambda o: k.ps[:, 0, o:o + 1], lambda o: None, signals)

        @block.vector
        def _(dve):
            link = Link(k.dvel, dve)
            dve.wait_ge(k.mm.sem, k.mm.at(total))
            m = k.mod1[:, first:first + count, :]
            link(dve.tensor_tensor(m, k.ps[:, 0, 0:24 * count].rearrange("p (a b) -> p a b", b=24),
                                   k.v("mod_b", first * 24, 24 * count).rearrange("p (a b) -> p a b", b=24), ALU.add))
            link(dve.tensor_scalar(m[:, :, 8:16], m[:, :, 8:16], 1.0, None, ALU.add))
            for i in range(count):
                link(dve.tensor_tensor(m[:, i, 8:16], m[:, i, 8:16], k.v("norm_g", (first + i) * 8, 8), ALU.mult))
            link.close()
    k.mm.base += total
    k.unit += count * U_ADA1


def stage_ada2(k, layer):
    nc = k.nc
    unit_done, out_done, signals, total = plan([i // KD for i in range(48 * KD)])
    with nc.Block() as block:
        @block.sync
        def _(sp):
            refill(k, sp, unit_done, U_ADA2)

        @block.tensor
        def _(pe):
            gemm(k, pe, 48, KD, lambda kk: k.cs[:, 8 + 2 * kk:10 + 2 * kk],
                 lambda o: k.ps[:, 0, 2 * o:2 * o + 2], lambda o: None, signals)

        @block.vector
        def _(dve):
            link = Link(k.dvel, dve)
            dve.wait_ge(k.mm.sem, k.mm.at(total))
            m = k.mod2[:, layer, :, :]
            link(dve.tensor_tensor(m, k.ps[:, 0, 0:96].rearrange("p (a b) -> p a b", b=2),
                                   k.v("mod_b2", layer * 48, 48).unsqueeze(2).to_broadcast([P, 48, 2]), ALU.add))
            for vector, g in ((1, 0), (4, 2)):
                w = m[:, vector * 8:vector * 8 + 8, :]
                link(dve.tensor_scalar(w, w, 1.0, None, ALU.add))
                link(dve.tensor_tensor(w, w, k.v("norm_g2", layer * 32 + g * 8, 8).unsqueeze(2).to_broadcast([P, 8, 2]), ALU.mult))
            link.close()
    k.mm.base += total
    k.unit += U_ADA2


def rms_scale(k, block, src, n, scr, rstd, bank, eps=EPS):
    @block.scalar
    def _(act):
        for i in range(KD):
            act.activation(scr[:, i * n:(i + 1) * n], src(i), ACT.Square).then_inc(k.act.sem, 1)
        act.wait_ge(k.dve.sem, k.dve.at(1))
        act.activation(rstd, rstd, ACT.Sqrt).then_inc(k.act.sem, 1)

    @block.tensor
    def _(pe):
        for i in range(KD):
            pe.wait_ge(k.act.sem, k.act.at(i + 1))
            mm = pe.matmul(k.ps[:, bank, 0:n], lhsT=k.ones, rhs=scr[:, i * n:(i + 1) * n],
                           start=i == 0, stop=i == KD - 1)
        mm.then_inc(k.mm.sem, 1)

    @block.vector
    def _(dve):
        dve.wait_ge(k.mm.sem, k.mm.at(1))
        dve.tensor_scalar(rstd, k.ps[:, bank, 0:n], 1.0 / D, eps, ALU.mult, ALU.add).then_inc(k.dve.sem, 1)
        dve.wait_ge(k.act.sem, k.act.at(KD + 1))
        dve.reciprocal(rstd, rstd).then_inc(k.dve.sem, 1)


def rms_counts(k):
    k.act.base += KD + 1
    k.mm.base += 1
    k.dve.base += 2


def stage_norm(k, cols, scale, shift, dst=None):
    nc = k.nc
    n = cols.stop - cols.start
    halves = [c for c in (CTX, LAT) if c.start >= cols.start and c.stop <= cols.stop]
    dst = k.H if dst is None else dst
    rstd = k.W[:, 8 * T:8 * T + n]
    with nc.Block() as block:
        rms_scale(k, block, lambda i: k.X[:, i, cols], n, k.W, rstd, 7)
    rms_counts(k)
    with nc.Block() as block:
        @block.vector
        def _(dve):
            for i in range(KD):
                for h, c in enumerate(halves):
                    half = 0 if c is CTX else 1
                    r = rstd[:, c.start - cols.start:c.stop - cols.start]
                    dve.scalar_tensor_tensor(dst[:, i, c], k.X[:, i, c], scale(i, half), r,
                                             ALU.mult, ALU.mult).then_inc(k.dve.sem, 1)

        @block.scalar
        def _(act):
            if shift is None:
                return
            for i in range(KD):
                for h, c in enumerate(halves):
                    half = 0 if c is CTX else 1
                    act.wait_ge(k.dve.sem, k.dve.at(i * len(halves) + h + 1))
                    act.activation(dst[:, i, c], dst[:, i, c], ACT.Identity, bias=shift(i, half))
    k.dve.base += KD * len(halves)


def stage_norm1(k, i):
    m = k.mod1
    stage_norm(k, LAT, lambda t, h: m[:, i, 8 + t:9 + t], lambda t, h: m[:, i, t:t + 1])


def stage_conv_in(k):
    nc = k.nc
    n_out = 24
    Z = k.W[:, 0:n_out * S].rearrange("p (o t) -> p o t", o=n_out)
    tmp = k.W[:, n_out * S:n_out * S + 8 * S].rearrange("p (o t) -> p o t", o=8)
    unit_done, out_done, signals, total = plan([i // KD for i in range(n_out * KD)])
    with nc.Block() as block:
        @block.sync
        def _(sp):
            refill(k, sp, unit_done, U_CONV_IN)

        @block.tensor
        def _(pe):
            def before(o):
                if o >= 4:
                    pe.wait_ge(k.act.sem, k.act.at(o - 3))
            gemm(k, pe, n_out, KD, lambda kk: k.H[:, kk, LAT], lambda o: k.ps[:, o % 4, 0:S], before, signals)

        @block.scalar
        def _(act):
            for o in range(n_out):
                act.wait_ge(k.mm.sem, k.mm.at(out_done[o]))
                act.activation(Z[:, o, :], k.ps[:, o % 4, 0:S], ACT.Copy).then_inc(k.act.sem, 1)

        @block.vector
        def _(dve):
            link = Link(k.dvel, dve)
            for i in range(8):
                dve.wait_ge(k.act.sem, k.act.at(17 + i))
                v, y = Z[:, 16 + i, :], tmp[:, i, :]
                w = lambda j: k.v("conv_w", j * 8 + i)
                link(dve.tensor_tensor(v, v, Z[:, 8 + i, :], ALU.mult))
                link(dve.tensor_scalar(y, v, w(2), None, ALU.mult))
                link(dve.scalar_tensor_tensor(y[:, 1:S], v[:, 0:S - 1], w(1), y[:, 1:S], ALU.mult, ALU.add))
                link(dve.scalar_tensor_tensor(y[:, 2:S], v[:, 0:S - 2], w(0), y[:, 2:S], ALU.mult, ALU.add))
            dve.wait_ge(k.mm.sem, k.mm.at(total))
            for i in range(8):
                link.mark(dve.tensor_tensor(k.H[:, i, LAT], tmp[:, i, :], Z[:, i, :], ALU.mult))
            link.close()
    k.mm.base += total
    k.act.base += n_out
    k.unit += U_CONV_IN


def stage_out_residual(k, gate):
    nc = k.nc
    unit_done, out_done, signals, total = plan([i // KD for i in range(8 * KD)])
    with nc.Block() as block:
        @block.sync
        def _(sp):
            refill(k, sp, unit_done, U_SQ)

        @block.tensor
        def _(pe):
            def before(o):
                if o >= 4:
                    pe.wait_ge(k.dve.sem, k.dve.at(o - 3))
            gemm(k, pe, 8, KD, lambda kk: k.H[:, kk, LAT], lambda o: k.ps[:, o % 4, 0:S], before, signals)

        @block.vector
        def _(dve):
            for o in range(8):
                dve.wait_ge(k.mm.sem, k.mm.at(out_done[o]))
                dve.scalar_tensor_tensor(k.X[:, o, LAT], k.ps[:, o % 4, 0:S], gate(o), k.X[:, o, LAT],
                                         ALU.mult, ALU.add).then_inc(k.dve.sem, 1)
    k.mm.base += total
    k.dve.base += 8
    k.unit += U_SQ


def stage_swiglu(k, i, experts):
    nc = k.nc
    m = k.mod1
    owner = [t // KD for t in range(2 * KF * KD)] + [2 * KF + t // KF for t in range(KD * KF)]
    unit_done, out_done, signals, total = plan(owner)
    A = k.W[:, 0:KF * S].rearrange("p (o t) -> p o t", o=KF)
    sil = k.W[:, KF * S:(KF + 2) * S].rearrange("p (o t) -> p o t", o=2)
    tmp = k.W[:, (KF + 2) * S:(KF + 4) * S].rearrange("p (o t) -> p o t", o=2)
    G = k.W[:, 8192:8192 + NE * S].rearrange("p (e t) -> p e t", e=NE)
    down0 = 2 * KF
    per_dve = KF + 8
    units = EXPERT_UNITS
    rounds = units // RING
    with nc.Block() as block:
        @block.sync
        def _(sp):
            if experts == 1:
                refill(k, sp, unit_done, units)
            else:
                with sp.Fori(0, experts) as e:
                    refill(k, sp, unit_done, units, turn=e, per=total)

        @block.tensor
        def _(pe):
            def body(e):
                at = lambda s, n, per: s.at(n) if e is None else e * per + s.at(n)

                def before(o):
                    if o < 4:
                        if e is not None:
                            pe.wait_ge(k.dve.sem, at(k.dve, 0, per_dve))
                    elif o < down0 and o % 2 == 0:
                        pe.wait_ge(k.act.sem, at(k.act, o // 2 - 1, KF))
                    elif o < down0:
                        pe.wait_ge(k.dve.sem, at(k.dve, o // 2 - 1, per_dve))
                gemm(k, pe, down0, KD, lambda kk: k.H[:, kk, LAT], lambda o: k.ps[:, o % 4, 0:S],
                     before, signals, turn=e, rounds=rounds)

                def before_down(o):
                    pe.wait_ge(k.dve.sem, at(k.dve, KF if o < 4 else KF + o - 3, per_dve))
                gemm(k, pe, 8, KF, lambda kk: A[:, kk, :], lambda o: k.ps[:, o % 4, 0:S],
                     before_down, signals, first=down0 * KD, turn=e, rounds=rounds)
            if experts == 1:
                body(None)
            else:
                with pe.Fori(0, experts) as e:
                    body(e)

        @block.scalar
        def _(act):
            def body(e):
                at = lambda s, n, per: s.at(n) if e is None else e * per + s.at(n)
                for f in range(KF):
                    act.wait_ge(k.mm.sem, at(k.mm, out_done[2 * f], total))
                    if f >= 2:
                        act.wait_ge(k.dve.sem, at(k.dve, f - 1, per_dve))
                    act.activation(sil[:, f % 2, :], k.ps[:, (2 * f) % 4, 0:S], ACT.Silu).then_inc(k.act.sem, 1)
            if experts == 1:
                body(None)
            else:
                with act.Fori(0, experts) as e:
                    body(e)

        @block.vector
        def _(dve):
            link = Link(k.dvel, dve)

            def body(e):
                at = lambda s, n, per: s.at(n) if e is None else e * per + s.at(n)
                for f in range(KF):
                    dve.wait_ge(k.mm.sem, at(k.mm, out_done[2 * f + 1], total))
                    dve.wait_ge(k.act.sem, at(k.act, f + 1, KF))
                    dve.tensor_tensor(A[:, f, :], k.ps[:, (2 * f + 1) % 4, 0:S], sil[:, f % 2, :],
                                      ALU.mult).then_inc(k.dve.sem, 1)
                for o in range(8):
                    dve.wait_ge(k.mm.sem, at(k.mm, out_done[down0 + o], total))
                    x, gate = k.X[:, o, LAT], m[:, i, 16 + o:17 + o]
                    if e is None:
                        dve.scalar_tensor_tensor(x, k.ps[:, o % 4, 0:S], gate, x, ALU.mult, ALU.add).then_inc(k.dve.sem, 1)
                    else:
                        g = G[:, bass.ds(e, 1), :].rearrange("p a t -> p (a t)")
                        dve.scalar_tensor_tensor(tmp[:, o % 2, :], k.ps[:, o % 4, 0:S], gate, g,
                                                 ALU.mult, ALU.mult).then_inc(k.dve.sem, 1)
                        dve.wait_ge(k.dve.sem, at(k.dve, KF + o + 1, per_dve))
                        link(dve.tensor_tensor(x, x, tmp[:, o % 2, :], ALU.add))
            if experts == 1:
                body(None)
            else:
                with dve.Fori(0, experts) as e:
                    link.loop(e, 8)
                    body(e)
                    link.end_loop(experts)
            link.close()
    k.mm.base += total * experts
    k.act.base += KF * experts
    k.dve.base += per_dve * experts
    k.unit += units * experts


def stage_attention(k):
    nc = k.nc
    W = k.W
    q2 = W[:, 0:16 * S].rearrange("p (o t) -> p o t", o=16)
    kT = W[:, 16 * S:24 * S].rearrange("p (o t) -> p o t", o=8)
    V = W[:, 24 * S:24 * S + 2 * D].rearrange("p (b d) -> p b d", b=2)
    Pm = W[:, 8192:8192 + 30 * S].rearrange("p (h b s) -> p h b s", h=NHEAD, b=2)
    raw = W[:, 8192:8192 + 16 * S].rearrange("p (o t) -> p o t", o=16)
    HC = k.H[:, :, CTX]
    cos, sin, ang, kk_ = (HC[:, i, :] for i in range(4))
    rot, tmp = HC[:, 4, :], HC[:, 5, :]
    pos = HC[:, 6, :].bitcast(I32)

    owner = [t // KD for t in range(16 * KD)] + [16 + u for u in range(4) for _ in range(UT)]
    unit_done, out_done, signals, total = plan(owner)
    with nc.Block() as block:
        @block.sync
        def _(sp):
            sp.dma_start(pos, k.a["positions"]).then_inc(k.dma.sem, 16)
            refill(k, sp, unit_done, 12)

        @block.tensor
        def _(pe):
            def before(o):
                if o >= 4:
                    pe.wait_ge(k.act.sem, k.act.at(o - 3))
            gemm(k, pe, 16, KD, lambda kk: k.H[:, kk, LAT], lambda o: k.ps[:, o % 4, 0:S], before, signals)
            for u in range(4):
                pe.wait_ge(k.w_in[k.slot(8 + u)], k.landed(8 + u))
                pe.wait_ge(k.act.sem, k.act.at(13 + u))
                for b in range(2):
                    for kk in range(KD):
                        mm = pe.matmul(k.ps[:, u % 4, b * S:(b + 1) * S], lhsT=k.H[:, kk, S + b * P:S + (b + 1) * P],
                                       rhs=k.ring[:, k.slot(8 + u), kk * S:(kk + 1) * S], start=kk == 0, stop=kk == KD - 1)
                mm.then_inc(k.mm.sem, 1)

        @block.scalar
        def _(act):
            for o in range(16):
                act.wait_ge(k.mm.sem, k.mm.at(out_done[o]))
                act.activation(raw[:, o, :], k.ps[:, o % 4, 0:S], ACT.Copy).then_inc(k.act.sem, 1)
            for u in range(4):
                act.wait_ge(k.mm.sem, k.mm.at(out_done[16 + u]))
                act.activation(V[:, :, u * S:(u + 1) * S], k.ps[:, u, :].rearrange("p (b d) -> p b d", b=2),
                               ACT.Copy).then_inc(k.act.sem, 1)

        @block.vector
        def _(dve):
            link = Link(k.dvel, dve)
            two_pi = 2 * np.pi
            c1 = 6.28125
            c2 = float(np.float32(np.round((two_pi - c1) * 2 ** 21) / 2 ** 21))
            c3 = two_pi - c1 - c2
            magic = 1.5 * 2 ** 23
            dve.wait_ge(k.dma.sem, k.dma.at(16))
            link(dve.tensor_copy(ang, pos))
            link(dve.tensor_scalar(ang, ang, k.v("invf"), None, ALU.mult))
            link(dve.tensor_scalar(kk_, ang, 1 / two_pi, magic, ALU.mult, ALU.add))
            link(dve.tensor_scalar(kk_, kk_, magic, None, ALU.subtract))
            for c in (c1, c2, c3):
                link(dve.scalar_tensor_tensor(ang, kk_, -c, ang, ALU.mult, ALU.add))
            lim = 3.141592
            link(dve.tensor_scalar(sin, ang, lim, -lim, ALU.min, ALU.max))
            link(dve.tensor_scalar(cos, ang, np.pi / 2, None, ALU.add))
            link(dve.tensor_scalar(kk_, cos, np.pi, two_pi, ALU.is_gt, ALU.mult))
            link(dve.tensor_tensor(cos, cos, kk_, ALU.subtract))
            link(dve.tensor_scalar(cos, cos, lim, -lim, ALU.min, ALU.max))
            link.close()
    k.dma.base += 16
    k.mm.base += total
    k.act.base += 20
    k.unit += 12

    with nc.Block() as block:
        @block.tensor
        def _(pe):
            for o in range(16):
                if o >= 4:
                    pe.wait_ge(k.dve.sem, k.dve.at(o - 3))
                pe.matmul(k.ps[:, o % 4, 0:S], lhsT=k.prot, rhs=raw[:, o, :], start=True, stop=True).then_inc(k.mm.sem, 1)

        @block.scalar
        def _(act):
            act.activation(sin, sin, ACT.Sin).then_inc(k.act.sem, 1)
            act.activation(cos, cos, ACT.Sin).then_inc(k.act.sem, 1)

        @block.vector
        def _(dve):
            link = Link(k.dvel, dve)
            dve.wait_ge(k.act.sem, k.act.at(2))
            for o in range(16):
                dve.wait_ge(k.mm.sem, k.mm.at(o + 1))
                dve.tensor_tensor(rot, k.ps[:, o % 4, 0:S], sin, ALU.mult).then_inc(k.dve.sem, 1)
                link(dve.tensor_tensor(tmp, raw[:, o, :], cos, ALU.mult))
                dve.wait_ge(k.dve.sem, k.dve.at(o + 1))
                if o < 8:
                    link(dve.tensor_tensor(tmp, tmp, rot, ALU.add))
                    for h in range(2):
                        link(dve.tensor_scalar(q2[:, 2 * o + h, :], tmp, k.v("hmask", h), None, ALU.mult))
                else:
                    link(dve.tensor_tensor(kT[:, o - 8, :], tmp, rot, ALU.add))
            link.close()
    k.dve.base += 16
    k.mm.base += 16
    k.act.base += 2

    mask = k.H[:, 0:6, CTX]
    mx = k.sm[:, 0:30]
    sums = k.sm[:, 32:62]
    lse = k.sm[:, 64:94]
    top = k.sm[:, 96:106]
    den = k.sm[:, 112:122]
    nmx = k.sm[:, 128:158]
    with nc.Block() as block:
        @block.sync
        def _(sp):
            sp.dma_start(mask, k.a["attn_mask"]).then_inc(k.dma.sem, 16)
            sp.wait_ge(k.dma.sem, k.dma.at(16))

        @block.tensor
        def _(pe):
            for h in range(NHEAD):
                if h >= 4:
                    pe.wait_ge(k.dve.sem, k.dve.at(h - 3))
                for b in range(2):
                    mm = pe.matmul(k.ps[:, h % 4, b * S:(b + 1) * S], lhsT=q2[:, h, b * P:(b + 1) * P],
                                   rhs=kT[:, h // 2, :], start=True, stop=True)
                mm.then_inc(k.mm.sem, 1)

        @block.vector
        def _(dve):
            link = Link(k.dvel, dve)
            dve.wait_ge(k.dma.sem, k.dma.at(16))
            for h in range(NHEAD):
                g = h // 5
                dve.wait_ge(k.mm.sem, k.mm.at(h + 1))
                dve.scalar_tensor_tensor(Pm[:, h, :, :], k.ps[:, h % 4, :].rearrange("p (b s) -> p b s", b=2), 0.125,
                                         mask[:, 2 * g:2 * g + 2, :], ALU.mult, ALU.add).then_inc(k.dve.sem, 1)
                dve.wait_ge(k.dve.sem, k.dve.at(h + 1))
                link(dve.tensor_reduce(mx[:, 2 * h:2 * h + 2], Pm[:, h, :, :], axis=AX.X, op=ALU.max))
                dve.tensor_scalar(nmx[:, 2 * h:2 * h + 2], mx[:, 2 * h:2 * h + 2], -1.0, None, ALU.mult).then_inc(k.pool.sem, 1)
            link.close()

        @block.scalar
        def _(act):
            for h in range(NHEAD):
                act.wait_ge(k.pool.sem, k.pool.at(h + 1))
                for b in range(2):
                    act.activation(Pm[:, h, b, :], Pm[:, h, b, :], ACT.Exp, bias=nmx[:, 2 * h + b:2 * h + b + 1],
                                   accum_out=sums[:, 2 * h + b:2 * h + b + 1]).then_inc(k.act.sem, 1)
            act.wait_ge(k.act.sem, k.act.at(30))
            act.activation(lse, sums, ACT.Ln)
    k.dma.base += 16
    k.mm.base += NHEAD
    k.dve.base += NHEAD
    k.pool.base += NHEAD
    k.act.base += 30

    with nc.Block() as block:
        @block.vector
        def _(dve):
            link = Link(k.dvel, dve)
            part = lambda t, g: t[:, 10 * g:10 * g + 10]
            link(dve.tensor_tensor(lse, lse, mx, ALU.add))
            link(dve.tensor_tensor(top, part(lse, 0), part(lse, 1), ALU.max))
            link(dve.tensor_tensor(top, top, part(lse, 2), ALU.max))
            for g in range(3):
                link(dve.tensor_tensor(part(lse, g), part(lse, g), top, ALU.subtract))
            dve.tensor_copy(nmx, lse).then_inc(k.dve.sem, 1)
            dve.wait_ge(k.act.sem, k.act.at(1))
            link(dve.tensor_tensor(den, part(lse, 0), part(lse, 1), ALU.add))
            link(dve.tensor_tensor(den, den, part(lse, 2), ALU.add))
            for g in range(3):
                link(dve.tensor_tensor(part(sums, g), part(sums, g), den, ALU.mult))
            link(dve.reciprocal(sums, sums))
            link(dve.tensor_tensor(lse, lse, sums, ALU.mult))
            for h in range(NHEAD):
                for b in range(2):
                    i = 2 * h + b
                    dve.tensor_scalar(Pm[:, h, b, :], Pm[:, h, b, :], lse[:, i:i + 1], None, ALU.mult).then_inc(k.dve.sem, 1)
            link.close()

        @block.scalar
        def _(act):
            act.wait_ge(k.dve.sem, k.dve.at(1))
            act.activation(lse, nmx, ACT.Exp).then_inc(k.act.sem, 1)
            for h in range(NHEAD):
                act.wait_ge(k.mm.sem, k.mm.at(h + 1))
                if h >= 2:
                    act.wait_ge(k.pel.sem, k.pel.at(h - 1))
                act.activation(k.H[:, 0:2, CTX] if h % 2 == 0 else k.H[:, 2:4, CTX],
                               k.ps[:, h % 2, :].rearrange("p (b s) -> p b s", b=2), ACT.Copy).then_inc(k.act.sem, 1)

        @block.tensor
        def _(pe):
            def turn(h):
                pe.wait_ge(k.dve.sem, k.dve.at(1 + 2 * h + 2))
                if h >= 2:
                    pe.wait_ge(k.act.sem, k.act.at(1 + h - 1))
                for sb in range(2):
                    for b in range(2):
                        mm = pe.transpose(k.ps[:, h % 2, sb * S + b * P:sb * S + (b + 1) * P],
                                          Pm[:, h, b, sb * P:(sb + 1) * P], k.ident)
                mm.then_inc(k.mm.sem, 1)

            def values(h):
                pe.wait_ge(k.act.sem, k.act.at(1 + h + 1))
                pt = k.H[:, 0:2, CTX] if h % 2 == 0 else k.H[:, 2:4, CTX]
                o, r = h // 2, 64 * (h % 2)
                bank = 2 + o // 2
                for sb in range(2):
                    mm = pe.matmul(k.ps[r:r + 64, bank, (o % 2) * S:(o % 2) * S + S], lhsT=V[:, sb, h * 64:(h + 1) * 64],
                                   rhs=pt[:, sb, :], start=sb == 0, stop=sb == 1)
                mm.then_inc(k.pel.sem, 1)
            turn(0)
            for h in range(NHEAD):
                if h + 1 < NHEAD:
                    turn(h + 1)
                values(h)
    k.dve.base += 1 + 2 * NHEAD
    k.act.base += 1 + NHEAD
    k.mm.base += NHEAD
    k.pel.base += NHEAD

    with nc.Block() as block:
        @block.vector
        def _(dve):
            dve.memset(k.H[64:128, 7, LAT], 0.0)
            for o in range(8):
                r = P if o < 7 else 64
                dve.tensor_copy(k.H[0:r, o, LAT], k.ps[0:r, 2 + o // 2, (o % 2) * S:(o % 2) * S + S])


def stage_router(k):
    nc = k.nc
    G = k.W[:, 8192:8192 + NE * S].rearrange("p (e t) -> p e t", e=NE)
    spread = k.W[:, 0:2 * NE * P].rearrange("p (b e q) -> p b e q", b=2, e=NE)
    sm = k.sm
    with nc.Block() as block:
        @block.tensor
        def _(pe):
            for b in range(2):
                for kk in range(KD):
                    mm = pe.matmul(k.ps[:, b, 0:NE], lhsT=k.H[:, kk, S + b * P:S + (b + 1) * P],
                                   rhs=k.v("router", kk * NE, NE), start=kk == 0, stop=kk == KD - 1)
                mm.then_inc(k.mm.sem, 1)
            for b in range(2):
                pe.wait_ge(k.dve.sem, k.dve.at(1 + b))
                for e in range(NE):
                    mm = pe.matmul(k.ps[:, 2 + e // 2, (e % 2) * S + b * P:(e % 2) * S + (b + 1) * P],
                                   lhsT=spread[:, b, e, :], rhs=k.ident, start=True, stop=True)
            mm.then_inc(k.mm.sem, 1)

        @block.gpsimd
        def _(pool):
            pool.iota(sm[:, 256:264].bitcast(I32), pattern=[[1, NE]], base=0, channel_multiplier=0).then_inc(k.pool.sem, 1)

        @block.scalar
        def _(act):
            for b in range(2):
                act.wait_ge(k.pool.sem, k.pool.at(2 + b))
                act.activation(sm[:, 100 * b + 40:100 * b + 41], sm[:, 100 * b + 40:100 * b + 41], ACT.Exp).then_inc(k.act.sem, 1)

        @block.vector
        def _(dve):
            link = Link(k.dvel, dve)
            dve.wait_ge(k.pool.sem, k.pool.at(1))
            experts = sm[:, 264:272]
            link(dve.tensor_copy(experts, sm[:, 256:264].bitcast(I32)))
            for b in range(2):
                c = 100 * b
                logit, best, idx, idf = (sm[:, c + 8 * i:c + 8 * i + 8] for i in range(4))
                one = lambda i: sm[:, c + 40 + i:c + 41 + i]
                gates, second = sm[:, c + 48:c + 56], sm[:, c + 56:c + 64]
                dve.wait_ge(k.mm.sem, k.mm.at(b + 1))
                link(dve.tensor_copy(logit, k.ps[:, b, 0:NE]))
                link(dve.max(best, logit))
                link(dve.max_index(idx.bitcast(U32), best, logit))
                link(dve.tensor_copy(idf, idx.bitcast(U32)))
                dve.tensor_tensor(one(0), best[:, 1:2], best[:, 0:1], ALU.subtract).then_inc(k.pool.sem, 1)
                dve.wait_ge(k.act.sem, k.act.at(b + 1))
                link(dve.tensor_scalar(one(1), one(0), 1.0, None, ALU.add))
                link(dve.reciprocal(one(1), one(1)))
                link(dve.tensor_tensor(one(2), one(0), one(1), ALU.mult))
                link(dve.tensor_scalar(gates, experts, idf[:, 0:1], one(1), ALU.is_equal, ALU.mult))
                link(dve.tensor_scalar(second, experts, idf[:, 1:2], one(2), ALU.is_equal, ALU.mult))
                link(dve.tensor_tensor(gates, gates, second, ALU.add))
                dve.tensor_copy(spread[:, b, :, :], gates.unsqueeze(2).to_broadcast([P, NE, P])).then_inc(k.dve.sem, 1)
            dve.wait_ge(k.mm.sem, k.mm.at(3))
            dve.tensor_copy(G, k.ps[:, 2:6, :].rearrange("p b (e t) -> p (b e) t", e=2))
            link.close()
    k.mm.base += 3
    k.pool.base += 3
    k.act.base += 2
    k.dve.base += 2


def stage_norm2(k, layer, which, cols):
    m, v = k.mod2, 3 * which
    stage_norm(k, cols, lambda t, h: m[:, layer, (v + 1) * 8 + t, h:h + 1], lambda t, h: m[:, layer, v * 8 + t, h:h + 1])


def stage_post_norm(k, layer, which, cols, Y):
    nc = k.nc
    n = cols.stop - cols.start
    gate = k.sm[:, 0:16].rearrange("p (t h) -> p t h", h=2)
    v = 3 * which + 2
    halves = [c for c in (CTX, LAT) if c.start >= cols.start and c.stop <= cols.stop]
    rstd = k.W[:, 8 * T:8 * T + n]
    with nc.Block() as block:
        rms_scale(k, block, lambda i: Y[:, i, 0:n], n, k.W, rstd, 7)
    rms_counts(k)
    with nc.Block() as block:
        @block.vector
        def _(dve):
            link = Link(k.dvel, dve)
            link(dve.tensor_tensor(gate, k.mod2[:, layer, v * 8:v * 8 + 8, :],
                                   k.v("norm_g2", layer * 32 + (2 * which + 1) * 8, 8).unsqueeze(2).to_broadcast([P, 8, 2]), ALU.mult))
            for i in range(KD):
                for c in halves:
                    half = 0 if c is CTX else 1
                    own = slice(c.start - cols.start, c.stop - cols.start)
                    link.mark(dve.scalar_tensor_tensor(Y[:, i, own], Y[:, i, own], gate[:, i, half:half + 1],
                                                       rstd[:, own], ALU.mult, ALU.mult))
            link.wait()
            for i in range(KD):
                link.mark(dve.tensor_tensor(k.X[:, i, cols], k.X[:, i, cols], Y[:, i, 0:n], ALU.add))
            link.close()


def stage_square(k, cols, Y):
    nc = k.nc
    n = cols.stop - cols.start
    unit_done, out_done, signals, total = plan([i // KD for i in range(8 * KD)])
    with nc.Block() as block:
        @block.sync
        def _(sp):
            refill(k, sp, unit_done, U_SQ)

        @block.tensor
        def _(pe):
            def before(o):
                if o >= 4:
                    pe.wait_ge(k.act.sem, k.act.at(o - 3))
            gemm(k, pe, 8, KD, lambda kk: k.H[:, kk, cols], lambda o: k.ps[:, o % 4, 0:n], before, signals)

        @block.scalar
        def _(act):
            for o in range(8):
                act.wait_ge(k.mm.sem, k.mm.at(out_done[o]))
                act.activation(Y[:, o, 0:n], k.ps[:, o % 4, 0:n], ACT.Copy).then_inc(k.act.sem, 1)
    k.mm.base += total
    k.act.base += 8
    k.unit += U_SQ


def stage_conv_ffn(k, layer, cols, Y):
    nc = k.nc
    n = cols.stop - cols.start
    both = n == T
    A = k.W[:, 0:KF * n].rearrange("p (o t) -> p o t", o=KF)
    conv = k.W[:, 15360:15360 + 2 * T].rearrange("p (b t) -> p b t", b=2)
    owner = [t // KD for t in range(2 * KF * KD)] + [2 * KF + t // KF for t in range(KD * KF)]
    unit_done, out_done, signals, total = plan(owner)
    down0 = 2 * KF
    lat0 = n - S
    rows = S // GRID_W

    def up(dve, f):
        dve.wait_ge(k.mm.sem, k.mm.at(out_done[2 * f + 1]))
        dve.wait_ge(k.act.sem, k.act.at(f + 1))
        dve.tensor_tensor(A[:, f, :], k.ps[:, (2 * f + 1) % 4, 0:n], conv[:, f % 2, 0:n],
                          ALU.mult).then_inc(k.dve.sem, 1)

    with nc.Block() as block:
        @block.sync
        def _(sp):
            refill(k, sp, unit_done, EXPERT_UNITS)

        @block.tensor
        def _(pe):
            def before(o):
                if o >= 4:
                    f = o // 2 - 2
                    pe.wait_ge(k.dve.sem, k.dve.at(conv_done(f) if o % 2 == 0 else up_done(f)))
            gemm(k, pe, down0, KD, lambda kk: k.H[:, kk, cols], lambda o: k.ps[:, o % 4, 0:n], before, signals)

            def before_down(o):
                pe.wait_ge(k.dve.sem, k.dve.at(down0))
                if o >= 4:
                    pe.wait_ge(k.act.sem, k.act.at(KF + o - 3))
            gemm(k, pe, 8, KF, lambda kk: A[:, kk, :], lambda o: k.ps[:, o % 4, 0:n], before_down,
                 signals, first=down0 * KD)

        @block.vector
        def _(dve):
            link = Link(k.dvel, dve)
            for f in range(KF):
                y, x = conv[:, f % 2, 0:n], k.ps[:, (2 * f) % 4, 0:n]
                w = lambda a, b: k.v("fcw", layer * 9 * KF + (3 * a + b) * KF + f)
                dve.wait_ge(k.mm.sem, k.mm.at(out_done[2 * f]))
                if f >= 2:
                    dve.wait_ge(k.dve.sem, k.dve.at(up_done(f - 2)))
                link(dve.tensor_scalar(y, x, w(1, 1), k.v("fcb", layer * KF + f), ALU.mult, ALU.add))
                taps = []
                if both:
                    taps += [(y[:, 1:S], x[:, 0:S - 1], w(1, 0)), (y[:, 0:S - 1], x[:, 1:S], w(1, 2))]
                yg = y[:, lat0:n].rearrange("p (r c) -> p r c", r=rows)
                xg = x[:, lat0:n].rearrange("p (r c) -> p r c", r=rows)
                for dr in (-1, 0, 1):
                    for dc in (-1, 0, 1):
                        if dr == 0 and dc == 0:
                            continue
                        r0, r1 = max(0, -dr), rows - max(0, dr)
                        c0, c1 = max(0, -dc), GRID_W - max(0, dc)
                        taps.append((yg[:, r0:r1, c0:c1], xg[:, r0 + dr:r1 + dr, c0 + dc:c1 + dc], w(dr + 1, dc + 1)))
                for j, (yo, xo, ww) in enumerate(taps):
                    ins = dve.scalar_tensor_tensor(yo, xo, ww, yo, ALU.mult, ALU.add)
                    if j < len(taps) - 1:
                        link(ins)
                    else:
                        ins.then_inc(k.dve.sem, 1)
                if f > 0:
                    up(dve, f - 1)
            up(dve, KF - 1)
            link.close()

        @block.scalar
        def _(act):
            for f in range(KF):
                act.wait_ge(k.dve.sem, k.dve.at(conv_done(f)))
                act.activation(conv[:, f % 2, 0:n], conv[:, f % 2, 0:n], ACT.Gelu_apprx_tanh).then_inc(k.act.sem, 1)
            for o in range(8):
                act.wait_ge(k.mm.sem, k.mm.at(out_done[down0 + o]))
                act.activation(Y[:, o, 0:n], k.ps[:, o % 4, 0:n], ACT.Copy).then_inc(k.act.sem, 1)
    k.mm.base += total
    k.act.base += KF + 8
    k.dve.base += 2 * KF
    k.unit += EXPERT_UNITS


def conv_done(f):
    return 1 if f == 0 else 2 * f


def up_done(f):
    return 2 * f + 3 if f < KF - 1 else 2 * KF


class Even:

    def __init__(self, k):
        W = k.W
        t = lambda at, n: W[:, at:at + n * T].rearrange("p (o t) -> p o t", o=n)
        self.qk = t(0, 8)
        self.gqk = t(4096, 4)
        self.gate = t(6144, 8)
        self.V = W[:, 10240:14336].rearrange("p (b d) -> p b d", b=NB)
        self.glr = W[:, 14336:14848]
        self.I = W[:, 14848:15360]
        self.Fg = W[:, 15360:15872]
        self.B = W[:, 15872:16384]
        self.c = k.sm[:, 256:512].rearrange("p (b r) -> p b r", b=NB)


def stage_even_project(k, ev):
    nc = k.nc
    n_out = 23
    owner = [i // KD for i in range(n_out * KD)]
    unit_done, out_done, signals, total = plan(owner)
    m_units = 4
    unit_all = dict(unit_done)
    for u in range(m_units):
        unit_all[U_EV + u] = total + u + 1
    with nc.Block() as block:
        @block.sync
        def _(sp):
            refill(k, sp, unit_all, U_EV + m_units)

        @block.tensor
        def _(pe):
            def before(o):
                if 4 <= o < 12:
                    pe.wait_ge(k.dve.sem, k.dve.at(o - 3))
                elif o >= 12:
                    pe.wait_ge(k.act.sem, k.act.at(o - 3))
            gemm(k, pe, n_out, KD, lambda kk: k.H[:, kk, :], lambda o: k.ps[:, o % 4, :], before, signals)
            for u in range(m_units):
                pe.wait_ge(k.w_in[k.slot(U_EV + u)], k.landed(U_EV + u))
                if u >= 2:
                    pe.wait_ge(k.act.sem, k.act.at(n_out + 2 * (u - 1)))
                for b in range(NB):
                    for kk in range(KD):
                        mm = pe.matmul(k.ps[:, 4 + 2 * (u % 2) + b // 2, (b % 2) * 256:(b % 2) * 256 + 256],
                                       lhsT=k.H[:, kk, b * P:(b + 1) * P],
                                       rhs=k.ring[:, k.slot(U_EV + u), kk * 256:(kk + 1) * 256],
                                       start=kk == 0, stop=kk == KD - 1)
                mm.then_inc(k.mm.sem, 1)

        @block.vector
        def _(dve):
            link = Link(k.dvel, dve)
            for o in range(8):
                y, x = ev.qk[:, o, :], k.ps[:, o % 4, :]
                w = lambda j: k.v("ecw", 8 * j + o)
                dve.wait_ge(k.mm.sem, k.mm.at(out_done[o]))
                link(dve.tensor_scalar(y, x, w(1), k.v("ecb", o), ALU.mult, ALU.add))
                for c in (CTX, LAT):
                    a, b = c.start, c.stop
                    link(dve.scalar_tensor_tensor(y[:, a + 1:b], x[:, a:b - 1], w(0), y[:, a + 1:b], ALU.mult, ALU.add))
                    ins = dve.scalar_tensor_tensor(y[:, a:b - 1], x[:, a + 1:b], w(2), y[:, a:b - 1], ALU.mult, ALU.add)
                    if c is CTX:
                        link(ins)
                    else:
                        ins.then_inc(k.dve.sem, 1)
            link.close()

        @block.scalar
        def _(act):
            for o in range(8):
                act.wait_ge(k.dve.sem, k.dve.at(o + 1))
                act.activation(ev.qk[:, o, :], ev.qk[:, o, :], ACT.Silu).then_inc(k.act.sem, 1)
            for o in range(8, n_out):
                act.wait_ge(k.mm.sem, k.mm.at(out_done[o]))
                x = k.ps[:, o % 4, :]
                if o < 10:
                    ins = act.activation(ev.gqk[:, o - 8, :], x, ACT.Copy, scale=64 ** -0.5)
                elif o < 12:
                    ins = act.activation(ev.gqk[:, o - 8, :], x, ACT.Copy)
                elif o == 12:
                    ins = act.activation(ev.glr, x, ACT.Copy)
                elif o < 15:
                    ins = act.activation(ev.I if o == 13 else ev.Fg, x, ACT.Identity, bias=k.v("ebg", o - 13))
                else:
                    ins = act.activation(ev.gate[:, o - 15, :], x, ACT.Sigmoid if o < 19 else ACT.Silu)
                ins.then_inc(k.act.sem, 1)
            for u in range(m_units):
                act.wait_ge(k.mm.sem, k.mm.at(total + u + 1))
                for h in range(2):
                    act.activation(ev.V[:, 2 * h:2 * h + 2, u * 256:(u + 1) * 256],
                                   k.ps[:, 4 + 2 * (u % 2) + h, :].rearrange("p (b d) -> p b d", b=2),
                                   ACT.Copy).then_inc(k.act.sem, 1)
    k.mm.base += total + m_units
    k.act.base += n_out + 2 * m_units
    k.dve.base += 8
    k.unit += U_EV + m_units


def stage_mlstm_gates(k, ev):
    nc = k.nc
    F_, B, I = ev.Fg, ev.B, ev.I
    runs = [(slice(0, 32), slice(0, T), 1, None), (slice(32, 64), CTX, -1, None), (slice(32, 64), LAT, -1, 0)]
    e = k.H[:, 0, :]
    one = k.ones[:, 0:1]
    with nc.Block() as block:
        @block.scalar
        def _(act):
            act.wait_ge(k.dve.sem, k.dve.at(1))
            act.activation(e, e, ACT.Exp, scale=-1.0).then_inc(k.act.sem, 1)
            act.wait_ge(k.dve.sem, k.dve.at(2))
            act.activation(e, e, ACT.Ln).then_inc(k.act.sem, 1)
            act.wait_ge(k.dve.sem, k.dve.at(3))
            act.activation(B, B, ACT.Exp, scale=-1.0)
            act.wait_ge(k.mm.sem, k.mm.at(1))
            act.activation(ev.c, k.ps[:, 0, :].rearrange("p (b r) -> p b r", b=NB)[:, :, 0:64], ACT.Copy)

        @block.tensor
        def _(pe):
            pe.wait_ge(k.dve.sem, k.dve.at(4))
            for b in range(NB):
                mm = pe.transpose(k.ps[:, 0, b * P:(b + 1) * P], I[:, b * P:(b + 1) * P], k.ident)
            mm.then_inc(k.mm.sem, 1)

        @block.vector
        def _(dve):
            link = Link(k.dvel, dve)
            dve.scalar_tensor_tensor(e, F_, -1.0, F_, ALU.mult, ALU.max).then_inc(k.dve.sem, 1)
            dve.wait_ge(k.act.sem, k.act.at(1))
            dve.tensor_scalar(e, e, 1.0, None, ALU.add).then_inc(k.dve.sem, 1)
            dve.wait_ge(k.act.sem, k.act.at(2))
            link(dve.scalar_tensor_tensor(F_, F_, 0.0, e, ALU.min, ALU.subtract))
            link(dve.memset(B[64:128, :], 0.0))
            for rows, c, step, after in runs:
                view = lambda x: x[rows, c] if step > 0 else x[rows, c][:, ::-1]
                init = 0.0 if after is None else B[rows, after:after + 1]
                n = c.stop - c.start
                link(dve.tensor_tensor_scan(view(B), one[rows, :].to_broadcast([32, n]), view(F_), init, ALU.mult, ALU.add))
            link(dve.tensor_tensor(I, I, B, ALU.subtract))
            link(dve.memset(F_[64:128, :], 0.0))
            for rows, c, step, after in runs:
                view = lambda x: x[rows, c] if step > 0 else x[rows, c][:, ::-1]
                init = 0.0 if after is None else F_[rows, after:after + 1]
                link(dve.tensor_tensor_scan(view(F_), view(I), view(I), init, ALU.max, ALU.max))
            dve.tensor_tensor(B, B, F_, ALU.add).then_inc(k.dve.sem, 1)
            dve.tensor_scalar(F_, F_, -1.0, None, ALU.mult).then_inc(k.dve.sem, 1)
            link.close()
    k.act.base += 2
    k.mm.base += 1
    k.dve.base += 4


def stage_mlstm(k, ev):
    nc = k.nc
    mask = k.H[:, 4, :]
    mk = k.H[:, 6:8, :].rearrange("p a t -> p (a t)").rearrange("p (z b t) -> p z b t", z=2, b=2)
    ST = k.H[:, 0:4, :]
    Wt = k.W
    A = [k.H[:, 4, :], k.H[:, 5, :]]
    d, t2 = ev.I, ev.glr
    with nc.Block() as block:
        @block.sync
        def _(sp):
            sp.dma_start(k.H[:, 6:8, :].rearrange("p a t -> p (a t)"), k.a["scan_mask"]).then_inc(k.dma.sem, 16)
            sp.wait_ge(k.dma.sem, k.dma.at(16))
    k.dma.base += 16
    cols = [slice(0, T), slice(0, T), LAT, LAT]
    with nc.Block() as block:
        @block.tensor
        def _(pe):
            n = 0
            for h in range(4):
                if h:
                    pe.wait_ge(k.act.sem, k.act.at(12 * h))
                    pe.wait_ge(k.dve.sem, k.dve.at(18 * h))
                for b in range(NB):
                    mm = pe.matmul(k.ps[:, b % 2, cols[b]], lhsT=ev.qk[:, 4 + h, b * P:(b + 1) * P],
                                   rhs=ev.qk[:, h, cols[b]], start=True, stop=True)
                    mm.then_inc(k.mm.sem, 1)
                    if b < 2:
                        pe.wait_ge(k.act.sem, k.act.at(12 * h + b + 1))
                for z in range(2):
                    r = 32 * z + h
                    if z:
                        pe.wait_ge(k.dve.sem, k.dve.at(18 * h + 9))
                    pick = k.ident[:, r:r + 1].to_broadcast([P, P])
                    pe.matmul(k.ps[:, 4, :], lhsT=pick, rhs=ev.Fg, start=True, stop=True).then_inc(k.mm.sem, 1)
                    pe.matmul(k.ps[:, 7, :], lhsT=pick, rhs=ev.B, start=True, stop=True)
                    for b in range(NB):
                        pe.wait_ge(k.pool.sem, k.pool.at(8 * h + 4 * z + b + 1))
                        a = A[b % 2][:, cols[b]]
                        pe.matmul(k.ps[:, 5, cols[b]], lhsT=ev.V[:, b, h * P:(h + 1) * P], rhs=a, start=b == 0, stop=b == 3)
                        pe.matmul(k.ps[:, 6, cols[b]], lhsT=k.ones, rhs=a, start=b == 0, stop=b == 3).then_inc(k.mm.sem, 1)

        @block.scalar
        def _(act):
            for h in range(4):
                for b in range(NB):
                    act.wait_ge(k.mm.sem, k.mm.at(14 * h + b + 1))
                    act.activation(ST[:, b, cols[b]], k.ps[:, b % 2, cols[b]], ACT.Copy, scale=P ** -0.5).then_inc(k.act.sem, 1)
                for z in range(2):
                    for b in range(NB):
                        act.wait_ge(k.dve.sem, k.dve.at(18 * h + 9 * z + 2 * b + 1))
                        a = A[b % 2][:, cols[b]]
                        act.activation(a, a, ACT.Exp).then_inc(k.act.sem, 1)

        @block.vector
        def _(dve):
            link = Link(k.dvel, dve)
            for h in range(4):
                for z in range(2):
                    dve.wait_ge(k.mm.sem, k.mm.at(14 * h + 4 + 5 * z + 1))
                    for b in range(NB):
                        a = A[b % 2][:, cols[b]]
                        if b >= 2:
                            dve.wait_ge(k.mm.sem, k.mm.at(14 * h + 4 + 5 * z + b))
                        dve.tensor_scalar(a, k.ps[:, 4, cols[b]], ev.c[:, b, 32 * z + h:32 * z + h + 1], 0.0,
                                          ALU.add, ALU.min).then_inc(k.dve.sem, 1)
                        dve.wait_ge(k.act.sem, k.act.at(12 * h + 4 + 4 * z + b + 1))
                        dve.tensor_tensor(a, a, ST[:, b, cols[b]], ALU.mult).then_inc(k.dve.sem, 1)
                    dve.wait_ge(k.mm.sem, k.mm.at(14 * h + 4 + 5 * z + 5))
                    link(dve.tensor_copy(d, k.ps[:, 7, :]))
                    link(dve.scalar_tensor_tensor(d, k.ps[:, 6, :], -1.0, d, ALU.mult, ALU.max))
                    link(dve.tensor_tensor(d, k.ps[:, 6, :], d, ALU.max))
                    link(dve.reciprocal(d, d))
                    if z == 0:
                        dve.tensor_tensor(ev.qk[:, h, :], k.ps[:, 5, :], d, ALU.mult).then_inc(k.dve.sem, 1)
                    else:
                        link(dve.tensor_tensor(d, k.ps[:, 5, :], d, ALU.mult))
                        dve.wait_ge(k.dve.sem, k.dve.at(18 * h + 9))
                        dve.tensor_tensor(ev.qk[:, h, :], ev.qk[:, h, :], d, ALU.add).then_inc(k.dve.sem, 1)
            link.close()

        @block.gpsimd
        def _(pool):
            for h in range(4):
                for z in range(2):
                    for b in range(NB):
                        c = CTX if b < 2 else LAT
                        a = A[b % 2][:, c]
                        pool.wait_ge(k.dve.sem, k.dve.at(18 * h + 9 * z + 2 * b + 2))
                        pool.tensor_tensor(a, a, mk[:, z, b % 2, :], ALU.mult).then_inc(k.pool.sem, 1)
    k.mm.base += 14 * 4
    k.act.base += 12 * 4
    k.dve.base += 18 * 4
    k.pool.base += 8 * 4


def stage_gla(k, ev):
    nc = k.nc
    w2 = k.H[:, 7, :]
    one = k.ones[:, 0:1]
    C = k.H[:, 0:2, :]
    E = k.H[:, 2, :]
    Kt = [k.H[:, 3, :], k.H[:, 4, :]]
    Q0 = [k.H[:, 5, :], k.H[:, 6, :]]
    Q1 = [ev.I, ev.Fg]
    tmp = ev.B
    acc = k.H[:, 7, :]
    accs = [k.H[:, 7, :], ev.glr]
    la = [k.H[:, 3, :], k.H[:, 4, :]]
    for j in range(2):
        with nc.Block() as block:
            @block.sync
            def _(sp):
                sp.dma_start(w2, k.a["gla_w2"]).then_inc(k.dma.sem, 16)

            @block.tensor
            def _(pe):
                pe.wait_ge(k.dma.sem, k.dma.at(16))
                src = ev.glr if j == 0 else ev.qk[:, 7, :]
                for z in range(2):
                    mm = pe.matmul(k.ps[:, z, :], lhsT=w2[:, z * 256 + j * P:z * 256 + (j + 1) * P], rhs=src, start=True, stop=True)
                mm.then_inc(k.mm.sem, 1)

            @block.scalar
            def _(act):
                act.wait_ge(k.mm.sem, k.mm.at(1))
                if j == 0:
                    act.activation(ev.qk[:, 7, :], ev.glr, ACT.Copy)
                for z in range(2):
                    act.activation(C[:, z, :], k.ps[:, z, :], ACT.Identity, bias=k.v("glab", 2 * z + j)).then_inc(k.act.sem, 1)
                for z in range(2):
                    act.wait_ge(k.dve.sem, k.dve.at(1 + z))
                    act.activation(la[z], la[z], ACT.Exp, scale=-1.0).then_inc(k.act.sem, 1)
                for z in range(2):
                    act.wait_ge(k.dve.sem, k.dve.at(3 + z))
                    act.activation(la[z], la[z], ACT.Ln).then_inc(k.act.sem, 1)

            @block.vector
            def _(dve):
                link = Link(k.dvel, dve)
                for z in range(2):
                    dve.wait_ge(k.act.sem, k.act.at(1 + z))
                    dve.scalar_tensor_tensor(la[z], C[:, z, :], -1.0, C[:, z, :], ALU.mult, ALU.max).then_inc(k.dve.sem, 1)
                for z in range(2):
                    dve.wait_ge(k.act.sem, k.act.at(3 + z))
                    dve.tensor_scalar(la[z], la[z], 1.0, None, ALU.add).then_inc(k.dve.sem, 1)
                for z in range(2):
                    dve.wait_ge(k.act.sem, k.act.at(5 + z))
                    link(dve.scalar_tensor_tensor(la[z], C[:, z, :], 0.0, la[z], ALU.min, ALU.subtract))
                    link(dve.tensor_scalar(la[z], la[z], 1.0 / 16, None, ALU.mult))
                    link(dve.tensor_tensor_scan(C[:, z, :], one.to_broadcast([P, T]), la[z], 0.0, ALU.mult, ALU.add))
                link(dve.tensor_copy(tmp[:, 0:1], C[:, 1, T - 1:T]))
                link(dve.tensor_tensor(C[:, 1, :], C[:, 1, :], la[1], ALU.subtract))
                link.close()
        k.dma.base += 16
        k.mm.base += 1
        k.act.base += 6
        k.dve.base += 4

        steps = [(z, l) for z in range(2) for l in range(9)]
        total_sum = k.sm[:, 0:1]
        def masked(dve, link, i):
            z, l = steps[i]
            if l >= 7:
                return
            dve.wait_ge(k.mm.sem, k.mm.at(i + 2))
            m = k.level[z][:, l * P:(l + 1) * P].unsqueeze(1).to_broadcast([P, NB, P])
            for h in range(2):
                bank = 2 * ((i + 1) % 2) + h
                a = accs[h].rearrange("p (b t) -> p b t", b=NB)
                t = ev.qk[:, 6, :].rearrange("p (b t) -> p b t", b=NB)
                link(dve.tensor_tensor(t, k.ps[:, bank, :].rearrange("p (b t) -> p b t", b=NB), m, ALU.mult))
                link(dve.tensor_tensor(a, a, t, ALU.add))
                dve.tensor_copy(k.sm[:, 1:2], accs[h][:, 0:1]).then_inc(k.pool.sem, 1)

        with nc.Block() as block:
            @block.tensor
            def _(pe):
                pe.wait_ge(k.dve.sem, k.dve.at(2))
                for h, q in enumerate((Q0[1], Q1[1])):
                    for b in range(NB):
                        mm = pe.matmul(k.ps[:, h, b * P:(b + 1) * P], lhsT=ev.gqk[:, 2 + j, b * P:(b + 1) * P],
                                       rhs=q[:, b * P:(b + 1) * P], start=True, stop=True)
                mm.then_inc(k.mm.sem, 1)
                n_dve = 2
                for i, (z, l) in enumerate(steps):
                    pe.wait_ge(k.dve.sem, k.dve.at(n_dve + 4 * i + 4))
                    kt, qs = Kt[i % 2], (Q0[i % 2], Q1[i % 2])
                    if l < 7:
                        pe.wait_ge(k.pool.sem, k.pool.at(masked_before(steps, i)))
                    for h in range(2):
                        if l < 7:
                            bank = 2 * ((i + 1) % 2) + h
                            for b in range(NB):
                                c = slice(b * P, (b + 1) * P)
                                mm = pe.matmul(k.ps[:, bank, c], lhsT=kt[:, c], rhs=qs[h][:, c], start=True, stop=True)
                        elif l == 7:
                            for b in (0, 2):
                                s, t = (b, b + 1) if z == 0 else (b + 1, b)
                                mm = pe.matmul(k.ps[:, 4 + h, s * P:(s + 1) * P], lhsT=kt[:, s * P:(s + 1) * P],
                                               rhs=qs[h][:, t * P:(t + 1) * P], start=True, stop=True)
                        else:
                            for s in range(2):
                                mm = pe.matmul(k.ps[:, 6 + h, s * 256:(s + 1) * 256], lhsT=kt[:, s * P:(s + 1) * P],
                                               rhs=qs[h][:, LAT], start=z == 0 and s == 0, stop=True, skip_group_check=True)
                    mm.then_inc(k.mm.sem, 1)

            @block.scalar
            def _(act):
                for i in range(len(steps)):
                    act.wait_ge(k.dve.sem, k.dve.at(2 + 4 * i + 1))
                    if i >= 1:
                        act.wait_ge(k.dve.sem, k.dve.at(2 + 4 * (i - 1) + 4))
                    act.activation(E, tmp, ACT.Exp, scale=-1.0).then_inc(k.act.sem, 1)

            @block.vector
            def _(dve):
                link = Link(k.dvel, dve)
                link(dve.tensor_copy(total_sum, tmp[:, 0:1]))
                q, kx = ev.gqk[:, j, :], ev.gqk[:, 2 + j, :]
                for h, qb in enumerate((Q0[1], Q1[1])):
                    dve.tensor_scalar(qb, q, k.v("hmask", h), None, ALU.mult).then_inc(k.dve.sem, 1)
                for i, (z, l) in enumerate(steps):
                    half = 1 << l
                    c = C[:, z, :]
                    if i >= 1:
                        dve.wait_ge(k.act.sem, k.act.at(i))
                    if l == 8 and z == 1:
                        link(dve.tensor_copy(tmp[:, CTX], c[:, CTX]))
                        link(dve.tensor_scalar(tmp[:, LAT], c[:, LAT], total_sum, None, ALU.subtract))
                    else:
                        cv = c.rearrange("p (n t) -> p n t", t=2 * half)
                        at = half - 1 if z == 0 else half
                        link(dve.tensor_tensor(tmp.rearrange("p (n t) -> p n t", t=2 * half), cv,
                                               cv[:, :, at:at + 1].to_broadcast([P, T // (2 * half), 2 * half]), ALU.subtract))
                    dve.scalar_tensor_tensor(tmp, tmp, -1.0, tmp, ALU.mult, ALU.max).then_inc(k.dve.sem, 1)
                    if i >= 2:
                        dve.wait_ge(k.mm.sem, k.mm.at(i))
                    elif i == 1:
                        dve.wait_ge(k.mm.sem, k.mm.at(1))
                    dve.wait_ge(k.act.sem, k.act.at(i + 1))
                    dve.tensor_tensor(Kt[i % 2], kx, E, ALU.mult).then_inc(k.dve.sem, 1)
                    for h, qb in enumerate((Q0[i % 2], Q1[i % 2])):
                        dve.scalar_tensor_tensor(qb, q, k.v("hmask", h), E, ALU.mult, ALU.mult).then_inc(k.dve.sem, 1)
                    if i == 0:
                        dve.wait_ge(k.mm.sem, k.mm.at(1))
                        for h in range(2):
                            link(dve.scalar_tensor_tensor(accs[h].rearrange("p (b t) -> p b t", b=NB),
                                                          k.ps[:, h, :].rearrange("p (b t) -> p b t", b=NB), 2.0,
                                                          k.ident.unsqueeze(1).to_broadcast([P, NB, P]), ALU.mult, ALU.mult))
                            dve.tensor_copy(k.sm[:, 1:2], accs[h][:, 0:1]).then_inc(k.pool.sem, 1)
                    else:
                        masked(dve, link, i - 1)
                masked(dve, link, len(steps) - 1)
                link.close()

        n_pool = 2 + 2 * 14
        k.mm.base += 1 + len(steps)
        k.act.base += len(steps)
        k.dve.base += 2 + 4 * len(steps)
        k.pool.base += n_pool

        off7 = [k.H[:, 3, :], k.H[:, 4, :]]
        off8 = [k.H[:, 5, :], k.H[:, 6, :]]
        with nc.Block() as block:
            @block.scalar
            def _(act):
                for h in range(2):
                    act.activation(off7[h], k.ps[:, 4 + h, :], ACT.Copy).then_inc(k.act.sem, 1)
                for h in range(2):
                    act.wait_ge(k.mm.sem, k.mm.at(h + 1))
                    act.activation(ev.qk[:, 4 + 2 * j + h, :], k.ps[:, h, :], ACT.Copy)

            @block.vector
            def _(dve):
                for h in range(2):
                    dve.tensor_copy(off8[h], k.ps[:, 6 + h, :]).then_inc(k.dve.sem, 1)

            @block.tensor
            def _(pe):
                for h in range(2):
                    pe.wait_ge(k.act.sem, k.act.at(h + 1))
                    pe.wait_ge(k.dve.sem, k.dve.at(h + 1))
                    v = lambda b: ev.V[:, b, 512 + (2 * j + h) * P:512 + (2 * j + h + 1) * P]
                    for t in range(NB):
                        parts = [(t, accs[h][:, t * P:(t + 1) * P]), (t ^ 1, off7[h][:, (t ^ 1) * P:((t ^ 1) + 1) * P])]
                        if t >= 2:
                            parts += [(s, off8[h][:, s * 256 + (t - 2) * P:s * 256 + (t - 1) * P]) for s in range(2)]
                        for n, (s, rhs) in enumerate(parts):
                            mm = pe.matmul(k.ps[:, h, t * P:(t + 1) * P], lhsT=v(s), rhs=rhs, start=n == 0, stop=n == len(parts) - 1)
                    mm.then_inc(k.mm.sem, 1)
        k.act.base += 2
        k.dve.base += 2
        k.mm.base += 2


def masked_before(steps, i):
    n = 2
    for z, l in steps[:max(i - 1, 0)]:
        n += 2 * (l < 7)
    return n if i >= 1 else 0


def stage_even_gate(k, ev):
    nc = k.nc
    sq = [k.W[:, 10240 + i * T:10240 + (i + 1) * T] for i in range(2)]
    rs = [k.W[:, 11264 + i * T:11264 + (i + 1) * T] for i in range(2)]
    with nc.Block() as block:
        @block.scalar
        def _(act):
            for i in range(8):
                if i >= 2:
                    act.wait_ge(k.mm.sem, k.mm.at(i - 1))
                act.activation(sq[i % 2], ev.qk[:, i, :], ACT.Square).then_inc(k.act.sem, 1)
                act.wait_ge(k.dve.sem, k.dve.at(2 * i + 1))
                act.activation(rs[i % 2], rs[i % 2], ACT.Sqrt).then_inc(k.act.sem, 1)

        @block.tensor
        def _(pe):
            for i in range(8):
                pe.wait_ge(k.act.sem, k.act.at(2 * i + 1))
                pe.matmul(k.ps[:, i % 2, :], lhsT=k.ones, rhs=sq[i % 2], start=True, stop=True).then_inc(k.mm.sem, 1)

        @block.vector
        def _(dve):
            link = Link(k.dvel, dve)
            for i in range(8):
                dve.wait_ge(k.mm.sem, k.mm.at(i + 1))
                dve.tensor_scalar(rs[i % 2], k.ps[:, i % 2, :], 1.0 / P, EPS, ALU.mult, ALU.add).then_inc(k.dve.sem, 1)
                dve.wait_ge(k.act.sem, k.act.at(2 * i + 2))
                link(dve.reciprocal(rs[i % 2], rs[i % 2]))
                link(dve.scalar_tensor_tensor(rs[i % 2], ev.qk[:, i, :], k.v("headg", i), rs[i % 2], ALU.mult, ALU.mult))
                dve.tensor_tensor(k.H[:, i, :], rs[i % 2], ev.gate[:, i, :], ALU.mult).then_inc(k.dve.sem, 1)
            link.close()
    k.act.base += 16
    k.mm.base += 8
    k.dve.base += 16


def block2_even(k):
    both = slice(0, T)
    ev = Even(k)
    stage_ada2(k, 0)
    stage_norm2(k, 0, 0, both)
    stage_even_project(k, ev)
    stage_mlstm_gates(k, ev)
    stage_mlstm(k, ev)
    stage_gla(k, ev)
    stage_even_gate(k, ev)
    Y = k.W[:, 11264:15360].rearrange("p (o t) -> p o t", o=KD)
    stage_square(k, both, Y)
    stage_post_norm(k, 0, 0, both, Y)
    stage_norm2(k, 0, 1, both)
    stage_conv_ffn(k, 0, both, Y)
    stage_post_norm(k, 0, 1, both, Y)


RW_ORDER = (0, 2, 3, 1, 4, 5)


def stage_rwkv_project(k):
    nc = k.nc
    XX = k.W[:, 0:4096].rearrange("p (o t) -> p o t", o=KD)
    XB = [k.W[:, 4096 * (b + 1):4096 * (b + 2)].rearrange("p (o t) -> p o t", o=KD) for b in range(2)]
    out = k.W[:, 12288:14336].rearrange("p (o t) -> p o t", o=4)
    owner = [i // KD for i in range(27 * KD)]
    unit_done, out_done, signals, total = plan(owner)
    last = [7, 15, 23, 24, 25, 26]
    rows = S // GRID_W
    with nc.Block() as block:
        @block.sync
        def _(sp):
            refill(k, sp, unit_done, 14)

        @block.tensor
        def _(pe):
            for n in range(6):
                first_o = 0 if n == 0 else last[n - 1] + 1

                def before(o, n=n, first_o=first_o):
                    pe.wait_ge(k.dve.sem, k.dve.at(8 * n + 8))
                    if first_o + o >= 4:
                        pe.wait_ge(k.act.sem, k.act.at(first_o + o - 3))
                gemm(k, pe, last[n] - first_o + 1, KD, lambda kk, n=n: XB[n % 2][:, kk, :],
                     lambda o, f=first_o: k.ps[:, (f + o) % 4, :], before, signals, first=first_o * KD)

        @block.vector
        def _(dve):
            link = Link(k.dvel, dve)
            for i in range(KD):
                link.mark(dve.tensor_scalar(XX[:, i, :], k.H[:, i, :], -1.0, None, ALU.mult))
            link.wait()
            for i in range(KD):
                quarter = i // 2
                x, h = XX[:, i, :], k.H[:, i, :]
                if quarter % 2 == 0:
                    pieces = [(x[:, 1:S], h[:, 0:S - 1])]
                else:
                    pieces = [(x[:, 0:S - 1], h[:, 1:S])]
                xg, hg = (y[:, LAT].rearrange("p (r c) -> p r c", r=rows) for y in (x, h))
                pieces.append([(xg[:, :, 1:GRID_W], hg[:, :, 0:GRID_W - 1]), (xg[:, :, 0:GRID_W - 1], hg[:, :, 1:GRID_W]),
                               (xg[:, 1:rows, :], hg[:, 0:rows - 1, :]), (xg[:, 0:rows - 1, :], hg[:, 1:rows, :])][quarter])
                for a, b in pieces:
                    link.mark(dve.tensor_tensor(a, a, b, ALU.add))
            link.wait()
            for n, m in enumerate(RW_ORDER):
                if n >= 2:
                    dve.wait_ge(k.mm.sem, k.mm.at(out_done[last[n - 2]]))
                for i in range(KD):
                    dve.scalar_tensor_tensor(XB[n % 2][:, i, :], XX[:, i, :], k.v("mu", m * 8 + i), k.H[:, i, :],
                                             ALU.mult, ALU.add).then_inc(k.dve.sem, 1)
            link.close()

        @block.scalar
        def _(act):
            for o in range(24):
                act.wait_ge(k.mm.sem, k.mm.at(out_done[o]))
                if o >= 4:
                    act.wait_ge(k.stored[o % 4], 16 * (o // 4))
                act.activation(out[:, o % 4, :], k.ps[:, o % 4, :], ACT.Copy).then_inc(k.act.sem, 1)
                act.wait_ge(k.act.sem, k.act.at(o + 1))
                act.dma_start(k.a["rkv"][o % 8, :, o // 8, :], out[:, o % 4, :]).then_inc(k.stored[o % 4], 16)
            for o, f in ((24, ACT.Tanh), (25, ACT.Copy), (26, ACT.Sigmoid)):
                act.wait_ge(k.mm.sem, k.mm.at(out_done[o]))
                act.activation(k.X[:, 2 * (o - 24):2 * (o - 24) + 2, CTX],
                               k.ps[:, o % 4, :].rearrange("p (a t) -> p a t", a=2), f).then_inc(k.act.sem, 1)
            for b in range(4):
                act.wait_ge(k.stored[b], 16 * 6)
    k.mm.base += total
    k.act.base += 27
    k.dve.base += 48
    k.unit += 14


class Events:

    def __init__(self, signal, names, turns):
        self.s, self.names, self.turns = signal, {n: i + 1 for i, n in enumerate(names)}, turns
        assert len(self.names) == len(names)
        self.per = len(names)
        self.sent = 0

    def fire(self, ins, name):
        self.sent += 1
        assert self.names[name] == self.sent, (name, self.names[name], self.sent)
        ins.then_inc(self.s.sem, 1)

    def at(self, turn, name):
        n = 0 if name is None else self.names[name]
        return turn * self.per + (self.s.base + n)

    def close(self):
        assert self.sent == self.per
        self.s.base += self.per * self.turns


def rwkv_events():
    pe, dve, act, pool = [], [], [], []
    for ph in range(2):
        p = f"{ph}."
        pe += [p + n for n in ["low", "vt", "ss", "gram0", "gram1", "tok0", "tok1", "m1_0", "m1_1"]]
        dve += [p + n for n in ["kk0"]]
        act += [p + n for n in ["sg0", "sg1", "a", "g", "vtok", "nrm"]]
        for z in "01":
            dve += [p + n + z for n in ("ref", "ie")]
            act += [p + n + z for n in ("io", "e0", "e1", "e2")]
        for z in "01":
            dve += [p + "ab" + z]
            pool += [p + "mk" + z]
        for z in "01":
            dve += [p + n + z for n in ("ge", "mt")]
        act += [p + "tokc0", p + "tokc1", p + "m1c0", p + "m1c1"]
        for l in range(1, 6):
            for z in "01":
                pe += [p + f"t{l}" + z]
                pool += [p + f"ot{l}" + z]
                act += [p + f"tc{l}" + z]
            for z in "01":
                pe += [p + f"n{l}" + z]
                dve += [p + f"mn{l}" + z]
        pe += [p + "rv0", p + "rv1"]
        act += [p + "rvc0", p + "rvc1"]
        for i in range(4):
            dve += [p + f"h{i}0", p + f"h{i}1", p + f"rh{i}0", p + f"rh{i}1"]
            pe += [p + f"{n}{i}{z}" for n in "rsu" for z in "01"]
            act += [p + f"sc{i}0", p + f"sc{i}1"]
        if ph == 0:
            dve += [p + "end"]
        else:
            pe += [p + "y", p + "bonus", p + "mean", p + "var"]
            act += [p + "yc", p + "ysq", p + "yrt"]
            dve += [p + n for n in ("rk", "yy", "yd", "yv", "end")]
    return pe, dve, act, pool


def stage_rwkv(k):
    nc = k.nc
    W, H, X = k.W, k.H, k.X
    at = [0]

    def take(n):
        at[0] += n
        assert at[0] <= 16384
        return W[:, at[0] - n:at[0]]
    rkv = take(1536).rearrange("p (i t) -> p i t", i=3)
    wj = take(520)
    VC = take(512).rearrange("p (a b v) -> p a b v", a=2, b=2)
    Vt = take(256).rearrange("p (b v) -> p b v", b=2)
    a_, kk, ka, k2, g_ = (take(256) for _ in range(5))
    reset = take(256)
    inc, exc, LT, KA, BR, KR, M, MT, T1, OT, tok, St, hatO, SA, RHS, masked = ([] for _ in range(16))
    for z in range(2):
        both_ = take(512)
        inc.append(both_[:, 0:256])
        exc.append(both_[:, 256:512])
        for lst in (LT, KA, BR, KR, M, MT):
            lst.append(take(512).rearrange("p (h b t) -> p h b t", h=2, b=2))
        mm_ = take(1024)
        masked.append(mm_.rearrange("p (i h t) -> p i h t", i=2, h=2))
        T1.append(mm_[:, 0:512].rearrange("p (h b t) -> p h b t", h=2, b=2))
        OT.append(mm_[:, 512:1024].rearrange("p (h b t) -> p h b t", h=2, b=2))
        tok.append(take(512).rearrange("p (i b v) -> p i b v", i=2, b=2))
        St.append(take(P))
        hatO.append(take(P))
        SA.append(take(256).rearrange("p (a v) -> p a v", a=2))
        RHS.append(take(P))
    RV = [inc[z] for z in range(2)]
    hat = [[k.hat[:, 2 * z + b, :] for b in range(2)] for z in range(2)]
    e = [[M[z].rearrange("p h b t -> p (h b t)")[:, 0:256], M[z].rearrange("p h b t -> p (h b t)")[:, 256:512],
          MT[z].rearrange("p h b t -> p (h b t)")[:, 0:256]] for z in range(2)]
    AR = [H[:, 2 * z:2 * z + 2, CTX] for z in range(2)]
    BK = [H[:, 4 + 2 * z:6 + 2 * z, CTX] for z in range(2)]
    TW, TA, TG = (X[:, 2 * i:2 * i + 2, CTX] for i in range(3))
    IO = [k.sm[:, 16 * z:16 * z + 8] for z in range(2)]
    ru = [k.sm[:, 32 + 16 * z:40 + 16 * z] for z in range(2)]
    wa2, ww2, wg2 = wj[:, 0:128], [wj[:, 128:256], wj[:, 256:384]], wj[:, 384:512]
    col = lambda i: wj[:, 512 + i:513 + i]
    cols4 = lambda x: x.rearrange("p (c t) -> p c t", c=4)
    TURNS = 8
    pe_n, dve_n, act_n, pool_n = rwkv_events()
    E_pe, E_dve = Events(k.mm, pe_n, TURNS), Events(k.dve, dve_n, TURNS)
    E_act, E_pool = Events(k.act, act_n, TURNS), Events(k.pool, pool_n, TURNS)
    chunk = lambda z, i: i if z == 0 else 3 - i
    cm = k.cmask
    bc4 = lambda m: m.unsqueeze(1).unsqueeze(1).to_broadcast([P, 2, 2, P])
    psb = lambda b, i: k.ps[:, b:b + 2, :].rearrange("p h (b i t) -> p h b i t", b=2, i=2)[:, :, :, i, :]
    flat = lambda t: t.rearrange("p h b t -> p (h b t)")

    def update(dve, link, W_, p, i, z):
        ch = chunk(z, i)
        cout = 4 + ch if z == 0 else ch
        W_(E_pe, p + f"u{i}{z}")
        for h in range(2):
            q = slice(64 * h, 64 * h + 64)
            link(dve.scalar_tensor_tensor(St[z][q, q], k.ps[q, 4 + 2 * z, q], IO[z][q, cout:cout + 1], hatO[z][q, q],
                                          ALU.mult, ALU.add))

    with nc.Block() as block:
        @block.vector
        def _(dve):
            for z in range(2):
                dve.memset(SA[z], 0.0)
                dve.memset(RHS[z], 0.0)
            dve.memset(VC, 0.0)
            link = Link(k.dvel, dve)
            link(dve.memset(reset, 1.0))
            link(dve.memset(cols4(reset)[:, :, 0:1], 0.0))
            link.close()

        @block.sync
        def _(sp):
            sp.dma_start(cm[:, :], k.a["chunk_masks"]).then_inc(k.dma.sem, 16)
            sp.wait_ge(k.dma.sem, k.dma.at(16))
    k.dma.base += 16

    with nc.Block() as block:
        @block.sync
        def _(sp):
            with sp.Fori(0, TURNS) as j:
                sp.wait_ge(k.dve.sem, E_dve.at(j, None))
                sp.dma_start(rkv, k.a["rkv"][bass.ds(j, 1)].rearrange("a p i t -> (a p) i t")).then_inc(k.dma.sem, 16)
                sp.dma_start(wj, k.a["rw_tiles"][bass.ds(j, 1)].rearrange("a p n -> (a p) n")).then_inc(k.dma.sem, 16)

        @block.tensor
        def _(pe):
            with pe.Fori(0, TURNS) as j:
                W_ = lambda E, n: pe.wait_ge(E.s.sem, E.at(j, n))
                pe.wait_ge(k.dma.sem, j * 32 + k.dma.at(32))
                for ph in range(2):
                    p = f"{ph}."
                    if ph:
                        W_(E_dve, "0.end")
                    mm = pe.matmul(k.ps[:, 0, 0:256], lhsT=wa2, rhs=TA[:, ph, :], start=True, stop=True)
                    for z in range(2):
                        mm = pe.matmul(k.ps[:, z, 256 * (1 - z):256 * (2 - z)], lhsT=ww2[z], rhs=TW[:, ph, :], start=True, stop=True)
                    mm = pe.matmul(k.ps[:, 1, 256:512], lhsT=wg2, rhs=TG[:, ph, :], start=True, stop=True)
                    E_pe.fire(mm, p + "low")
                    for b in range(2):
                        mm = pe.transpose(k.ps[:, 2, b * P:(b + 1) * P], rkv[:, 2, ph * S + b * P:ph * S + (b + 1) * P], k.ident)
                    E_pe.fire(mm, p + "vt")
                    W_(E_dve, p + "kk0")
                    mm = pe.matmul(k.ps[:, 3, 0:256], lhsT=k.hblock, rhs=e[1][0], start=True, stop=True)
                    E_pe.fire(mm, p + "ss")
                    for z in range(2):
                        W_(E_pool, p + f"mk{z}")
                        if z:
                            W_(E_dve, p + "ge0")
                        for i in range(2):
                            for h in range(2):
                                for b in range(2):
                                    bc = slice(b * P, (b + 1) * P)
                                    n = 1 + ph
                                    mm = pe.matmul(k.ps[:, 4 + 2 * i + h, b * 256:b * 256 + n * P].rearrange("p (i t) -> p i t", i=n),
                                                   lhsT=masked[z][:, i, h, bc], rhs=AR[z][:, 0:n, bc], start=True, stop=True)
                        E_pe.fire(mm, p + f"gram{z}")
                    for z in range(2):
                        if z == 0:
                            W_(E_act, p + "vtok")
                        else:
                            W_(E_act, p + "nrm")
                        for i in range(2):
                            for b in range(2):
                                mm = pe.transpose(k.ps[:, 2 + z, (2 * i + b) * P:(2 * i + b + 1) * P],
                                                  BK[z][:, i, b * P:(b + 1) * P], k.ident)
                        E_pe.fire(mm, p + f"tok{z}")
                    for z in range(2):
                        W_(E_dve, p + f"mt{z}")
                        if z == 0:
                            W_(E_act, p + "g")
                        for n in range(4):
                            mm = pe.transpose(k.ps[:, z, n * P:(n + 1) * P], MT[z][:, n // 2, n % 2, :], k.ident)
                        E_pe.fire(mm, p + f"m1_{z}")
                    for l in range(1, 6):
                        for z in range(2):
                            W_(E_pool, p + f"ot{l}{z}")
                            W_(E_act, p + f"m1c{z}") if l == 1 else W_(E_dve, p + f"mn{l - 1}{z}")
                            for n in range(4):
                                mm = pe.matmul(k.ps[:, z, n * P:(n + 1) * P], lhsT=OT[z][:, n // 2, n % 2, :],
                                               rhs=M[z][:, n // 2, n % 2, :], start=True, stop=True)
                            E_pe.fire(mm, p + f"t{l}{z}")
                        for z in range(2):
                            W_(E_act, p + f"tc{l}{z}")
                            if l == 1:
                                W_(E_dve, p + "ge1")
                            for n in range(4):
                                q = (n // 2, n % 2)
                                mm = pe.matmul(k.ps[:, 4 + 2 * z, n * P:(n + 1) * P], lhsT=T1[z][:, q[0], q[1], :],
                                               rhs=MT[z][:, q[0], q[1], :], start=True, stop=True)
                                if l < 5:
                                    mm = pe.matmul(k.ps[:, 5 + 2 * z, n * P:(n + 1) * P], lhsT=MT[z][:, q[0], q[1], :],
                                                   rhs=T1[z][:, q[0], q[1], :], start=True, stop=True)
                            E_pe.fire(mm, p + f"n{l}{z}")
                    for z in range(2):
                        W_(E_act, p + f"tokc{z}")
                        for b in range(2):
                            for h in range(2):
                                mm = pe.matmul(k.ps[:, 2 + z, b * P + h * 64:b * P + h * 64 + 64], lhsT=KA[z][:, h, b, :],
                                               rhs=Vt[:, b, h * 64:h * 64 + 64], start=True, stop=True)
                        E_pe.fire(mm, p + f"rv{z}")
                    for i in range(4):
                        for z in range(2):
                            ch = chunk(z, i)
                            r = 64 * (ch % 2)
                            W_(E_dve, p + f"h{i}{z}")
                            mm = pe.matmul(k.ps[r:r + 64, z, 0:P], lhsT=AR[z][:, 0, ch * 64:ch * 64 + 64],
                                           rhs=hat[z][i % 2], start=True, stop=True)
                            E_pe.fire(mm, p + f"r{i}{z}")
                        for z in range(2):
                            ch = chunk(z, i)
                            b, r = ch // 2, 64 * (ch % 2)
                            W_(E_dve, p + f"rh{i}{z}")
                            if i == 0:
                                W_(E_dve, p + f"mn5{z}")
                            for h in range(2):
                                mm = pe.matmul(k.ps[r:r + 64, z, h * 64:h * 64 + 64], lhsT=MT[z][:, h, b, r:r + 64],
                                               rhs=RHS[z][:, h * 64:h * 64 + 64], start=True, stop=True)
                            E_pe.fire(mm, p + f"s{i}{z}")
                        for z in range(2):
                            ch = chunk(z, i)
                            b, par = ch // 2, ch % 2
                            r = 64 * par
                            W_(E_act, p + f"sc{i}{z}")
                            pe.matmul(k.ps[:, 4 + 2 * z, 0:P], lhsT=tok[z][:, 0, b, :], rhs=SA[z][:, par, :], start=True, stop=False)
                            mm = pe.matmul(k.ps[:, 4 + 2 * z, 0:P], lhsT=tok[z][:, 1, b, :], rhs=VC[:, par, b, :], start=False, stop=True)
                            E_pe.fire(mm, p + f"u{i}{z}")
                            if ph:
                                yo = k.ps[:, 5 + 2 * z, ch * 64:ch * 64 + 64]
                                mm = pe.matmul(yo, lhsT=hat[z][i % 2], rhs=AR[z][:, 1, ch * 64:ch * 64 + 64], start=True, stop=False,
                                               skip_group_check=True)
                                for h in range(2):
                                    yh = k.ps[64 * h:64 * h + 64, 5 + 2 * z, ch * 64:ch * 64 + 64]
                                    pe.matmul(yh, lhsT=SA[z][:, par, h * 64:h * 64 + 64], rhs=BR[z][:, h, b, r:r + 64],
                                              start=False, stop=False, skip_group_check=True)
                                    mm = pe.matmul(yh, lhsT=VC[:, par, b, h * 64:h * 64 + 64], rhs=KR[z][:, h, b, r:r + 64],
                                                   start=False, stop=True, skip_group_check=True)
                    if ph:
                        E_pe.fire(mm, p + "y")
                        W_(E_dve, p + "rk")
                        E_pe.fire(pe.matmul(k.ps[:, 0, 0:S], lhsT=k.hblock, rhs=T1[0].rearrange("p h b t -> p (h b t)")[:, 0:256],
                                            start=True, stop=True), p + "bonus")
                        W_(E_dve, p + "yy")
                        E_pe.fire(pe.matmul(k.ps[:, 2, 0:S], lhsT=k.hblock, rhs=flat(M[0])[:, 0:256], start=True, stop=True), p + "mean")
                        W_(E_act, p + "ysq")
                        E_pe.fire(pe.matmul(k.ps[:, 3, 0:S], lhsT=k.hblock, rhs=flat(M[1])[:, 0:256], start=True, stop=True), p + "var")

        @block.scalar
        def _(act):
            with act.Fori(0, TURNS) as j:
                W_ = lambda E, n: act.wait_ge(E.s.sem, E.at(j, n))

                def go(name, *args, **kw):
                    E_act.fire(act.activation(*args, **kw), name)
                act.wait_ge(k.dma.sem, j * 32 + k.dma.at(32))
                for ph in range(2):
                    p = f"{ph}."
                    if ph:
                        W_(E_dve, "0.end")
                    W_(E_pe, p + "low")
                    for z in range(2):
                        go(p + f"sg{z}", inc[z], k.ps[:, z, 256 * (1 - z):256 * (2 - z)], ACT.Sigmoid, bias=col(z))
                    go(p + "a", a_, k.ps[:, 0, 0:256], ACT.Sigmoid, bias=col(2))
                    go(p + "g", g_, k.ps[:, 1, 256:512], ACT.Copy)
                    W_(E_pe, p + "vt")
                    vt = k.ps[:, 2, 0:256].rearrange("p (b v) -> p b v", b=2)
                    act.activation(VC[0:64, 0, :, :], vt[0:64], ACT.Copy)
                    act.activation(VC[64:128, 1, :, :], vt[64:128], ACT.Copy)
                    go(p + "vtok", Vt, vt, ACT.Copy)
                    W_(E_pe, p + "ss")
                    go(p + "nrm", e[1][1], k.ps[:, 3, 0:256], ACT.Sqrt)
                    for z in range(2):
                        W_(E_dve, p + f"ref{z}")
                        go(p + f"io{z}", IO[z], ru[z], ACT.Exp)
                        W_(E_dve, p + f"ie{z}")
                        src = [(inc[z], 1.0), (exc[z], 1.0), (inc[z], -1.0)] if z == 0 else \
                              [(exc[z], -1.0), (inc[z], -1.0), (exc[z], 1.0)]
                        for n, (x, sc) in enumerate(src):
                            go(p + f"e{n}{z}", e[z][n], x, ACT.Exp, scale=sc)
                    for z in range(2):
                        W_(E_pe, p + f"tok{z}")
                        go(p + f"tokc{z}", tok[z].rearrange("p i b v -> p (i b v)"), k.ps[:, 2 + z, :], ACT.Copy)
                    for z in range(2):
                        W_(E_pe, p + f"m1_{z}")
                        go(p + f"m1c{z}", flat(M[z]), k.ps[:, z, :], ACT.Copy)
                    for l in range(1, 6):
                        for z in range(2):
                            W_(E_pe, p + f"t{l}{z}")
                            go(p + f"tc{l}{z}", flat(T1[z]), k.ps[:, z, :], ACT.Copy)
                    for z in range(2):
                        W_(E_pe, p + f"rv{z}")
                        go(p + f"rvc{z}", RV[z], k.ps[:, 2 + z, 0:256], ACT.Copy)
                    for i in range(4):
                        for z in range(2):
                            par = chunk(z, i) % 2
                            r = slice(64 * par, 64 * par + 64)
                            W_(E_pe, p + f"s{i}{z}")
                            go(p + f"sc{i}{z}", SA[z][r, par, :], k.ps[r, z, 0:P], ACT.Copy, scale=-1.0)
                    if ph:
                        W_(E_pe, p + "y")
                        go(p + "yc", flat(M[0])[:, 0:256], k.ps[:, 7, 0:256], ACT.Copy)
                        W_(E_dve, p + "yd")
                        go(p + "ysq", flat(M[1])[:, 0:256], flat(M[0])[:, 256:512], ACT.Square)
                        W_(E_dve, p + "yv")
                        go(p + "yrt", flat(M[1])[:, 256:512], flat(M[1])[:, 256:512], ACT.Sqrt)

        @block.gpsimd
        def _(pool):
            with pool.Fori(0, TURNS) as j:
                W_ = lambda E, n: pool.wait_ge(E.s.sem, E.at(j, n))
                for ph in range(2):
                    p = f"{ph}."
                    for z in range(2):
                        W_(E_dve, p + f"ab{z}")
                        for h in range(2):
                            ins = pool.tensor_tensor(masked[z][:, :, h, :], BK[z],
                                                     k.v("hmask", h).unsqueeze(2).to_broadcast([P, 2, S]), ALU.mult)
                        E_pool.fire(ins, p + f"mk{z}")
                    for l in range(1, 6):
                        for z in range(2):
                            if l == 1:
                                W_(E_dve, p + f"ge{z}")
                            else:
                                W_(E_pe, p + f"t{l - 1}{z}")
                            m = k.level[z][:, l * P:(l + 1) * P]
                            E_pool.fire(pool.tensor_tensor(OT[z], LT[z], bc4(m), ALU.mult), p + f"ot{l}{z}")

        @block.vector
        def _(dve):
            link = Link(k.dvel, dve)
            with dve.Fori(0, TURNS) as j:
                link.loop(j, RW_LINKS)
                W_ = lambda E, n: dve.wait_ge(E.s.sem, E.at(j, n))

                def fire(name, ins):
                    E_dve.fire(ins, name)
                    W_(E_dve, name)
                dve.wait_ge(k.dma.sem, j * 32 + k.dma.at(32))
                for z in range(2):
                    link(dve.memset(St[z], 0.0))
                    link(dve.memset(hat[z][0], 0.0))
                for ph in range(2):
                    p = f"{ph}."
                    cols = slice(ph * S, ph * S + S)
                    r_, kx, vx = (rkv[:, n, cols] for n in range(3))
                    kk0, sq, nrm = kk, e[1][0], e[1][1]
                    link(dve.tensor_scalar(kk0, kx, col(3), None, ALU.mult))
                    fire(p + "kk0", dve.tensor_tensor(sq, kk0, kk0, ALU.mult))
                    W_(E_act, p + "nrm")
                    link(dve.tensor_scalar(nrm, nrm, 1e-12, None, ALU.max))
                    link(dve.reciprocal(nrm, nrm))
                    link(dve.tensor_tensor(kk, kk0, nrm, ALU.mult))
                    link(dve.tensor_tensor(ka, kk, a_, ALU.mult))
                    link(dve.tensor_scalar(k2, a_, 1.0, col(4), ALU.subtract, ALU.mult))
                    link(dve.scalar_tensor_tensor(k2, k2, 1.0, kx, ALU.add, ALU.mult))
                    for z in range(2):
                        link(dve.tensor_scalar(exc[z], inc[z], -float(np.exp(-0.5)), None, ALU.mult))
                        link(dve.tensor_tensor_scan(inc[z], reset, exc[z], 0.0, ALU.mult, ALU.add))
                        C4 = cols4(inc[z])
                        ref, rest = ru[z][:, 0:4], ru[z][:, 4:8]
                        link(dve.tensor_copy(ref.unsqueeze(2), C4[:, :, 31:32]))
                        fire(p + f"ref{z}", dve.tensor_tensor(rest.unsqueeze(2), C4[:, :, 63:64], ref.unsqueeze(2), ALU.subtract))
                        link(dve.tensor_tensor(C4, C4, ref.unsqueeze(2).to_broadcast([P, 4, 64]), ALU.subtract))
                        fire(p + f"ie{z}", dve.tensor_tensor(exc[z], inc[z], exc[z], ALU.subtract))
                    for z in range(2):
                        W_(E_act, p + f"e2{z}")
                        link(dve.tensor_tensor(AR[z][:, 0, :], kk, e[z][1], ALU.mult))
                        link(dve.tensor_tensor(AR[z][:, 1, :], r_, e[z][0], ALU.mult))
                        link(dve.tensor_tensor(BK[z][:, 0, :], ka, e[z][2], ALU.mult))
                        fire(p + f"ab{z}", dve.tensor_tensor(BK[z][:, 1, :], k2, e[z][2], ALU.mult))
                    for z in range(2):
                        W_(E_pe, p + f"gram{z}")
                        s_, i_ = bc4(cm[:, (2 * z) * P:(2 * z + 1) * P]), bc4(cm[:, (2 * z + 1) * P:(2 * z + 2) * P])
                        link(dve.tensor_tensor(LT[z], psb(4, 0), s_, ALU.mult))
                        if ph:
                            link(dve.tensor_tensor(BR[z], psb(4, 1), i_, ALU.mult))
                            link(dve.tensor_tensor(KR[z], psb(6, 1), i_, ALU.mult))
                        fire(p + f"ge{z}", dve.tensor_tensor(KA[z], psb(6, 0), s_, ALU.mult))
                        link(dve.tensor_tensor(MT[z], LT[z], bc4(k.level[z][:, 0:P]), ALU.mult))
                        fire(p + f"mt{z}", dve.tensor_tensor(MT[z], bc4(k.ident), MT[z], ALU.subtract))
                    for l in range(1, 6):
                        for z in range(2):
                            W_(E_pe, p + f"n{l}{z}")
                            if l < 5:
                                link(dve.tensor_tensor(flat(M[z]), flat(M[z]), k.ps[:, 5 + 2 * z, :], ALU.subtract))
                            fire(p + f"mn{l}{z}", dve.tensor_tensor(flat(MT[z]), flat(MT[z]), k.ps[:, 4 + 2 * z, :], ALU.subtract))
                    for i in range(4):
                        for z in range(2):
                            ch = chunk(z, i)
                            cin, cout = (ch, 4 + ch) if z == 0 else (4 + ch, ch)
                            if i:
                                update(dve, link, W_, p, i - 1, z)
                            elif z == 0:
                                W_(E_act, p + "io1")
                            link(dve.tensor_scalar(hat[z][i % 2], St[z], IO[z][:, cin:cin + 1], None, ALU.mult))
                            fire(p + f"h{i}{z}", dve.tensor_scalar(hatO[z], hat[z][i % 2], IO[z][:, cout:cout + 1], None, ALU.mult))
                        for z in range(2):
                            ch = chunk(z, i)
                            b, r = ch // 2, slice(64 * (ch % 2), 64 * (ch % 2) + 64)
                            W_(E_pe, p + f"r{i}{z}")
                            if i == 0:
                                W_(E_act, p + f"rvc{z}")
                            fire(p + f"rh{i}{z}", dve.tensor_tensor(RHS[z][r, :], k.ps[r, z, 0:P], RV[z][r, b * P:(b + 1) * P], ALU.add))
                    for z in range(2):
                        update(dve, link, W_, p, 3, z)
                    if ph == 0:
                        fire(p + "end", dve.tensor_copy(k.sm[:, 80:81], St[1][:, 0:1]))
                        continue
                    f0, f1 = flat(M[0]), flat(M[1])
                    y, d, rs = f0[:, 0:256], f0[:, 256:512], f1[:, 256:512]
                    link(dve.tensor_tensor(k2, k2, r_, ALU.mult))
                    fire(p + "rk", dve.tensor_scalar(flat(T1[0])[:, 0:256], k2, col(5), None, ALU.mult))
                    W_(E_act, p + "yc")
                    fire(p + "yy", dve.tensor_tensor(y, y, k.ps[:, 5, 0:256], ALU.add))
                    W_(E_pe, p + "mean")
                    fire(p + "yd", dve.scalar_tensor_tensor(d, k.ps[:, 2, 0:256], -1.0 / 64, y, ALU.mult, ALU.add))
                    W_(E_pe, p + "var")
                    fire(p + "yv", dve.tensor_scalar(rs, k.ps[:, 3, 0:256], 1.0 / 64, 64e-5, ALU.mult, ALU.add))
                    W_(E_act, p + "yrt")
                    link(dve.reciprocal(rs, rs))
                    link(dve.scalar_tensor_tensor(d, d, col(6), rs, ALU.mult, ALU.mult))
                    link(dve.tensor_tensor(y, k.ps[:, 0, 0:256], vx, ALU.mult))
                    link(dve.scalar_tensor_tensor(d, d, col(7), y, ALU.add, ALU.add))
                    dst = H[:, bass.ds(j, 1), LAT].rearrange("p a t -> p (a t)")
                    fire(p + "end", dve.tensor_tensor(dst, d, g_, ALU.mult))
                link.end_loop(TURNS)
            link.close()

    for E in (E_pe, E_dve, E_act, E_pool):
        E.close()
    k.dma.base += 32 * TURNS

def block2_rwkv(k):
    both = slice(0, T)
    stage_ada2(k, 1)
    stage_norm2(k, 1, 0, both)
    stage_rwkv_project(k)
    stage_rwkv(k)
    Y = k.W[:, 11264:15360].rearrange("p (o t) -> p o t", o=KD)
    stage_square(k, LAT, Y)
    stage_post_norm(k, 1, 0, LAT, Y)
    stage_norm2(k, 1, 1, LAT)
    stage_conv_ffn(k, 1, LAT, Y)
    stage_post_norm(k, 1, 1, LAT, Y)


def stage_store(k, name, src):
    with k.nc.Block() as block:
        @block.sync
        def _(sp):
            sp.dma_start(k.a[name], src).then_inc(k.dma.sem, 16)
            sp.wait_ge(k.dma.sem, k.dma.at(16))
    k.dma.base += 16


def block1(k):
    gate = lambda i: (lambda o: k.mod1[:, i, 16 + o:17 + o])
    stage_ada1(k, 0, 2)
    stage_norm1(k, 0)
    stage_conv_in(k)
    stage_out_residual(k, gate(0))
    stage_norm1(k, 1)
    stage_swiglu(k, 1, 1)
    stage_ada1(k, 2, 2)
    stage_norm1(k, 2)
    stage_attention(k)
    stage_out_residual(k, gate(2))
    stage_norm1(k, 3)
    stage_router(k)
    stage_swiglu(k, 3, NE)
    stage_norm(k, LAT, lambda t, h: k.v("final_g", t), None, dst=k.X)


def build(nc, aps):
    k = Kernel(nc, aps)
    k.a["rkv"] = nc.dram_tensor("rkv", (KD, P, 3, T), F32, kind="Internal").ap()
    stage_load(k)
    block1(k)
    block2_even(k)
    block2_rwkv(k)
    stage_store(k, "out", k.X[:, :, LAT])


def tiles(w):
    kk, n = w.shape
    kp, np_ = -(-kk // P) * P, -(-n // P) * P
    if (kp, np_) != (kk, n):
        w = np.pad(w, ((0, kp - kk), (0, np_ - n)))
    return w.reshape(kp // P, P, np_ // P, P).transpose(2, 0, 1, 3)


def units(t):
    t = t.reshape(-1, P, P)
    pad = -len(t) % UT
    if pad:
        t = np.concatenate([t, np.zeros((pad, P, P), t.dtype)])
    return t.reshape(-1, UT, P, P).transpose(0, 2, 1, 3).reshape(-1, P, UT * P)


def moving(w):
    n = w.shape[1]
    np_ = -(-n // 256) * 256
    w = np.pad(w, ((0, 0), (0, np_ - n)))
    return w.reshape(KD, P, np_ // 256, 256).transpose(2, 1, 0, 3).reshape(-1, P, KD * 256)


def cols(v):
    return np.ascontiguousarray(v).reshape(-1, P).T


def swiglu_units(g, u, d):
    gu = np.stack([tiles(g), tiles(u)], axis=1).reshape(-1, P, P)
    return units(np.concatenate([gu, tiles(d).reshape(-1, P, P)]))


def constants():
    i = np.arange(P)
    out = [np.eye(P), np.ones((P, P))]
    rot = np.zeros((P, P))
    for m in range(P):
        rot[m + 32 if m % 64 < 32 else m - 32, m] = -1.0 if m % 64 < 32 else 1.0
    out.append(rot)
    s, t = i[:, None], i[None, :]
    fwd = [((s >> l) % 2 == 0) & ((t >> l) % 2 == 1) & (s >> (l + 1) == t >> (l + 1)) for l in range(7)]
    out += fwd + [m.T for m in fwd]
    out.append(s // 64 == t // 64)
    return np.concatenate([np.asarray(o, np.float32) for o in out], axis=1)


def layout(i):
    q, kx, v = np.split(i["attn_w_qkv"][0], 3, axis=1)
    pad64 = lambda w: np.pad(w, ((0, 0), (0, 64)))
    parts = [units(tiles(i["mod_w"][0, 0])), units(tiles(i["mod_w"][0, 1])),
             units(tiles(i["conv_w_in"][0])), units(tiles(i["conv_w_out"][0])),
             swiglu_units(i["ffn_w_gate"][0], i["ffn_w_up"][0], i["ffn_w_down"][0]),
             units(tiles(i["mod_w"][1, 0])), units(tiles(i["mod_w"][1, 1])),
             units(tiles(np.concatenate([pad64(q), pad64(kx)], axis=1))), moving(v),
             units(tiles(i["attn_w_o"][0]))]
    parts += [swiglu_units(i["moe_w_gate"][0, e], i["moe_w_up"][0, e], i["moe_w_down"][0, e]) for e in range(NE)]
    vectors = np.zeros((P, NVEC), np.float32)

    def put(name, a):
        vectors[:, VEC[name]] = a
    put("c", cols(i["c"]))
    put("c2", np.stack([cols(i["c_ctx_2"]), cols(i["c_2"])], axis=2).reshape(P, 16))
    put("norm_g", cols(i["norm_g"]))
    put("mod_b", cols(i["mod_b"]))
    put("final_g", cols(i["final_g"]))
    put("conv_w", cols(i["conv_w"]))
    put("router", i["router_w"][0].reshape(KD, P, NE).transpose(1, 0, 2).reshape(P, -1))
    put("hmask", np.repeat(np.eye(2, dtype=np.float32), 64, axis=0))
    inv = np.float32(10000.0) ** (-np.arange(0, 64, 2, dtype=np.float32) / np.float32(64))
    put("invf", np.tile(inv, 4)[:, None])
    put("mod_b2", cols(i["b_mod_2"]))
    put("norm_g2", cols(i["norm_g_2"]))
    tok = lambda x: x.T.reshape(KD, P, S).transpose(1, 0, 2)
    w = i["ev_w_in_2"][0]
    at = np.cumsum([0, 512, 512, 512, 512, 16, 256, 256, 512, 512, 32])
    mq, mk, mv, mo, mg, gq, gk, gv, gg, glr = (w[:, a:b] for a, b in zip(at[:-1], at[1:]))
    glr_t, in_t, f_t = (np.zeros((D, P), np.float32) for _ in range(3))
    glr_t[:, 0:16], glr_t[:, 32:48] = glr[:, 0:16], glr[:, 16:32]
    bias = np.zeros((P, 2), np.float32)
    bg = i["ev_b_gates_2"][0]
    for z in range(2):
        in_t[:, 32 * z:32 * z + 4], f_t[:, 32 * z:32 * z + 4] = mg[:, 8 * z:8 * z + 4], mg[:, 8 * z + 4:8 * z + 8]
        bias[32 * z:32 * z + 4, 0], bias[32 * z:32 * z + 4, 1] = bg[8 * z:8 * z + 4], bg[8 * z + 4:8 * z + 8]
    up = lambda l: np.split(i["ffn_w_up_2"][l], 2, axis=1)
    parts += [units(tiles(i["w_mod_2"][0])),
              units(tiles(np.concatenate([mq, mk, gq, gk, glr_t, in_t, f_t, mo, gg], axis=1))),
              moving(np.concatenate([mv, gv], axis=1)),
              units(tiles(i["ev_w_out_2"][0])),
              swiglu_units(*up(0), i["ffn_w_down_2"][0])]
    h64 = lambda w: np.pad(w, ((0, 0), (0, 64)))
    parts += [units(tiles(i["w_mod_2"][1])),
              units(tiles(np.concatenate([i["rw_w_rkv_2"][0, 0], i["rw_w_rkv_2"][0, 1], i["rw_w_rkv_2"][0, 2],
                                          i["rw_w1_2"][0, 0], i["rw_w1_2"][0, 1], h64(i["rw_a1_2"][0]),
                                          i["rw_g1_2"][0]], axis=1))),
              units(tiles(i["rw_w_o_2"][0])),
              swiglu_units(*up(1), i["ffn_w_down_2"][1])]
    put("mu", cols(i["rw_mu_2"][0]))
    rw = np.zeros((KD, P, 520), np.float32)
    by_tile = lambda w: w.reshape(w.shape[0], KD, P).transpose(1, 0, 2)
    rw[:, 0:64, 0:128] = by_tile(i["rw_a2_2"][0])
    rw[:, 0:64, 128:256] = by_tile(i["rw_w2_2"][0, 0])
    rw[:, 64:128, 256:384] = by_tile(i["rw_w2_2"][0, 1])
    rw[:, :, 384:512] = by_tile(i["rw_g2_2"][0])
    for n, v in enumerate([*i["rw_w0_2"][0], i["rw_a0_2"][0], *i["rw_kvec_2"][0], *i["rw_lnx_2"][0]]):
        rw[:, :, 512 + n] = v.reshape(KD, P)
    u, t = np.arange(P)[:, None], np.arange(P)[None, :]
    own = u // CH == t // CH
    chunk_masks = np.concatenate([own & (u < t), own & (u <= t), own & (u > t), own & (u >= t)], axis=1).astype(np.float32)
    put("fcw", cols(i["ffn_conv_w_2"]))
    put("fcb", cols(i["ffn_conv_b_2"]))
    put("ecw", cols(i["ev_conv_w_2"][0]))
    put("ecb", cols(i["ev_conv_b_2"][0]))
    put("ebg", bias)
    put("glab", cols(i["ev_gla_b_2"][0]))
    put("headg", cols(i["ev_head_g_2"][0]))
    gw2 = np.zeros((P, 2, 256), np.float32)
    gw2[0:16, 0], gw2[32:48, 1] = i["ev_gla_w2_2"][0]
    t, s = np.arange(S)[:, None], np.arange(S)[None, :]
    scan = np.stack([(t <= s), (t >= s)]).astype(np.float32).reshape(2, 2, P, S).transpose(2, 0, 1, 3)
    mask = [np.where((t >= s) & ((t - s) % dil == 0) & (t - s <= win), 0.0, -1e30).reshape(2, P, S)
            for win, dil in GROUPS]
    return parts, {
        "vectors": vectors,
        "tokens": np.ascontiguousarray(np.concatenate([tok(i["ctx_2"][0]), tok(i["x"][0])], axis=2)),
        "constants": constants(),
        "scan_mask": np.ascontiguousarray(scan.reshape(P, -1)),
        "chunk_masks": chunk_masks,
        "rw_tiles": rw,
        "gla_w2": gw2.reshape(P, -1),
        "positions": np.ascontiguousarray(np.broadcast_to(i["positions"], (P, S))),
        "attn_mask": np.ascontiguousarray(np.concatenate(mask).transpose(1, 0, 2).astype(np.float32)),
    }


def kernel(**inputs):
    import concourse.bacc as bacc
    from concourse.bass_utils import run_bass_kernel_spmd
    parts, arrays = layout({n: np.asarray(a) for n, a in inputs.items()})
    arrays["weights"] = np.concatenate(parts)
    nc = bacc.Bacc("TRN2", target_bir_lowering=False, num_devices=1)
    aps = {n: nc.dram_tensor(n, a.shape, mybir.dt.from_np(a.dtype), kind="ExternalInput").ap() for n, a in arrays.items()}
    aps["out"] = nc.dram_tensor("out", (P, KD, S), F32, kind="ExternalOutput").ap()
    build(nc, aps)
    r = run_bass_kernel_spmd(nc, [arrays], core_ids=[0])
    got = r.results[0]["out"]
    return np.ascontiguousarray(got.transpose(1, 0, 2).reshape(D, S).T)[None]
```

```python
import numpy as np
import concourse.bass as bass
from concourse import mybir

F32 = mybir.dt.float32
I32 = mybir.dt.int32
U32 = mybir.dt.uint32
ALU = mybir.AluOpType
ACT = mybir.ActivationFunctionType
AX = mybir.AxisListType

P = 128
D = 1024
KD = D // P
S = 256
T = 2 * S
F = 2816
KF = F // P
NE = 8
NHEAD = 15
GROUPS = ((128, 1), (512, 4), (2048, 16))
EPS = 1e-6
RW_LINKS = 125
RING = 11
UT = 16
EXPERT_UNITS = (2 * KF * KD + KF * KD) // UT
LAT = slice(S, T)
CTX = slice(0, S)
GRID_W = 64
CH = 64
NB = T // P


def vec_layout():
    sizes = [("c", 8), ("c2", 16), ("norm_g", 32), ("mod_b", 96), ("final_g", 8), ("conv_w", 24),
             ("router", 64), ("hmask", 2), ("invf", 1),
             ("mod_b2", 96), ("norm_g2", 64), ("fcw", 2 * 9 * KF), ("fcb", 2 * KF),
             ("ecw", 24), ("ecb", 8), ("ebg", 2), ("glab", 4), ("headg", 8),
             ("mu", 48), ("lnx", 16)]
    at, out = 0, {}
    for name, n in sizes:
        out[name] = slice(at, at + n)
        at += n
    return out, at


VEC, NVEC = vec_layout()
U_ADA1 = 12
U_CONV_IN, U_SQ = 12, 4
U_UP, U_DOWN = 22, 11
U_ADA2 = 24
U_EV = 12
NCONST = 3 * P + 14 * P + P


class Signal:

    def __init__(self, nc, name):
        self.sem = nc.alloc_semaphore(name)
        self.base = 0

    def at(self, n):
        return self.base + n


class Link:

    def __init__(self, signal, eng):
        self.s, self.eng, self.n, self.turn, self.per = signal, eng, 0, None, 0

    def loop(self, turn, per):
        self.turn, self.per, self.start = turn, per, self.n

    def value(self):
        if self.turn is None:
            return self.s.base + self.n
        return self.turn * self.per + (self.s.base + self.n)

    def __call__(self, ins):
        self.mark(ins)
        self.eng.wait_ge(self.s.sem, self.value())

    def mark(self, ins):
        ins.then_inc(self.s.sem, 1)
        self.n += 1

    def wait(self):
        self.eng.wait_ge(self.s.sem, self.value())

    def end_loop(self, turns):
        assert self.n - self.start == self.per, f"{self.s.sem}: {self.n - self.start} a turn, not {self.per}"
        self.n = self.start + self.per * turns
        self.turn = None

    def close(self):
        self.s.base += self.n


class Kernel:

    def __init__(self, nc, aps):
        self.nc, self.a = nc, aps
        sb = lambda name, shape, dt=F32: nc.alloc_sbuf_tensor(name, shape, dt)
        self.ring = sb("ring", [P, RING, UT * P])
        self.X = sb("X", [P, KD, T])
        self.H = sb("H", [P, KD, T])
        self.W = sb("W", [P, 16384])
        self.vec = sb("vec", [P, NVEC])
        self.const = sb("const", [P, NCONST])
        self.mod1 = sb("mod1", [P, 4, 24])
        self.mod2 = sb("mod2", [P, 2, 48, 2])
        self.cs = sb("cs", [P, 24])
        self.sm = sb("sm", [P, 512])
        self.ps = nc.alloc_psum_tensor("ps", [P, 8, 512], F32)
        c = lambda i, n=1: self.const[:, i * P:(i + n) * P]
        self.ident, self.ones, self.prot = c(0), c(1), c(2)
        self.level = [c(3, 7), c(10, 7)]
        self.hblock = c(17)
        self.hat = sb("hat", [P, 4, P])
        self.cmask = sb("cmask", [P, 4 * P])
        self.stored = [nc.alloc_semaphore(f"stored_{i}") for i in range(4)]
        self.w_in = [nc.alloc_semaphore(f"weights_in_{i}") for i in range(RING)]
        self.unit = 0
        sig = lambda n: Signal(nc, n)
        self.mm = sig("matmul_done")
        self.act = sig("act_done")
        self.dve = sig("dve_done")
        self.pool = sig("pool_done")
        self.dma = sig("dma_done")
        self.pel = sig("tensor_order")
        self.dvel = sig("dve_order")
        self.pooll = sig("pool_order")
        self.mm2, self.act2, self.dve2 = sig("second_matmul_done"), sig("second_act_done"), sig("second_dve_done")
        self.side_in = [nc.alloc_semaphore(f"second_weights_in_{i}") for i in range(4)]
        self.pickl = nc.alloc_semaphore("first_half_picked")
        self.pick_base = 0
        self.ctx_in, self.lat_in = nc.alloc_semaphore("rwkv_context_in"), nc.alloc_semaphore("rwkv_latents_in")
        self.turns_over = nc.alloc_semaphore("second_slots_over")

    def v(self, name, i=0, n=1):
        s = VEC[name].start + i
        return self.vec[:, s:s + n]

    def slot(self, u):
        return (self.unit + u) % RING

    def landed(self, u):
        return 16 * ((self.unit + u) // RING + 1)


def plan(owner):
    unit_done, out_done, signals, n = {}, {}, set(), 0
    for i, o in enumerate(owner):
        ends_unit = i % UT == UT - 1 or i == len(owner) - 1
        ends_out = i == len(owner) - 1 or owner[i + 1] != o
        if ends_unit or ends_out:
            n += 1
            signals.add(i)
        if ends_unit:
            unit_done[i // UT] = n
        if ends_out:
            out_done[o] = n
    return unit_done, out_done, signals, n


def refill(k, sp, unit_done, n_units, turn=None, per=0, total_units=None):
    for u in range(n_units):
        if turn is None:
            if k.unit + u + RING >= k.a["weights"].shape[0]:
                break
            sp.wait_ge(k.mm.sem, k.mm.at(unit_done[u]))
            src = k.a["weights"][k.unit + u + RING]
        else:
            sp.wait_ge(k.mm.sem, turn * per + k.mm.at(unit_done[u]))
            src = k.a["weights"][bass.ds(turn * n_units + (k.unit + u + RING), 1)].squeeze(0)
        sp.dma_start(k.ring[:, k.slot(u), :], src).then_inc(k.w_in[k.slot(u)], 16)


def gemm(k, pe, n_out, kt, rhs, out, before, signals, first=0, turn=None, rounds=0):
    for i in range(first, first + n_out * kt):
        o, kk = divmod(i - first, kt)
        u, p = divmod(i, UT)
        if p == 0 or i == first:
            need = k.landed(u)
            pe.wait_ge(k.w_in[k.slot(u)], need if turn is None else turn * (16 * rounds) + need)
        if kk == 0:
            before(o)
        mm = pe.matmul(out(o), lhsT=k.ring[:, k.slot(u), p * P:(p + 1) * P], rhs=rhs(kk),
                       start=kk == 0, stop=kk == kt - 1)
        if i in signals:
            mm.then_inc(k.mm.sem, 1)


def stage_load(k):
    nc = k.nc
    with nc.Block() as block:
        @block.sync
        def _(sp):
            sp.dma_start(k.vec[:, :], k.a["vectors"]).then_inc(k.dma.sem, 16)
            sp.dma_start(k.X[:, :, :], k.a["tokens"]).then_inc(k.dma.sem, 16)
            sp.dma_start(k.const[:, :], k.a["constants"]).then_inc(k.dma.sem, 16)
            for u in range(RING):
                sp.dma_start(k.ring[:, u, :], k.a["weights"][u]).then_inc(k.w_in[u], 16)
            sp.wait_ge(k.dma.sem, 48)

        @block.scalar
        def _(act):
            act.wait_ge(k.dma.sem, 48)
            act.activation(k.cs[:, :], k.vec[:, VEC["c"].start:VEC["c2"].stop], ACT.Silu).then_inc(k.act.sem, 1)
    k.dma.base += 48
    k.act.base += 1


def modulation(k, n_out, c, width, finish):
    nc = k.nc
    at = width * (n_out - 1)
    part = at + P
    spread = k.W[:, 0:KD * part].rearrange("p (k n) -> p k n", k=KD)
    rows = k.W[:, KD * part:KD * part + P]
    units = n_out * KD // UT
    unit_done, out_done, signals, total = plan([0] * (n_out * KD))
    with nc.Block() as block:
        @block.sync
        def _(sp):
            refill(k, sp, unit_done, units)

        @block.tensor
        def _(pe):
            pe.wait_ge(k.dve.sem, k.dve.at(1))
            for o in range(n_out):
                for kk in range(KD):
                    i = o * KD + kk
                    u, p = divmod(i, UT)
                    if p == 0:
                        pe.wait_ge(k.w_in[k.slot(u)], k.landed(u))
                    start = at - width * o
                    mm = pe.matmul(k.ps[:, 0, 0:P], lhsT=spread[:, kk, start:start + P],
                                   rhs=k.ring[:, k.slot(u), p * P:(p + 1) * P],
                                   start=i == 0, stop=i == n_out * KD - 1)
                    if i in signals:
                        mm.then_inc(k.mm.sem, 1)
            pe.wait_ge(k.act.sem, k.act.at(1))
            pe.transpose(k.ps[:, 1, 0:P], rows, k.ident).then_inc(k.mm.sem, 1)

        @block.scalar
        def _(act):
            act.wait_ge(k.mm.sem, k.mm.at(total))
            act.activation(rows, k.ps[:, 0, 0:P], ACT.Copy).then_inc(k.act.sem, 1)

        @block.vector
        def _(dve):
            link = Link(k.dvel, dve)
            link(dve.memset(k.W[:, 0:KD * part], 0.0))
            dve.tensor_copy(spread[:, :, at:at + width],
                            k.cs[:, c:c + width * KD].rearrange("p (k n) -> p k n", k=KD)).then_inc(k.dve.sem, 1)
            dve.wait_ge(k.mm.sem, k.mm.at(total + 1))
            finish(dve, link, k.ps[:, 1, 0:width * n_out])
            link.close()
    k.mm.base += total + 1
    k.act.base += 1
    k.dve.base += 1
    k.unit += units


def stage_ada1(k, first, count):
    def finish(dve, link, columns):
        m = k.mod1[:, first:first + count, :]
        link(dve.tensor_tensor(m, columns.rearrange("p (a b) -> p a b", b=24),
                               k.v("mod_b", first * 24, 24 * count).rearrange("p (a b) -> p a b", b=24), ALU.add))
        link(dve.tensor_scalar(m[:, :, 8:16], m[:, :, 8:16], 1.0, None, ALU.add))
        for i in range(count):
            link(dve.tensor_tensor(m[:, i, 8:16], m[:, i, 8:16], k.v("norm_g", (first + i) * 8, 8), ALU.mult))
    modulation(k, 24 * count, 0, 1, finish)


def stage_ada2(k, layer):
    def finish(dve, link, columns):
        m = k.mod2[:, layer, :, :]
        link(dve.tensor_tensor(m, columns.rearrange("p (a b) -> p a b", b=2),
                               k.v("mod_b2", layer * 48, 48).unsqueeze(2).to_broadcast([P, 48, 2]), ALU.add))
        for vector, g in ((1, 0), (4, 2)):
            w = m[:, vector * 8:vector * 8 + 8, :]
            link(dve.tensor_scalar(w, w, 1.0, None, ALU.add))
            link(dve.tensor_tensor(w, w, k.v("norm_g2", layer * 32 + g * 8, 8).unsqueeze(2).to_broadcast([P, 8, 2]), ALU.mult))
    modulation(k, 48, 8, 2, finish)


def rms_scale(k, block, src, n, scr, rstd, bank, eps=EPS):
    @block.scalar
    def _(act):
        for i in range(KD):
            act.activation(scr[:, i * n:(i + 1) * n], src(i), ACT.Square).then_inc(k.act.sem, 1)
        act.wait_ge(k.dve.sem, k.dve.at(1))
        act.activation(rstd, rstd, ACT.Sqrt).then_inc(k.act.sem, 1)

    @block.tensor
    def _(pe):
        for i in range(KD):
            pe.wait_ge(k.act.sem, k.act.at(i + 1))
            mm = pe.matmul(k.ps[:, bank, 0:n], lhsT=k.ones, rhs=scr[:, i * n:(i + 1) * n],
                           start=i == 0, stop=i == KD - 1)
        mm.then_inc(k.mm.sem, 1)

    @block.vector
    def _(dve):
        dve.wait_ge(k.mm.sem, k.mm.at(1))
        dve.tensor_scalar(rstd, k.ps[:, bank, 0:n], 1.0 / D, eps, ALU.mult, ALU.add).then_inc(k.dve.sem, 1)
        dve.wait_ge(k.act.sem, k.act.at(KD + 1))
        dve.reciprocal(rstd, rstd).then_inc(k.dve.sem, 1)


def rms_counts(k):
    k.act.base += KD + 1
    k.mm.base += 1
    k.dve.base += 2


def stage_norm(k, cols, scale, shift, dst=None):
    nc = k.nc
    n = cols.stop - cols.start
    halves = [c for c in (CTX, LAT) if c.start >= cols.start and c.stop <= cols.stop]
    dst = k.H if dst is None else dst
    rstd = k.W[:, 8 * T:8 * T + n]
    with nc.Block() as block:
        rms_scale(k, block, lambda i: k.X[:, i, cols], n, k.W, rstd, 7)
    rms_counts(k)
    with nc.Block() as block:
        @block.vector
        def _(dve):
            for i in range(KD):
                for h, c in enumerate(halves):
                    half = 0 if c is CTX else 1
                    r = rstd[:, c.start - cols.start:c.stop - cols.start]
                    dve.scalar_tensor_tensor(dst[:, i, c], k.X[:, i, c], scale(i, half), r,
                                             ALU.mult, ALU.mult).then_inc(k.dve.sem, 1)

        @block.scalar
        def _(act):
            if shift is None:
                return
            for i in range(KD):
                for h, c in enumerate(halves):
                    half = 0 if c is CTX else 1
                    act.wait_ge(k.dve.sem, k.dve.at(i * len(halves) + h + 1))
                    act.activation(dst[:, i, c], dst[:, i, c], ACT.Identity, bias=shift(i, half))
    k.dve.base += KD * len(halves)


def stage_norm1(k, i):
    m = k.mod1
    stage_norm(k, LAT, lambda t, h: m[:, i, 8 + t:9 + t], lambda t, h: m[:, i, t:t + 1])


def stage_conv_in(k):
    nc = k.nc
    n_out = 24
    Z = k.W[:, 0:n_out * S].rearrange("p (o t) -> p o t", o=n_out)
    tmp = k.W[:, n_out * S:n_out * S + 8 * S].rearrange("p (o t) -> p o t", o=8)
    unit_done, out_done, signals, total = plan([i // KD for i in range(n_out * KD)])
    with nc.Block() as block:
        @block.sync
        def _(sp):
            refill(k, sp, unit_done, U_CONV_IN)

        @block.tensor
        def _(pe):
            def before(o):
                if o >= 4:
                    pe.wait_ge(k.act.sem, k.act.at(o - 3))
            gemm(k, pe, n_out, KD, lambda kk: k.H[:, kk, LAT], lambda o: k.ps[:, o % 4, 0:S], before, signals)

        @block.scalar
        def _(act):
            for o in range(n_out):
                act.wait_ge(k.mm.sem, k.mm.at(out_done[o]))
                act.activation(Z[:, o, :], k.ps[:, o % 4, 0:S], ACT.Copy).then_inc(k.act.sem, 1)

        @block.vector
        def _(dve):
            link = Link(k.dvel, dve)
            for i in range(8):
                dve.wait_ge(k.act.sem, k.act.at(17 + i))
                v, y = Z[:, 16 + i, :], tmp[:, i, :]
                w = lambda j: k.v("conv_w", j * 8 + i)
                link(dve.tensor_tensor(v, v, Z[:, 8 + i, :], ALU.mult))
                link(dve.tensor_scalar(y, v, w(2), None, ALU.mult))
                link(dve.scalar_tensor_tensor(y[:, 1:S], v[:, 0:S - 1], w(1), y[:, 1:S], ALU.mult, ALU.add))
                link(dve.scalar_tensor_tensor(y[:, 2:S], v[:, 0:S - 2], w(0), y[:, 2:S], ALU.mult, ALU.add))
            dve.wait_ge(k.mm.sem, k.mm.at(total))
            for i in range(8):
                link.mark(dve.tensor_tensor(k.H[:, i, LAT], tmp[:, i, :], Z[:, i, :], ALU.mult))
            link.close()
    k.mm.base += total
    k.act.base += n_out
    k.unit += U_CONV_IN


def stage_out_residual(k, gate):
    nc = k.nc
    unit_done, out_done, signals, total = plan([i // KD for i in range(8 * KD)])
    with nc.Block() as block:
        @block.sync
        def _(sp):
            refill(k, sp, unit_done, U_SQ)

        @block.tensor
        def _(pe):
            def before(o):
                if o >= 4:
                    pe.wait_ge(k.dve.sem, k.dve.at(o - 3))
            gemm(k, pe, 8, KD, lambda kk: k.H[:, kk, LAT], lambda o: k.ps[:, o % 4, 0:S], before, signals)

        @block.vector
        def _(dve):
            for o in range(8):
                dve.wait_ge(k.mm.sem, k.mm.at(out_done[o]))
                dve.scalar_tensor_tensor(k.X[:, o, LAT], k.ps[:, o % 4, 0:S], gate(o), k.X[:, o, LAT],
                                         ALU.mult, ALU.add).then_inc(k.dve.sem, 1)
    k.mm.base += total
    k.dve.base += 8
    k.unit += U_SQ


def stage_swiglu(k, i):
    nc = k.nc
    m = k.mod1
    owner = [t // KD for t in range(2 * KF * KD)] + [2 * KF + t // KF for t in range(KD * KF)]
    unit_done, out_done, signals, total = plan(owner)
    A = k.W[:, 0:KF * S].rearrange("p (o t) -> p o t", o=KF)
    sil = k.W[:, KF * S:(KF + 2) * S].rearrange("p (o t) -> p o t", o=2)
    down0 = 2 * KF
    with nc.Block() as block:
        @block.sync
        def _(sp):
            refill(k, sp, unit_done, EXPERT_UNITS)

        @block.tensor
        def _(pe):
            def before(o):
                if o >= 4 and o % 2 == 0:
                    pe.wait_ge(k.act.sem, k.act.at(o // 2 - 1))
                elif o >= 4:
                    pe.wait_ge(k.dve.sem, k.dve.at(o // 2 - 1))
            gemm(k, pe, down0, KD, lambda kk: k.H[:, kk, LAT], lambda o: k.ps[:, o % 4, 0:S], before, signals)

            def before_down(o):
                pe.wait_ge(k.dve.sem, k.dve.at(KF if o < 4 else KF + o - 3))
            gemm(k, pe, 8, KF, lambda kk: A[:, kk, :], lambda o: k.ps[:, o % 4, 0:S],
                 before_down, signals, first=down0 * KD)

        @block.scalar
        def _(act):
            for f in range(KF):
                act.wait_ge(k.mm.sem, k.mm.at(out_done[2 * f]))
                if f >= 2:
                    act.wait_ge(k.dve.sem, k.dve.at(f - 1))
                act.activation(sil[:, f % 2, :], k.ps[:, (2 * f) % 4, 0:S], ACT.Silu).then_inc(k.act.sem, 1)

        @block.vector
        def _(dve):
            for f in range(KF):
                dve.wait_ge(k.mm.sem, k.mm.at(out_done[2 * f + 1]))
                dve.wait_ge(k.act.sem, k.act.at(f + 1))
                dve.tensor_tensor(A[:, f, :], k.ps[:, (2 * f + 1) % 4, 0:S], sil[:, f % 2, :],
                                  ALU.mult).then_inc(k.dve.sem, 1)
            for o in range(8):
                dve.wait_ge(k.mm.sem, k.mm.at(out_done[down0 + o]))
                x = k.X[:, o, LAT]
                dve.scalar_tensor_tensor(x, k.ps[:, o % 4, 0:S], m[:, i, 16 + o:17 + o], x,
                                         ALU.mult, ALU.add).then_inc(k.dve.sem, 1)
    k.mm.base += total
    k.act.base += KF
    k.dve.base += KF + 8
    k.unit += EXPERT_UNITS


def stage_attention(k):
    nc = k.nc
    W = k.W
    q2 = W[:, 0:16 * S].rearrange("p (o t) -> p o t", o=16)
    kT = W[:, 16 * S:24 * S].rearrange("p (o t) -> p o t", o=8)
    V = W[:, 24 * S:24 * S + 2 * D].rearrange("p (b d) -> p b d", b=2)
    Pm = W[:, 8192:8192 + 30 * S].rearrange("p (h b s) -> p h b s", h=NHEAD, b=2)
    raw = W[:, 8192:8192 + 16 * S].rearrange("p (o t) -> p o t", o=16)
    HC = k.H[:, :, CTX]
    cos, sin, ang, kk_ = (HC[:, i, :] for i in range(4))
    rot, tmp = HC[:, 4, :], HC[:, 5, :]
    pos = HC[:, 6, :].bitcast(I32)

    owner = [t // KD for t in range(16 * KD)] + [16 + u for u in range(4) for _ in range(UT)]
    unit_done, out_done, signals, total = plan(owner)
    with nc.Block() as block:
        @block.sync
        def _(sp):
            sp.dma_start(pos, k.a["positions"]).then_inc(k.dma.sem, 16)
            refill(k, sp, unit_done, 12)

        @block.tensor
        def _(pe):
            def before(o):
                if o >= 4:
                    pe.wait_ge(k.act.sem, k.act.at(o - 3))
            gemm(k, pe, 16, KD, lambda kk: k.H[:, kk, LAT], lambda o: k.ps[:, o % 4, 0:S], before, signals)
            for u in range(4):
                pe.wait_ge(k.w_in[k.slot(8 + u)], k.landed(8 + u))
                pe.wait_ge(k.act.sem, k.act.at(13 + u))
                for b in range(2):
                    for kk in range(KD):
                        mm = pe.matmul(k.ps[:, u % 4, b * S:(b + 1) * S], lhsT=k.H[:, kk, S + b * P:S + (b + 1) * P],
                                       rhs=k.ring[:, k.slot(8 + u), kk * S:(kk + 1) * S], start=kk == 0, stop=kk == KD - 1)
                mm.then_inc(k.mm.sem, 1)

        @block.scalar
        def _(act):
            for o in range(16):
                act.wait_ge(k.mm.sem, k.mm.at(out_done[o]))
                act.activation(raw[:, o, :], k.ps[:, o % 4, 0:S], ACT.Copy).then_inc(k.act.sem, 1)
            for u in range(4):
                act.wait_ge(k.mm.sem, k.mm.at(out_done[16 + u]))
                act.activation(V[:, :, u * S:(u + 1) * S], k.ps[:, u, :].rearrange("p (b d) -> p b d", b=2),
                               ACT.Copy).then_inc(k.act.sem, 1)

        @block.vector
        def _(dve):
            link = Link(k.dvel, dve)
            two_pi = 2 * np.pi
            c1 = 6.28125
            c2 = float(np.float32(np.round((two_pi - c1) * 2 ** 21) / 2 ** 21))
            c3 = two_pi - c1 - c2
            magic = 1.5 * 2 ** 23
            dve.wait_ge(k.dma.sem, k.dma.at(16))
            link(dve.tensor_copy(ang, pos))
            link(dve.tensor_scalar(ang, ang, k.v("invf"), None, ALU.mult))
            link(dve.tensor_scalar(kk_, ang, 1 / two_pi, magic, ALU.mult, ALU.add))
            link(dve.tensor_scalar(kk_, kk_, magic, None, ALU.subtract))
            for c in (c1, c2, c3):
                link(dve.scalar_tensor_tensor(ang, kk_, -c, ang, ALU.mult, ALU.add))
            lim = 3.141592
            link(dve.tensor_scalar(sin, ang, lim, -lim, ALU.min, ALU.max))
            link(dve.tensor_scalar(cos, ang, np.pi / 2, None, ALU.add))
            link(dve.tensor_scalar(kk_, cos, np.pi, two_pi, ALU.is_gt, ALU.mult))
            link(dve.tensor_tensor(cos, cos, kk_, ALU.subtract))
            link(dve.tensor_scalar(cos, cos, lim, -lim, ALU.min, ALU.max))
            link.close()
    k.dma.base += 16
    k.mm.base += total
    k.act.base += 20
    k.unit += 12

    with nc.Block() as block:
        @block.tensor
        def _(pe):
            for o in range(16):
                if o >= 4:
                    pe.wait_ge(k.dve.sem, k.dve.at(o - 3))
                pe.matmul(k.ps[:, o % 4, 0:S], lhsT=k.prot, rhs=raw[:, o, :], start=True, stop=True).then_inc(k.mm.sem, 1)

        @block.scalar
        def _(act):
            act.activation(sin, sin, ACT.Sin).then_inc(k.act.sem, 1)
            act.activation(cos, cos, ACT.Sin).then_inc(k.act.sem, 1)

        @block.vector
        def _(dve):
            link = Link(k.dvel, dve)
            dve.wait_ge(k.act.sem, k.act.at(2))
            for o in range(16):
                dve.wait_ge(k.mm.sem, k.mm.at(o + 1))
                dve.tensor_tensor(rot, k.ps[:, o % 4, 0:S], sin, ALU.mult).then_inc(k.dve.sem, 1)
                link(dve.tensor_tensor(tmp, raw[:, o, :], cos, ALU.mult))
                dve.wait_ge(k.dve.sem, k.dve.at(o + 1))
                if o < 8:
                    link(dve.tensor_tensor(tmp, tmp, rot, ALU.add))
                    for h in range(2):
                        link(dve.tensor_scalar(q2[:, 2 * o + h, :], tmp, k.v("hmask", h), None, ALU.mult))
                else:
                    link(dve.tensor_tensor(kT[:, o - 8, :], tmp, rot, ALU.add))
            link.close()
    k.dve.base += 16
    k.mm.base += 16
    k.act.base += 2

    mask = k.H[:, 0:6, CTX]
    mx = k.sm[:, 0:30]
    sums = k.sm[:, 32:62]
    lse = k.sm[:, 64:94]
    top = k.sm[:, 96:106]
    den = k.sm[:, 112:122]
    nmx = k.sm[:, 128:158]
    with nc.Block() as block:
        @block.sync
        def _(sp):
            sp.dma_start(mask, k.a["attn_mask"]).then_inc(k.dma.sem, 16)
            sp.wait_ge(k.dma.sem, k.dma.at(16))

        @block.tensor
        def _(pe):
            for h in range(NHEAD):
                if h >= 4:
                    pe.wait_ge(k.dve.sem, k.dve.at(h - 3))
                for b in range(2):
                    mm = pe.matmul(k.ps[:, h % 4, b * S:(b + 1) * S], lhsT=q2[:, h, b * P:(b + 1) * P],
                                   rhs=kT[:, h // 2, :], start=True, stop=True)
                mm.then_inc(k.mm.sem, 1)

        @block.vector
        def _(dve):
            link = Link(k.dvel, dve)
            dve.wait_ge(k.dma.sem, k.dma.at(16))
            for h in range(NHEAD):
                g = h // 5
                dve.wait_ge(k.mm.sem, k.mm.at(h + 1))
                dve.scalar_tensor_tensor(Pm[:, h, :, :], k.ps[:, h % 4, :].rearrange("p (b s) -> p b s", b=2), 0.125,
                                         mask[:, 2 * g:2 * g + 2, :], ALU.mult, ALU.add).then_inc(k.dve.sem, 1)
                dve.wait_ge(k.dve.sem, k.dve.at(h + 1))
                link(dve.tensor_reduce(mx[:, 2 * h:2 * h + 2], Pm[:, h, :, :], axis=AX.X, op=ALU.max))
                dve.tensor_scalar(nmx[:, 2 * h:2 * h + 2], mx[:, 2 * h:2 * h + 2], -1.0, None, ALU.mult).then_inc(k.pool.sem, 1)
            link.close()

        @block.scalar
        def _(act):
            for h in range(NHEAD):
                act.wait_ge(k.pool.sem, k.pool.at(h + 1))
                for b in range(2):
                    act.activation(Pm[:, h, b, :], Pm[:, h, b, :], ACT.Exp, bias=nmx[:, 2 * h + b:2 * h + b + 1],
                                   accum_out=sums[:, 2 * h + b:2 * h + b + 1]).then_inc(k.act.sem, 1)
            act.wait_ge(k.act.sem, k.act.at(30))
            act.activation(lse, sums, ACT.Ln)
    k.dma.base += 16
    k.mm.base += NHEAD
    k.dve.base += NHEAD
    k.pool.base += NHEAD
    k.act.base += 30

    with nc.Block() as block:
        @block.vector
        def _(dve):
            link = Link(k.dvel, dve)
            part = lambda t, g: t[:, 10 * g:10 * g + 10]
            link(dve.tensor_tensor(lse, lse, mx, ALU.add))
            link(dve.tensor_tensor(top, part(lse, 0), part(lse, 1), ALU.max))
            link(dve.tensor_tensor(top, top, part(lse, 2), ALU.max))
            for g in range(3):
                link(dve.tensor_tensor(part(lse, g), part(lse, g), top, ALU.subtract))
            dve.tensor_copy(nmx, lse).then_inc(k.dve.sem, 1)
            dve.wait_ge(k.act.sem, k.act.at(1))
            link(dve.tensor_tensor(den, part(lse, 0), part(lse, 1), ALU.add))
            link(dve.tensor_tensor(den, den, part(lse, 2), ALU.add))
            for g in range(3):
                link(dve.tensor_tensor(part(sums, g), part(sums, g), den, ALU.mult))
            link(dve.reciprocal(sums, sums))
            link(dve.tensor_tensor(lse, lse, sums, ALU.mult))
            for h in range(NHEAD):
                for b in range(2):
                    i = 2 * h + b
                    dve.tensor_scalar(Pm[:, h, b, :], Pm[:, h, b, :], lse[:, i:i + 1], None, ALU.mult).then_inc(k.dve.sem, 1)
            link.close()

        @block.scalar
        def _(act):
            act.wait_ge(k.dve.sem, k.dve.at(1))
            act.activation(lse, nmx, ACT.Exp).then_inc(k.act.sem, 1)
            for h in range(NHEAD):
                act.wait_ge(k.mm.sem, k.mm.at(h + 1))
                if h >= 2:
                    act.wait_ge(k.pel.sem, k.pel.at(h - 1))
                act.activation(k.H[:, 0:2, CTX] if h % 2 == 0 else k.H[:, 2:4, CTX],
                               k.ps[:, h % 2, :].rearrange("p (b s) -> p b s", b=2), ACT.Copy).then_inc(k.act.sem, 1)

        @block.tensor
        def _(pe):
            def turn(h):
                pe.wait_ge(k.dve.sem, k.dve.at(1 + 2 * h + 2))
                if h >= 2:
                    pe.wait_ge(k.act.sem, k.act.at(1 + h - 1))
                for sb in range(2):
                    for b in range(2):
                        mm = pe.transpose(k.ps[:, h % 2, sb * S + b * P:sb * S + (b + 1) * P],
                                          Pm[:, h, b, sb * P:(sb + 1) * P], k.ident)
                mm.then_inc(k.mm.sem, 1)

            def values(h):
                pe.wait_ge(k.act.sem, k.act.at(1 + h + 1))
                pt = k.H[:, 0:2, CTX] if h % 2 == 0 else k.H[:, 2:4, CTX]
                o, r = h // 2, 64 * (h % 2)
                bank = 2 + o // 2
                for sb in range(2):
                    mm = pe.matmul(k.ps[r:r + 64, bank, (o % 2) * S:(o % 2) * S + S], lhsT=V[:, sb, h * 64:(h + 1) * 64],
                                   rhs=pt[:, sb, :], start=sb == 0, stop=sb == 1)
                mm.then_inc(k.pel.sem, 1)
            turn(0)
            for h in range(NHEAD):
                if h + 1 < NHEAD:
                    turn(h + 1)
                values(h)
    k.dve.base += 1 + 2 * NHEAD
    k.act.base += 1 + NHEAD
    k.mm.base += NHEAD
    k.pel.base += NHEAD

    with nc.Block() as block:
        @block.vector
        def _(dve):
            dve.memset(k.H[64:128, 7, LAT], 0.0)
            for o in range(8):
                r = P if o < 7 else 64
                dve.tensor_copy(k.H[0:r, o, LAT], k.ps[0:r, 2 + o // 2, (o % 2) * S:(o % 2) * S + S])


class Moe:

    def __init__(self, k):
        W = k.W
        at = [0]

        def take(n):
            at[0] += n
            return W[:, at[0] - n:at[0]]
        self.A = take(KF * P).rearrange("p (f n) -> p f n", f=KF)
        self.Ht = take(2 * D).rearrange("p (b d) -> p b d", b=2)
        self.Hg = take(D).rearrange("p (k n) -> p k n", k=KD)
        self.Y = take(D)
        self.pick = take(2 * P).rearrange("p (b n) -> p b n", b=2)
        self.gated = take(2 * P).rearrange("p (b n) -> p b n", b=2)
        self.back = take(2 * P)
        self.sil = take(2 * P).rearrange("p (b n) -> p b n", b=2)
        self.side = W[:, 8192:16384].rearrange("p (s n) -> p s n", s=4)
        self.columns = k.hat[:, 0:2, :]
        self.rank = k.sm[:, 0:16].rearrange("p (b e) -> p b e", b=2)
        self.gates = k.sm[:, 16:32].rearrange("p (b e) -> p b e", b=2)
        self.n_over = k.sm[:, 32:33].bitcast(I32)
        self.over = k.sm[:, 40:48].bitcast(I32)


MM_UP, MM_BACK, MM_DOWN, MM_OUT = 1, 46, 46, 57
MM_SLOT = 65
DVE_SLOT = 2 + KF + 8
ACT_SLOT = 2 + KF + 3
SLOT_UNIT_DONE = [MM_UP + 2 * u + 2 for u in range(KF)] + [MM_DOWN + u + 1 for u in range(KF // 2)]


def stage_router(k, moe):
    nc = k.nc
    sm = k.sm
    before_t = k.W[:, 8192:8192 + 4 * S].rearrange("p (z b t) -> p z b t", z=2, b=2)
    sel = [sm[:, 100 * b + 160:100 * b + 168] for b in range(2)]
    with nc.Block() as block:
        @block.sync
        def _(sp):
            sp.dma_start(k.W[:, 8192:8192 + 4 * S], k.a["scan_mask"]).then_inc(k.dma.sem, 16)

        @block.tensor
        def _(pe):
            for b in range(2):
                for kk in range(KD):
                    mm = pe.matmul(k.ps[:, b, 0:NE], lhsT=k.H[:, kk, S + b * P:S + (b + 1) * P],
                                   rhs=k.v("router", kk * NE, NE), start=kk == 0, stop=kk == KD - 1)
                mm.then_inc(k.mm.sem, 1)
            for b in range(2):
                for kk in range(KD):
                    mm = pe.transpose(k.ps[:, 4 + 2 * b + kk // 4, (kk % 4) * P:(kk % 4 + 1) * P],
                                      k.H[:, kk, S + b * P:S + (b + 1) * P], k.ident)
            mm.then_inc(k.mm.sem, 1)
            pe.wait_ge(k.dma.sem, k.dma.at(16))
            pe.wait_ge(k.dve.sem, k.dve.at(2))
            for b in range(2):
                for a in range(b + 1):
                    pe.matmul(k.ps[:, 2, b * NE:(b + 1) * NE], lhsT=before_t[:, 0, a, b * P:(b + 1) * P],
                              rhs=sel[a], start=a == 0, stop=a == b)
            for a in range(2):
                mm = pe.matmul(k.ps[:, 2, 2 * NE:3 * NE], lhsT=k.ones, rhs=sel[a], start=a == 0, stop=a == 1)
            mm.then_inc(k.mm.sem, 1)

        @block.gpsimd
        def _(pool):
            pool.iota(moe.columns.rearrange("p q n -> p (q n)").bitcast(I32), pattern=[[1, 2 * P]], base=0,
                      channel_multiplier=0).then_inc(k.pool.sem, 1)

        @block.scalar
        def _(act):
            act.wait_ge(k.mm.sem, k.mm.at(3))
            for b in range(2):
                for half in range(2):
                    act.activation(moe.Ht[:, b, 512 * half:512 * half + 512], k.ps[:, 4 + 2 * b + half, :], ACT.Copy)
            for b in range(2):
                act.wait_ge(k.pool.sem, k.pool.at(2 + b))
                one = sm[:, 100 * b + 140:100 * b + 141]
                act.activation(one, one, ACT.Exp).then_inc(k.act.sem, 1)

        @block.vector
        def _(dve):
            link = Link(k.dvel, dve)
            dve.wait_ge(k.pool.sem, k.pool.at(1))
            columns = moe.columns.rearrange("p q n -> p (q n)")
            link(dve.tensor_copy(columns, columns.bitcast(I32)))
            experts = columns[:, 0:8]
            for b in range(2):
                c = 100 * b + 100
                logit, best, idx, idf = (sm[:, c + 8 * i:c + 8 * i + 8] for i in range(4))
                one = lambda i: sm[:, c + 40 + i:c + 41 + i]
                first, second = sm[:, c + 48:c + 56], sm[:, c + 68:c + 76]
                dve.wait_ge(k.mm.sem, k.mm.at(b + 1))
                link(dve.tensor_copy(logit, k.ps[:, b, 0:NE]))
                link(dve.max(best, logit))
                link(dve.max_index(idx.bitcast(U32), best, logit))
                link(dve.tensor_copy(idf, idx.bitcast(U32)))
                dve.tensor_tensor(one(0), best[:, 1:2], best[:, 0:1], ALU.subtract).then_inc(k.pool.sem, 1)
                link(dve.tensor_scalar(first, experts, idf[:, 0:1], None, ALU.is_equal))
                link(dve.tensor_scalar(second, experts, idf[:, 1:2], None, ALU.is_equal))
                dve.tensor_tensor(sel[b], first, second, ALU.add).then_inc(k.dve.sem, 1)
                dve.wait_ge(k.act.sem, k.act.at(b + 1))
                link(dve.tensor_scalar(one(1), one(0), 1.0, None, ALU.add))
                link(dve.reciprocal(one(1), one(1)))
                link(dve.tensor_tensor(one(2), one(0), one(1), ALU.mult))
                link(dve.tensor_scalar(first, first, one(1), None, ALU.mult))
                link(dve.scalar_tensor_tensor(moe.gates[:, b, :], second, one(2), first, ALU.mult, ALU.add))
            dve.wait_ge(k.mm.sem, k.mm.at(4))
            dve.wait_ge(k.dve.sem, k.dve.at(2))
            for b in range(2):
                link(dve.tensor_tensor(moe.rank[:, b, :], k.ps[:, 2, b * NE:(b + 1) * NE], sel[b], ALU.mult))
                link(dve.tensor_scalar(moe.rank[:, b, :], moe.rank[:, b, :], 1.0, None, ALU.subtract))
            over, score, down = sm[:, 60:68], sm[:, 70:78], sm[:, 80:88]
            link(dve.tensor_scalar(over, k.ps[:, 2, 2 * NE:3 * NE], float(P), None, ALU.is_gt))
            link(dve.tensor_scalar(down, experts, -1.0, float(NE), ALU.mult, ALU.add))
            link(dve.tensor_tensor(down, down, over, ALU.mult))
            link(dve.max(score, down))
            link(dve.tensor_reduce(sm[:, 90:91], over, axis=AX.X, op=ALU.add))
            link(dve.tensor_copy(moe.n_over, sm[:, 90:91]))
            link(dve.tensor_scalar(score, score, -1.0, float(NE), ALU.mult, ALU.add))
            link(dve.tensor_scalar(score, score, float(NE - 1), None, ALU.min))
            link(dve.tensor_copy(moe.over, score))
            link.close()
    k.dma.base += 16
    k.mm.base += 4
    k.pool.base += 3
    k.act.base += 2
    k.dve.base += 2


class Slot:

    def __init__(self, k, moe, turn, mm, act, dve, weights, landed):
        self.k, self.moe, self.turn = k, moe, turn
        self.mm, self.act, self.dve = mm, act, dve
        self.weights, self.landed = weights, landed

    def value(self, s, n):
        per = {id(self.mm): MM_SLOT, id(self.act): ACT_SLOT, id(self.dve): DVE_SLOT}[id(s)]
        return self.turn * per + (s.base + n)

    def tensor(self, pe):
        k, moe = self.k, self.moe
        pe.wait_ge(self.dve.sem, self.value(self.dve, 1))
        for kk in range(KD):
            for b in range(2):
                mm = pe.matmul(k.ps[:, 4 + kk // 4, (kk % 4) * P:(kk % 4 + 1) * P], lhsT=moe.Ht[:, b, kk * P:(kk + 1) * P],
                               rhs=moe.pick[:, b, :], start=b == 0, stop=b == 1)
        mm.then_inc(self.mm.sem, 1)
        pe.wait_ge(self.act.sem, self.value(self.act, 2))
        for o in range(2 * KF):
            u = o // 2
            if o % 2 == 0:
                self.landed(pe, u)
            if o >= 4 and o % 2 == 0:
                pe.wait_ge(self.act.sem, self.value(self.act, 2 + u - 1))
            elif o >= 4:
                pe.wait_ge(self.dve.sem, self.value(self.dve, 2 + u - 1))
            for kk in range(KD):
                i = (o % 2) * KD + kk
                mm = pe.matmul(k.ps[:, o % 4, 0:P], lhsT=self.weights(u)[:, i * P:(i + 1) * P], rhs=moe.Hg[:, kk, :],
                               start=kk == 0, stop=kk == KD - 1)
            mm.then_inc(self.mm.sem, 1)
        pe.wait_ge(self.dve.sem, self.value(self.dve, 2 + KF))
        for b in range(2):
            mm = pe.transpose(k.ps[:, 0, b * P:(b + 1) * P], moe.gated[:, b, :], k.ident)
        mm.then_inc(self.mm.sem, 1)
        for u in range(KF // 2):
            self.landed(pe, KF + u)
            for f in (2 * u, 2 * u + 1):
                for half in range(2):
                    c = (f % 2) * D + half * 512
                    mm = pe.matmul(k.ps[:, 6 + half, :], lhsT=moe.A[:, f, :], rhs=self.weights(KF + u)[:, c:c + 512],
                                   start=f == 0, stop=f == KF - 1)
            mm.then_inc(self.mm.sem, 1)
        pe.wait_ge(self.act.sem, self.value(self.act, ACT_SLOT))
        for o in range(KD):
            if o >= 4:
                pe.wait_ge(self.dve.sem, self.value(self.dve, 2 + KF + o - 3))
            pe.matmul(k.ps[:, o % 4, 0:S], lhsT=moe.Y[:, o * P:(o + 1) * P], rhs=moe.back, start=True, stop=True)\
              .then_inc(self.mm.sem, 1)

    def scalar(self, act):
        k, moe = self.k, self.moe
        act.wait_ge(self.mm.sem, self.value(self.mm, 1))
        for half in range(2):
            act.activation(moe.Hg[:, 4 * half:4 * half + 4, :].rearrange("p k n -> p (k n)"), k.ps[:, 4 + half, :],
                           ACT.Copy).then_inc(self.act.sem, 1)
        for f in range(KF):
            act.wait_ge(self.mm.sem, self.value(self.mm, MM_UP + 2 * f + 1))
            if f >= 2:
                act.wait_ge(self.dve.sem, self.value(self.dve, 2 + f - 1))
            act.activation(moe.sil[:, f % 2, :], k.ps[:, (2 * f) % 4, 0:P], ACT.Silu).then_inc(self.act.sem, 1)
        act.wait_ge(self.mm.sem, self.value(self.mm, MM_BACK))
        act.activation(moe.back, k.ps[:, 0, 0:2 * P], ACT.Copy).then_inc(self.act.sem, 1)
        act.wait_ge(self.mm.sem, self.value(self.mm, MM_OUT))
        for half in range(2):
            act.activation(moe.Y[:, 512 * half:512 * half + 512], k.ps[:, 6 + half, :], ACT.Copy).then_inc(self.act.sem, 1)

    def vector(self, dve, expert, slot, gate):
        k, moe = self.k, self.moe
        for b in range(2):
            rank = moe.rank[:, b, bass.ds(expert, 1)]
            ins = dve.tensor_scalar(moe.pick[:, b, :], moe.columns[:, slot, :], rank, None, ALU.is_equal)
            if b == 0:
                ins.then_inc(k.pickl, 1)
        ins.then_inc(self.dve.sem, 1)
        dve.wait_ge(k.pickl, self.turn + (k.pick_base + 1))
        dve.wait_ge(self.dve.sem, self.value(self.dve, 1))
        for b in range(2):
            ins = dve.tensor_scalar(moe.gated[:, b, :], moe.pick[:, b, :], moe.gates[:, b, bass.ds(expert, 1)], None, ALU.mult)
        ins.then_inc(self.dve.sem, 1)
        for f in range(KF):
            dve.wait_ge(self.mm.sem, self.value(self.mm, MM_UP + 2 * f + 2))
            dve.wait_ge(self.act.sem, self.value(self.act, 2 + f + 1))
            dve.tensor_tensor(moe.A[:, f, :], k.ps[:, (2 * f + 1) % 4, 0:P], moe.sil[:, f % 2, :],
                              ALU.mult).then_inc(self.dve.sem, 1)
        for o in range(KD):
            dve.wait_ge(self.mm.sem, self.value(self.mm, MM_OUT + o + 1))
            x = k.X[:, o, LAT]
            dve.scalar_tensor_tensor(x, k.ps[:, o % 4, 0:S], gate(o), x, ALU.mult, ALU.add).then_inc(self.dve.sem, 1)


def stage_experts(k, moe, gate):
    nc = k.nc
    rounds = EXPERT_UNITS // RING
    unit0 = k.unit

    def landed(eng, u, e):
        eng.wait_ge(k.w_in[k.slot(u)], e * (16 * rounds) + k.landed(u))
    slot = lambda e: Slot(k, moe, e, k.mm, k.act, k.dve, lambda u: k.ring[:, k.slot(u), :],
                          lambda eng, u: landed(eng, u, e))
    with nc.Block() as block:
        @block.sync
        def _(sp):
            with sp.Fori(0, NE) as e:
                refill(k, sp, SLOT_UNIT_DONE, EXPERT_UNITS, turn=e, per=MM_SLOT)

        @block.tensor
        def _(pe):
            with pe.Fori(0, NE) as e:
                slot(e).tensor(pe)

        @block.scalar
        def _(act):
            with act.Fori(0, NE) as e:
                slot(e).scalar(act)

        @block.vector
        def _(dve):
            with dve.Fori(0, NE) as e:
                slot(e).vector(dve, e, 0, gate)
    k.pick_base += NE
    k.mm.base += MM_SLOT * NE
    k.act.base += ACT_SLOT * NE
    k.dve.base += DVE_SLOT * NE
    k.unit += EXPERT_UNITS * NE
    return unit0


def stage_second_slots(k, moe, gate, unit0):
    nc = k.nc
    mm, act_s, dve_s = k.mm2, k.act2, k.dve2
    uses = [len(range(s, EXPERT_UNITS, 4)) for s in range(4)]

    def landed(eng, u, t):
        eng.wait_ge(k.side_in[u % 4], t * (16 * uses[u % 4]) + 16 * (u // 4 + 1))
    slot = lambda t: Slot(k, moe, t, mm, act_s, dve_s, lambda u: moe.side[:, u % 4, :], lambda eng, u: landed(eng, u, t))

    def turns(eng, body, last=lambda: None):
        n = eng.value_load(moe.n_over[0:1, 0:1], min_val=0, max_val=3)
        with eng.If(n > 0):
            with eng.Fori(0, n) as t:
                body(t)
                eng.wait_ge(dve_s.sem, slot(t).value(dve_s, DVE_SLOT))
                last()

    def expert(eng, t):
        return eng.value_load(moe.over[0:1, bass.ds(t, 1)], min_val=0, max_val=NE - 1)

    with nc.Block() as block:
        @block.sync
        def _(sp):
            def body(t):
                e = expert(sp, t)
                for u in range(EXPERT_UNITS):
                    if u >= 4:
                        sp.wait_ge(mm.sem, slot(t).value(mm, SLOT_UNIT_DONE[u - 4]))
                    sp.dma_start(moe.side[:, u % 4, :], k.a["weights"][bass.ds(e * EXPERT_UNITS + (unit0 + u), 1)].squeeze(0))\
                      .then_inc(k.side_in[u % 4], 16)
            turns(sp, body, last=lambda: sp.sem_inc(k.turns_over, 1))

        @block.tensor
        def _(pe):
            turns(pe, lambda t: slot(t).tensor(pe))

        @block.scalar
        def _(act):
            turns(act, lambda t: slot(t).scalar(act))

        @block.vector
        def _(dve):
            turns(dve, lambda t: slot(t).vector(dve, expert(dve, t), 1, gate))


def stage_norm2(k, layer, which, cols):
    m, v = k.mod2, 3 * which
    stage_norm(k, cols, lambda t, h: m[:, layer, (v + 1) * 8 + t, h:h + 1], lambda t, h: m[:, layer, v * 8 + t, h:h + 1])


def stage_post_norm(k, layer, which, cols, Y):
    nc = k.nc
    n = cols.stop - cols.start
    gate = k.sm[:, 0:16].rearrange("p (t h) -> p t h", h=2)
    v = 3 * which + 2
    halves = [c for c in (CTX, LAT) if c.start >= cols.start and c.stop <= cols.stop]
    rstd = k.W[:, 8 * T:8 * T + n]
    with nc.Block() as block:
        rms_scale(k, block, lambda i: Y[:, i, 0:n], n, k.W, rstd, 7)
    rms_counts(k)
    with nc.Block() as block:
        @block.vector
        def _(dve):
            link = Link(k.dvel, dve)
            link(dve.tensor_tensor(gate, k.mod2[:, layer, v * 8:v * 8 + 8, :],
                                   k.v("norm_g2", layer * 32 + (2 * which + 1) * 8, 8).unsqueeze(2).to_broadcast([P, 8, 2]), ALU.mult))
            for i in range(KD):
                for c in halves:
                    half = 0 if c is CTX else 1
                    own = slice(c.start - cols.start, c.stop - cols.start)
                    link.mark(dve.scalar_tensor_tensor(Y[:, i, own], Y[:, i, own], gate[:, i, half:half + 1],
                                                       rstd[:, own], ALU.mult, ALU.mult))
            link.wait()
            for i in range(KD):
                link.mark(dve.tensor_tensor(k.X[:, i, cols], k.X[:, i, cols], Y[:, i, 0:n], ALU.add))
            link.close()


def stage_square(k, cols, Y):
    nc = k.nc
    n = cols.stop - cols.start
    unit_done, out_done, signals, total = plan([i // KD for i in range(8 * KD)])
    with nc.Block() as block:
        @block.sync
        def _(sp):
            refill(k, sp, unit_done, U_SQ)

        @block.tensor
        def _(pe):
            def before(o):
                if o >= 4:
                    pe.wait_ge(k.act.sem, k.act.at(o - 3))
            gemm(k, pe, 8, KD, lambda kk: k.H[:, kk, cols], lambda o: k.ps[:, o % 4, 0:n], before, signals)

        @block.scalar
        def _(act):
            for o in range(8):
                act.wait_ge(k.mm.sem, k.mm.at(out_done[o]))
                act.activation(Y[:, o, 0:n], k.ps[:, o % 4, 0:n], ACT.Copy).then_inc(k.act.sem, 1)
    k.mm.base += total
    k.act.base += 8
    k.unit += U_SQ


def stage_conv_ffn(k, layer, cols, Y):
    nc = k.nc
    n = cols.stop - cols.start
    both = n == T
    A = k.W[:, 0:KF * n].rearrange("p (o t) -> p o t", o=KF)
    conv = k.W[:, 15360:15360 + 2 * T].rearrange("p (b t) -> p b t", b=2)
    owner = [t // KD for t in range(2 * KF * KD)] + [2 * KF + t // KF for t in range(KD * KF)]
    unit_done, out_done, signals, total = plan(owner)
    down0 = 2 * KF
    lat0 = n - S
    rows = S // GRID_W

    def up(dve, f):
        dve.wait_ge(k.mm.sem, k.mm.at(out_done[2 * f + 1]))
        dve.wait_ge(k.act.sem, k.act.at(f + 1))
        dve.tensor_tensor(A[:, f, :], k.ps[:, (2 * f + 1) % 4, 0:n], conv[:, f % 2, 0:n],
                          ALU.mult).then_inc(k.dve.sem, 1)

    with nc.Block() as block:
        @block.sync
        def _(sp):
            refill(k, sp, unit_done, EXPERT_UNITS)

        @block.tensor
        def _(pe):
            def before(o):
                if o >= 4:
                    f = o // 2 - 2
                    pe.wait_ge(k.dve.sem, k.dve.at(conv_done(f) if o % 2 == 0 else up_done(f)))
            gemm(k, pe, down0, KD, lambda kk: k.H[:, kk, cols], lambda o: k.ps[:, o % 4, 0:n], before, signals)

            def before_down(o):
                pe.wait_ge(k.dve.sem, k.dve.at(down0))
                if o >= 4:
                    pe.wait_ge(k.act.sem, k.act.at(KF + o - 3))
            gemm(k, pe, 8, KF, lambda kk: A[:, kk, :], lambda o: k.ps[:, o % 4, 0:n], before_down,
                 signals, first=down0 * KD)

        @block.vector
        def _(dve):
            link = Link(k.dvel, dve)
            for f in range(KF):
                y, x = conv[:, f % 2, 0:n], k.ps[:, (2 * f) % 4, 0:n]
                w = lambda a, b: k.v("fcw", layer * 9 * KF + (3 * a + b) * KF + f)
                dve.wait_ge(k.mm.sem, k.mm.at(out_done[2 * f]))
                if f >= 2:
                    dve.wait_ge(k.dve.sem, k.dve.at(up_done(f - 2)))
                link(dve.tensor_scalar(y, x, w(1, 1), k.v("fcb", layer * KF + f), ALU.mult, ALU.add))
                taps = []
                if both:
                    taps += [(y[:, 1:S], x[:, 0:S - 1], w(1, 0)), (y[:, 0:S - 1], x[:, 1:S], w(1, 2))]
                yg = y[:, lat0:n].rearrange("p (r c) -> p r c", r=rows)
                xg = x[:, lat0:n].rearrange("p (r c) -> p r c", r=rows)
                for dr in (-1, 0, 1):
                    for dc in (-1, 0, 1):
                        if dr == 0 and dc == 0:
                            continue
                        r0, r1 = max(0, -dr), rows - max(0, dr)
                        c0, c1 = max(0, -dc), GRID_W - max(0, dc)
                        taps.append((yg[:, r0:r1, c0:c1], xg[:, r0 + dr:r1 + dr, c0 + dc:c1 + dc], w(dr + 1, dc + 1)))
                for j, (yo, xo, ww) in enumerate(taps):
                    ins = dve.scalar_tensor_tensor(yo, xo, ww, yo, ALU.mult, ALU.add)
                    if j < len(taps) - 1:
                        link(ins)
                    else:
                        ins.then_inc(k.dve.sem, 1)
                if f > 0:
                    up(dve, f - 1)
            up(dve, KF - 1)
            link.close()

        @block.scalar
        def _(act):
            for f in range(KF):
                act.wait_ge(k.dve.sem, k.dve.at(conv_done(f)))
                act.activation(conv[:, f % 2, 0:n], conv[:, f % 2, 0:n], ACT.Gelu_apprx_tanh).then_inc(k.act.sem, 1)
            for o in range(8):
                act.wait_ge(k.mm.sem, k.mm.at(out_done[down0 + o]))
                act.activation(Y[:, o, 0:n], k.ps[:, o % 4, 0:n], ACT.Copy).then_inc(k.act.sem, 1)
    k.mm.base += total
    k.act.base += KF + 8
    k.dve.base += 2 * KF
    k.unit += EXPERT_UNITS


def conv_done(f):
    return 1 if f == 0 else 2 * f


def up_done(f):
    return 2 * f + 3 if f < KF - 1 else 2 * KF


class Even:

    def __init__(self, k):
        W = k.W
        t = lambda at, n: W[:, at:at + n * T].rearrange("p (o t) -> p o t", o=n)
        self.qk = t(0, 8)
        self.gqk = t(4096, 4)
        self.gate = t(6144, 8)
        self.V = W[:, 10240:14336].rearrange("p (b d) -> p b d", b=NB)
        self.glr = W[:, 14336:14848]
        self.I = W[:, 14848:15360]
        self.Fg = W[:, 15360:15872]
        self.B = W[:, 15872:16384]
        self.c = k.sm[:, 256:512].rearrange("p (b r) -> p b r", b=NB)


def stage_even_project(k, ev):
    nc = k.nc
    n_out = 23
    owner = [i // KD for i in range(n_out * KD)]
    unit_done, out_done, signals, total = plan(owner)
    m_units = 4
    unit_all = dict(unit_done)
    for u in range(m_units):
        unit_all[U_EV + u] = total + u + 1
    with nc.Block() as block:
        @block.sync
        def _(sp):
            refill(k, sp, unit_all, U_EV + m_units)

        @block.tensor
        def _(pe):
            def before(o):
                if 4 <= o < 12:
                    pe.wait_ge(k.dve.sem, k.dve.at(o - 3))
                elif o >= 12:
                    pe.wait_ge(k.act.sem, k.act.at(o - 3))
            gemm(k, pe, n_out, KD, lambda kk: k.H[:, kk, :], lambda o: k.ps[:, o % 4, :], before, signals)
            for u in range(m_units):
                pe.wait_ge(k.w_in[k.slot(U_EV + u)], k.landed(U_EV + u))
                if u >= 2:
                    pe.wait_ge(k.act.sem, k.act.at(n_out + 2 * (u - 1)))
                for b in range(NB):
                    for kk in range(KD):
                        mm = pe.matmul(k.ps[:, 4 + 2 * (u % 2) + b // 2, (b % 2) * 256:(b % 2) * 256 + 256],
                                       lhsT=k.H[:, kk, b * P:(b + 1) * P],
                                       rhs=k.ring[:, k.slot(U_EV + u), kk * 256:(kk + 1) * 256],
                                       start=kk == 0, stop=kk == KD - 1)
                mm.then_inc(k.mm.sem, 1)

        @block.vector
        def _(dve):
            link = Link(k.dvel, dve)
            for o in range(8):
                y, x = ev.qk[:, o, :], k.ps[:, o % 4, :]
                w = lambda j: k.v("ecw", 8 * j + o)
                dve.wait_ge(k.mm.sem, k.mm.at(out_done[o]))
                link(dve.tensor_scalar(y, x, w(1), k.v("ecb", o), ALU.mult, ALU.add))
                for c in (CTX, LAT):
                    a, b = c.start, c.stop
                    link(dve.scalar_tensor_tensor(y[:, a + 1:b], x[:, a:b - 1], w(0), y[:, a + 1:b], ALU.mult, ALU.add))
                    ins = dve.scalar_tensor_tensor(y[:, a:b - 1], x[:, a + 1:b], w(2), y[:, a:b - 1], ALU.mult, ALU.add)
                    if c is CTX:
                        link(ins)
                    else:
                        ins.then_inc(k.dve.sem, 1)
            link.close()

        @block.scalar
        def _(act):
            for o in range(8):
                act.wait_ge(k.dve.sem, k.dve.at(o + 1))
                act.activation(ev.qk[:, o, :], ev.qk[:, o, :], ACT.Silu).then_inc(k.act.sem, 1)
            for o in range(8, n_out):
                act.wait_ge(k.mm.sem, k.mm.at(out_done[o]))
                x = k.ps[:, o % 4, :]
                if o < 10:
                    ins = act.activation(ev.gqk[:, o - 8, :], x, ACT.Copy, scale=64 ** -0.5)
                elif o < 12:
                    ins = act.activation(ev.gqk[:, o - 8, :], x, ACT.Copy)
                elif o == 12:
                    ins = act.activation(ev.glr, x, ACT.Copy)
                elif o < 15:
                    ins = act.activation(ev.I if o == 13 else ev.Fg, x, ACT.Identity, bias=k.v("ebg", o - 13))
                else:
                    ins = act.activation(ev.gate[:, o - 15, :], x, ACT.Sigmoid if o < 19 else ACT.Silu)
                ins.then_inc(k.act.sem, 1)
            for u in range(m_units):
                act.wait_ge(k.mm.sem, k.mm.at(total + u + 1))
                for h in range(2):
                    act.activation(ev.V[:, 2 * h:2 * h + 2, u * 256:(u + 1) * 256],
                                   k.ps[:, 4 + 2 * (u % 2) + h, :].rearrange("p (b d) -> p b d", b=2),
                                   ACT.Copy).then_inc(k.act.sem, 1)
    k.mm.base += total + m_units
    k.act.base += n_out + 2 * m_units
    k.dve.base += 8
    k.unit += U_EV + m_units


def stage_mlstm_gates(k, ev):
    nc = k.nc
    F_, B, I = ev.Fg, ev.B, ev.I
    runs = [(slice(0, 32), slice(0, T), 1, None), (slice(32, 64), CTX, -1, None), (slice(32, 64), LAT, -1, 0)]
    e = k.H[:, 0, :]
    one = k.ones[:, 0:1]
    with nc.Block() as block:
        @block.scalar
        def _(act):
            act.wait_ge(k.dve.sem, k.dve.at(1))
            act.activation(e, e, ACT.Exp, scale=-1.0).then_inc(k.act.sem, 1)
            act.wait_ge(k.dve.sem, k.dve.at(2))
            act.activation(e, e, ACT.Ln).then_inc(k.act.sem, 1)
            act.wait_ge(k.dve.sem, k.dve.at(3))
            act.activation(B, B, ACT.Exp, scale=-1.0)
            act.wait_ge(k.mm.sem, k.mm.at(1))
            act.activation(ev.c, k.ps[:, 0, :].rearrange("p (b r) -> p b r", b=NB)[:, :, 0:64], ACT.Copy)

        @block.tensor
        def _(pe):
            pe.wait_ge(k.dve.sem, k.dve.at(4))
            for b in range(NB):
                mm = pe.transpose(k.ps[:, 0, b * P:(b + 1) * P], I[:, b * P:(b + 1) * P], k.ident)
            mm.then_inc(k.mm.sem, 1)

        @block.vector
        def _(dve):
            link = Link(k.dvel, dve)
            dve.scalar_tensor_tensor(e, F_, -1.0, F_, ALU.mult, ALU.max).then_inc(k.dve.sem, 1)
            dve.wait_ge(k.act.sem, k.act.at(1))
            dve.tensor_scalar(e, e, 1.0, None, ALU.add).then_inc(k.dve.sem, 1)
            dve.wait_ge(k.act.sem, k.act.at(2))
            link(dve.scalar_tensor_tensor(F_, F_, 0.0, e, ALU.min, ALU.subtract))
            link(dve.memset(B[64:128, :], 0.0))
            for rows, c, step, after in runs:
                view = lambda x: x[rows, c] if step > 0 else x[rows, c][:, ::-1]
                init = 0.0 if after is None else B[rows, after:after + 1]
                n = c.stop - c.start
                link(dve.tensor_tensor_scan(view(B), one[rows, :].to_broadcast([32, n]), view(F_), init, ALU.mult, ALU.add))
            link(dve.tensor_tensor(I, I, B, ALU.subtract))
            link(dve.memset(F_[64:128, :], 0.0))
            for rows, c, step, after in runs:
                view = lambda x: x[rows, c] if step > 0 else x[rows, c][:, ::-1]
                init = 0.0 if after is None else F_[rows, after:after + 1]
                link(dve.tensor_tensor_scan(view(F_), view(I), view(I), init, ALU.max, ALU.max))
            dve.tensor_tensor(B, B, F_, ALU.add).then_inc(k.dve.sem, 1)
            dve.tensor_scalar(F_, F_, -1.0, None, ALU.mult).then_inc(k.dve.sem, 1)
            link.close()
    k.act.base += 2
    k.mm.base += 1
    k.dve.base += 4


LOGS, WEIGHED = (1, 2, 5, 6), (3, 4, 7, 8)


def stage_mlstm(k, ev):
    nc = k.nc
    mk = k.H[:, 6:8, :].rearrange("p a t -> p (a t)").rearrange("p (z b t) -> p z b t", z=2, b=2)
    ST = k.H[:, 0:4, :]
    A = [k.H[:, 4, :], k.H[:, 5, :]]
    d = ev.I
    with nc.Block() as block:
        @block.sync
        def _(sp):
            sp.dma_start(k.H[:, 6:8, :].rearrange("p a t -> p (a t)"), k.a["scan_mask"]).then_inc(k.dma.sem, 16)
            sp.wait_ge(k.dma.sem, k.dma.at(16))
    k.dma.base += 16
    cols = [slice(0, T), slice(0, T), LAT, LAT]
    with nc.Block() as block:
        @block.tensor
        def _(pe):
            for h in range(4):
                if h:
                    pe.wait_ge(k.act.sem, k.act.at(12 * h))
                    pe.wait_ge(k.dve.sem, k.dve.at(18 * h - 1))
                for b in range(NB):
                    mm = pe.matmul(k.ps[:, b % 2, cols[b]], lhsT=ev.qk[:, 4 + h, b * P:(b + 1) * P],
                                   rhs=ev.qk[:, h, cols[b]], start=True, stop=True)
                    mm.then_inc(k.mm.sem, 1)
                    if b < 2:
                        pe.wait_ge(k.act.sem, k.act.at(12 * h + b + 1))
                for z in range(2):
                    r = 32 * z + h
                    before = 18 * h + 9 * z
                    pick = k.ident[:, r:r + 1].to_broadcast([P, P])
                    if before:
                        pe.wait_ge(k.dve.sem, k.dve.at(before - 9 + LOGS[3]))
                    pe.matmul(k.ps[:, 4, :], lhsT=pick, rhs=ev.Fg, start=True, stop=True).then_inc(k.mm.sem, 1)
                    if before:
                        pe.wait_ge(k.dve.sem, k.dve.at(before))
                    pe.matmul(k.ps[:, 7, :], lhsT=pick, rhs=ev.B, start=True, stop=True)
                    for b in range(NB):
                        pe.wait_ge(k.pool.sem, k.pool.at(8 * h + 4 * z + b + 1))
                        a = A[b % 2][:, cols[b]]
                        pe.matmul(k.ps[:, 5, cols[b]], lhsT=ev.V[:, b, h * P:(h + 1) * P], rhs=a, start=b == 0, stop=b == 3)
                        pe.matmul(k.ps[:, 6, cols[b]], lhsT=k.ones, rhs=a, start=b == 0, stop=b == 3).then_inc(k.mm.sem, 1)

        @block.scalar
        def _(act):
            for h in range(4):
                for b in range(NB):
                    act.wait_ge(k.mm.sem, k.mm.at(14 * h + b + 1))
                    act.activation(ST[:, b, cols[b]], k.ps[:, b % 2, cols[b]], ACT.Copy, scale=P ** -0.5).then_inc(k.act.sem, 1)
                for z in range(2):
                    for b in range(NB):
                        act.wait_ge(k.dve.sem, k.dve.at(18 * h + 9 * z + LOGS[b]))
                        a = A[b % 2][:, cols[b]]
                        act.activation(a, a, ACT.Exp).then_inc(k.act.sem, 1)

        @block.vector
        def _(dve):
            link = Link(k.dvel, dve)
            for h in range(4):
                for z in range(2):
                    dve.wait_ge(k.mm.sem, k.mm.at(14 * h + 4 + 5 * z + 1))
                    for pair in ((0, 1), (2, 3)):
                        for b in pair:
                            a = A[b % 2][:, cols[b]]
                            if b >= 2:
                                dve.wait_ge(k.mm.sem, k.mm.at(14 * h + 4 + 5 * z + b))
                            dve.tensor_scalar(a, k.ps[:, 4, cols[b]], ev.c[:, b, 32 * z + h:32 * z + h + 1], 0.0,
                                              ALU.add, ALU.min).then_inc(k.dve.sem, 1)
                        for b in pair:
                            a = A[b % 2][:, cols[b]]
                            dve.wait_ge(k.act.sem, k.act.at(12 * h + 4 + 4 * z + b + 1))
                            dve.tensor_tensor(a, a, ST[:, b, cols[b]], ALU.mult).then_inc(k.dve.sem, 1)
                    dve.wait_ge(k.mm.sem, k.mm.at(14 * h + 4 + 5 * z + 5))
                    link(dve.tensor_copy(d, k.ps[:, 7, :]))
                    link(dve.scalar_tensor_tensor(d, k.ps[:, 6, :], -1.0, d, ALU.mult, ALU.max))
                    link(dve.tensor_tensor(d, k.ps[:, 6, :], d, ALU.max))
                    link(dve.reciprocal(d, d))
                    if z == 0:
                        dve.tensor_tensor(ev.qk[:, h, :], k.ps[:, 5, :], d, ALU.mult).then_inc(k.dve.sem, 1)
                    else:
                        link(dve.tensor_tensor(d, k.ps[:, 5, :], d, ALU.mult))
                        dve.wait_ge(k.dve.sem, k.dve.at(18 * h + 9))
                        dve.tensor_tensor(ev.qk[:, h, :], ev.qk[:, h, :], d, ALU.add).then_inc(k.dve.sem, 1)
            link.close()

        @block.gpsimd
        def _(pool):
            for h in range(4):
                for z in range(2):
                    for b in range(NB):
                        c = CTX if b < 2 else LAT
                        a = A[b % 2][:, c]
                        pool.wait_ge(k.dve.sem, k.dve.at(18 * h + 9 * z + WEIGHED[b]))
                        pool.tensor_tensor(a, a, mk[:, z, b % 2, :], ALU.mult).then_inc(k.pool.sem, 1)
    k.mm.base += 14 * 4
    k.act.base += 12 * 4
    k.dve.base += 18 * 4
    k.pool.base += 8 * 4


def stage_gla(k, ev):
    nc = k.nc
    w2 = k.H[:, 7, :]
    one = k.ones[:, 0:1]
    C = k.H[:, 0:2, :]
    E = k.H[:, 2, :]
    Kt = [k.H[:, 3, :], k.H[:, 4, :]]
    Q0 = [k.H[:, 5, :], k.H[:, 6, :]]
    Q1 = [ev.I, ev.Fg]
    tmp = ev.B
    accs = [k.H[:, 7, :], ev.glr]
    la = [k.H[:, 3, :], k.H[:, 4, :]]
    for j in range(2):
        with nc.Block() as block:
            @block.sync
            def _(sp):
                sp.dma_start(w2, k.a["gla_w2"]).then_inc(k.dma.sem, 16)

            @block.tensor
            def _(pe):
                pe.wait_ge(k.dma.sem, k.dma.at(16))
                src = ev.glr if j == 0 else ev.qk[:, 7, :]
                for z in range(2):
                    mm = pe.matmul(k.ps[:, z, :], lhsT=w2[:, z * 256 + j * P:z * 256 + (j + 1) * P], rhs=src, start=True, stop=True)
                mm.then_inc(k.mm.sem, 1)

            @block.scalar
            def _(act):
                act.wait_ge(k.mm.sem, k.mm.at(1))
                if j == 0:
                    act.activation(ev.qk[:, 7, :], ev.glr, ACT.Copy)
                for z in range(2):
                    act.activation(C[:, z, :], k.ps[:, z, :], ACT.Identity, bias=k.v("glab", 2 * z + j)).then_inc(k.act.sem, 1)
                for z in range(2):
                    act.wait_ge(k.dve.sem, k.dve.at(1 + z))
                    act.activation(la[z], la[z], ACT.Exp, scale=-1.0).then_inc(k.act.sem, 1)
                for z in range(2):
                    act.wait_ge(k.dve.sem, k.dve.at(3 + z))
                    act.activation(la[z], la[z], ACT.Ln).then_inc(k.act.sem, 1)

            @block.vector
            def _(dve):
                link = Link(k.dvel, dve)
                for z in range(2):
                    dve.wait_ge(k.act.sem, k.act.at(1 + z))
                    dve.scalar_tensor_tensor(la[z], C[:, z, :], -1.0, C[:, z, :], ALU.mult, ALU.max).then_inc(k.dve.sem, 1)
                for z in range(2):
                    dve.wait_ge(k.act.sem, k.act.at(3 + z))
                    dve.tensor_scalar(la[z], la[z], 1.0, None, ALU.add).then_inc(k.dve.sem, 1)
                for z in range(2):
                    dve.wait_ge(k.act.sem, k.act.at(5 + z))
                    link(dve.scalar_tensor_tensor(la[z], C[:, z, :], 0.0, la[z], ALU.min, ALU.subtract))
                    link(dve.tensor_scalar(la[z], la[z], 1.0 / 16, None, ALU.mult))
                    link(dve.tensor_tensor_scan(C[:, z, :], one.to_broadcast([P, T]), la[z], 0.0, ALU.mult, ALU.add))
                link(dve.tensor_copy(tmp[:, 0:1], C[:, 1, T - 1:T]))
                link(dve.tensor_tensor(C[:, 1, :], C[:, 1, :], la[1], ALU.subtract))
                link.close()
        k.dma.base += 16
        k.mm.base += 1
        k.act.base += 6
        k.dve.base += 4

        steps = [(z, l) for z in range(2) for l in range(9)]
        total_sum = k.sm[:, 0:1]
        products = [ev.qk[:, 6, :], ev.qk[:, 5 if j == 0 else 7, :]]

        def masked(dve, i):
            z, l = steps[i]
            if l >= 7:
                return
            dve.wait_ge(k.mm.sem, k.mm.at(i + 2))
            m = k.level[z][:, l * P:(l + 1) * P].unsqueeze(1).to_broadcast([P, NB, P])
            for h in range(2):
                n = 2 * (l + 7 * z) + h
                if n >= 2:
                    dve.wait_ge(k.pooll.sem, k.pooll.at(n - 1))
                dve.tensor_tensor(products[h].rearrange("p (b t) -> p b t", b=NB),
                                  k.ps[:, 2 * ((i + 1) % 2) + h, :].rearrange("p (b t) -> p b t", b=NB),
                                  m, ALU.mult).then_inc(k.pool.sem, 1)

        with nc.Block() as block:
            @block.tensor
            def _(pe):
                pe.wait_ge(k.dve.sem, k.dve.at(2))
                for h, q in enumerate((Q0[1], Q1[1])):
                    for b in range(NB):
                        mm = pe.matmul(k.ps[:, h, b * P:(b + 1) * P], lhsT=ev.gqk[:, 2 + j, b * P:(b + 1) * P],
                                       rhs=q[:, b * P:(b + 1) * P], start=True, stop=True)
                mm.then_inc(k.mm.sem, 1)
                for i, (z, l) in enumerate(steps):
                    pe.wait_ge(k.dve.sem, k.dve.at(2 + 4 * i + 4))
                    kt, qs = Kt[i % 2], (Q0[i % 2], Q1[i % 2])
                    if l < 7:
                        pe.wait_ge(k.pool.sem, k.pool.at(masked_before(steps, i)))
                    for h in range(2):
                        if l < 7:
                            bank = 2 * ((i + 1) % 2) + h
                            for b in range(NB):
                                c = slice(b * P, (b + 1) * P)
                                mm = pe.matmul(k.ps[:, bank, c], lhsT=kt[:, c], rhs=qs[h][:, c], start=True, stop=True)
                        elif l == 7:
                            for b in (0, 2):
                                s, t = (b, b + 1) if z == 0 else (b + 1, b)
                                mm = pe.matmul(k.ps[:, 4 + h, s * P:(s + 1) * P], lhsT=kt[:, s * P:(s + 1) * P],
                                               rhs=qs[h][:, t * P:(t + 1) * P], start=True, stop=True)
                        else:
                            for s in range(2):
                                mm = pe.matmul(k.ps[:, 6 + h, s * 256:(s + 1) * 256], lhsT=kt[:, s * P:(s + 1) * P],
                                               rhs=qs[h][:, LAT], start=z == 0 and s == 0, stop=True, skip_group_check=True)
                    mm.then_inc(k.mm.sem, 1)

            @block.scalar
            def _(act):
                for i in range(len(steps)):
                    act.wait_ge(k.dve.sem, k.dve.at(2 + 4 * i + 1))
                    if i >= 1:
                        act.wait_ge(k.dve.sem, k.dve.at(2 + 4 * (i - 1) + 4))
                    act.activation(E, tmp, ACT.Exp, scale=-1.0).then_inc(k.act.sem, 1)

            @block.gpsimd
            def _(pool):
                for n in range(28):
                    pool.wait_ge(k.pool.sem, k.pool.at(3 + n))
                    if n >= 2:
                        pool.wait_ge(k.pooll.sem, k.pooll.at(n - 1))
                    pool.tensor_tensor(accs[n % 2], accs[n % 2], products[n % 2], ALU.add).then_inc(k.pooll.sem, 1)

            @block.vector
            def _(dve):
                link = Link(k.dvel, dve)
                link(dve.tensor_copy(total_sum, tmp[:, 0:1]))
                q, kx = ev.gqk[:, j, :], ev.gqk[:, 2 + j, :]
                for h, qb in enumerate((Q0[1], Q1[1])):
                    dve.tensor_scalar(qb, q, k.v("hmask", h), None, ALU.mult).then_inc(k.dve.sem, 1)
                for i, (z, l) in enumerate(steps):
                    half = 1 << l
                    c = C[:, z, :]
                    if i >= 1:
                        dve.wait_ge(k.act.sem, k.act.at(i))
                    if l == 8 and z == 1:
                        link(dve.tensor_copy(tmp[:, CTX], c[:, CTX]))
                        link(dve.tensor_scalar(tmp[:, LAT], c[:, LAT], total_sum, None, ALU.subtract))
                    else:
                        cv = c.rearrange("p (n t) -> p n t", t=2 * half)
                        at = half - 1 if z == 0 else half
                        link(dve.tensor_tensor(tmp.rearrange("p (n t) -> p n t", t=2 * half), cv,
                                               cv[:, :, at:at + 1].to_broadcast([P, T // (2 * half), 2 * half]), ALU.subtract))
                    dve.scalar_tensor_tensor(tmp, tmp, -1.0, tmp, ALU.mult, ALU.max).then_inc(k.dve.sem, 1)
                    if i >= 2:
                        dve.wait_ge(k.mm.sem, k.mm.at(i))
                    elif i == 1:
                        dve.wait_ge(k.mm.sem, k.mm.at(1))
                    dve.wait_ge(k.act.sem, k.act.at(i + 1))
                    dve.tensor_tensor(Kt[i % 2], kx, E, ALU.mult).then_inc(k.dve.sem, 1)
                    for h, qb in enumerate((Q0[i % 2], Q1[i % 2])):
                        dve.scalar_tensor_tensor(qb, q, k.v("hmask", h), E, ALU.mult, ALU.mult).then_inc(k.dve.sem, 1)
                    if i == 0:
                        dve.wait_ge(k.mm.sem, k.mm.at(1))
                        for h in range(2):
                            dve.scalar_tensor_tensor(accs[h].rearrange("p (b t) -> p b t", b=NB),
                                                     k.ps[:, h, :].rearrange("p (b t) -> p b t", b=NB), 2.0,
                                                     k.ident.unsqueeze(1).to_broadcast([P, NB, P]),
                                                     ALU.mult, ALU.mult).then_inc(k.pool.sem, 1)
                    else:
                        masked(dve, i - 1)
                masked(dve, len(steps) - 1)
                link.close()

        k.mm.base += 1 + len(steps)
        k.act.base += len(steps)
        k.dve.base += 2 + 4 * len(steps)
        k.pooll.base += 28
        k.pool.base += 2 + 2 * 14

        off7 = [k.H[:, 3, :], k.H[:, 4, :]]
        off8 = [k.H[:, 5, :], k.H[:, 6, :]]
        with nc.Block() as block:
            @block.scalar
            def _(act):
                for h in range(2):
                    act.activation(off7[h], k.ps[:, 4 + h, :], ACT.Copy).then_inc(k.act.sem, 1)
                for h in range(2):
                    act.wait_ge(k.mm.sem, k.mm.at(h + 1))
                    act.activation(ev.qk[:, 4 + 2 * j + h, :], k.ps[:, h, :], ACT.Copy)

            @block.vector
            def _(dve):
                for h in range(2):
                    dve.tensor_copy(off8[h], k.ps[:, 6 + h, :]).then_inc(k.dve.sem, 1)

            @block.tensor
            def _(pe):
                for h in range(2):
                    pe.wait_ge(k.act.sem, k.act.at(h + 1))
                    pe.wait_ge(k.dve.sem, k.dve.at(h + 1))
                    v = lambda b: ev.V[:, b, 512 + (2 * j + h) * P:512 + (2 * j + h + 1) * P]
                    for t in range(NB):
                        parts = [(t, accs[h][:, t * P:(t + 1) * P]), (t ^ 1, off7[h][:, (t ^ 1) * P:((t ^ 1) + 1) * P])]
                        if t >= 2:
                            parts += [(s, off8[h][:, s * 256 + (t - 2) * P:s * 256 + (t - 1) * P]) for s in range(2)]
                        for n, (s, rhs) in enumerate(parts):
                            mm = pe.matmul(k.ps[:, h, t * P:(t + 1) * P], lhsT=v(s), rhs=rhs, start=n == 0, stop=n == len(parts) - 1)
                    mm.then_inc(k.mm.sem, 1)
        k.act.base += 2
        k.dve.base += 2
        k.mm.base += 2


def masked_before(steps, i):
    n = 2
    for z, l in steps[:max(i - 1, 0)]:
        n += 2 * (l < 7)
    return n if i >= 1 else 0


def stage_even_gate(k, ev):
    nc = k.nc
    sq = [k.W[:, 10240 + i * T:10240 + (i + 1) * T] for i in range(2)]
    rows = k.W[:, 11264:11264 + T]
    one_at = k.W[:, 11776:11776 + 2 * P]
    y = [k.W[:, 12288 + i * T:12288 + (i + 1) * T] for i in range(2)]
    with nc.Block() as block:
        @block.scalar
        def _(act):
            for i in range(8):
                if i >= 2:
                    act.wait_ge(k.mm.sem, k.mm.at(i - 1))
                act.activation(sq[i % 2], ev.qk[:, i, :], ACT.Square).then_inc(k.act.sem, 1)
            act.wait_ge(k.dve.sem, k.dve.at(2))
            act.activation(rows, rows, ACT.Sqrt).then_inc(k.act.sem, 1)

        @block.tensor
        def _(pe):
            pe.wait_ge(k.dve.sem, k.dve.at(1))
            for i in range(8):
                pe.wait_ge(k.act.sem, k.act.at(i + 1))
                pe.matmul(k.ps[:, 0, :], lhsT=one_at[:, P - 1 - i:2 * P - 1 - i], rhs=sq[i % 2],
                          start=i == 0, stop=i == 7).then_inc(k.mm.sem, 1)
            pe.wait_ge(k.dve.sem, k.dve.at(3))
            for i in range(8):
                if i >= 4:
                    pe.wait_ge(k.dve.sem, k.dve.at(2 * i - 4))
                pe.matmul(k.ps[:, 1 + i % 4, :], lhsT=k.ident[:, i:i + 1].to_broadcast([P, P]), rhs=rows,
                          start=True, stop=True).then_inc(k.mm.sem, 1)

        @block.vector
        def _(dve):
            link = Link(k.dvel, dve)
            link(dve.memset(one_at, 0.0))
            dve.memset(one_at[:, P - 1:P], 1.0).then_inc(k.dve.sem, 1)
            dve.wait_ge(k.mm.sem, k.mm.at(8))
            dve.tensor_scalar(rows, k.ps[:, 0, :], 1.0 / P, EPS, ALU.mult, ALU.add).then_inc(k.dve.sem, 1)
            dve.wait_ge(k.act.sem, k.act.at(9))
            dve.reciprocal(rows, rows).then_inc(k.dve.sem, 1)
            for i in range(8):
                dve.wait_ge(k.mm.sem, k.mm.at(9 + i))
                if i >= 2:
                    dve.wait_ge(k.dve.sem, k.dve.at(2 * i + 1))
                dve.scalar_tensor_tensor(y[i % 2], ev.qk[:, i, :], k.v("headg", i), k.ps[:, 1 + i % 4, :],
                                         ALU.mult, ALU.mult).then_inc(k.dve.sem, 1)
                dve.wait_ge(k.dve.sem, k.dve.at(2 * i + 4))
                dve.tensor_tensor(k.H[:, i, :], y[i % 2], ev.gate[:, i, :], ALU.mult).then_inc(k.dve.sem, 1)
            link.close()
    k.act.base += 9
    k.mm.base += 16
    k.dve.base += 3 + 16


def block2_even(k):
    both = slice(0, T)
    ev = Even(k)
    stage_ada2(k, 0)
    stage_norm2(k, 0, 0, both)
    stage_even_project(k, ev)
    stage_mlstm_gates(k, ev)
    stage_mlstm(k, ev)
    stage_gla(k, ev)
    stage_even_gate(k, ev)
    Y = k.W[:, 11264:15360].rearrange("p (o t) -> p o t", o=KD)
    stage_square(k, both, Y)
    stage_post_norm(k, 0, 0, both, Y)
    stage_norm2(k, 0, 1, both)
    stage_conv_ffn(k, 0, both, Y)
    stage_post_norm(k, 0, 1, both, Y)


RW_ORDER = (0, 2, 3, 1, 4, 5)


def stage_rwkv_project(k):
    nc = k.nc
    XX = k.W[:, 0:4096].rearrange("p (o t) -> p o t", o=KD)
    XB = [k.W[:, 4096 * (b + 1):4096 * (b + 2)].rearrange("p (o t) -> p o t", o=KD) for b in range(2)]
    out = k.W[:, 12288:14336].rearrange("p (o t) -> p o t", o=4)
    owner = [i // KD for i in range(27 * KD)]
    unit_done, out_done, signals, total = plan(owner)
    last = [7, 15, 23, 24, 25, 26]
    tokens = lambda n: LAT if n in (0, 5) else slice(0, T)
    rows = S // GRID_W
    with nc.Block() as block:
        @block.sync
        def _(sp):
            refill(k, sp, unit_done, 14)

        @block.tensor
        def _(pe):
            for n in range(6):
                first_o = 0 if n == 0 else last[n - 1] + 1

                def before(o, n=n, first_o=first_o):
                    pe.wait_ge(k.dve.sem, k.dve.at(8 * n + 8))
                    if first_o + o >= 4:
                        pe.wait_ge(k.act.sem, k.act.at(first_o + o - 3))
                gemm(k, pe, last[n] - first_o + 1, KD, lambda kk, n=n: XB[n % 2][:, kk, tokens(n)],
                     lambda o, n=n, f=first_o: k.ps[:, (f + o) % 4, tokens(n)], before, signals, first=first_o * KD)

        @block.vector
        def _(dve):
            link = Link(k.dvel, dve)
            for i in range(KD):
                link.mark(dve.tensor_scalar(XX[:, i, :], k.H[:, i, :], -1.0, None, ALU.mult))
            link.wait()
            for i in range(KD):
                quarter = i // 2
                x, h = XX[:, i, :], k.H[:, i, :]
                if quarter % 2 == 0:
                    pieces = [(x[:, 1:S], h[:, 0:S - 1])]
                else:
                    pieces = [(x[:, 0:S - 1], h[:, 1:S])]
                xg, hg = (y[:, LAT].rearrange("p (r c) -> p r c", r=rows) for y in (x, h))
                pieces.append([(xg[:, :, 1:GRID_W], hg[:, :, 0:GRID_W - 1]), (xg[:, :, 0:GRID_W - 1], hg[:, :, 1:GRID_W]),
                               (xg[:, 1:rows, :], hg[:, 0:rows - 1, :]), (xg[:, 0:rows - 1, :], hg[:, 1:rows, :])][quarter])
                for a, b in pieces:
                    link.mark(dve.tensor_tensor(a, a, b, ALU.add))
            link.wait()
            for n, m in enumerate(RW_ORDER):
                if n >= 2:
                    dve.wait_ge(k.mm.sem, k.mm.at(out_done[last[n - 2]]))
                for i in range(KD):
                    c = tokens(n)
                    dve.scalar_tensor_tensor(XB[n % 2][:, i, c], XX[:, i, c], k.v("mu", m * 8 + i), k.H[:, i, c],
                                             ALU.mult, ALU.add).then_inc(k.dve.sem, 1)
            link.close()

        @block.scalar
        def _(act):
            for o in range(24):
                act.wait_ge(k.mm.sem, k.mm.at(out_done[o]))
                if o >= 4:
                    act.wait_ge(k.stored[o % 4], 16 * (o // 4))
                c = tokens(o // 8)
                act.activation(out[:, o % 4, c], k.ps[:, o % 4, c], ACT.Copy).then_inc(k.act.sem, 1)
                act.wait_ge(k.act.sem, k.act.at(o + 1))
                act.dma_start(k.a["rkv"][o % 8, :, o // 8, c], out[:, o % 4, c]).then_inc(k.stored[o % 4], 16)
            for o, f in ((24, ACT.Tanh), (25, ACT.Copy)):
                act.wait_ge(k.mm.sem, k.mm.at(out_done[o]))
                act.activation(k.X[:, 2 * (o - 24):2 * (o - 24) + 2, CTX],
                               k.ps[:, o % 4, :].rearrange("p (a t) -> p a t", a=2), f).then_inc(k.act.sem, 1)
            act.wait_ge(k.mm.sem, k.mm.at(out_done[26]))
            act.activation(k.X[:, 5, CTX], k.ps[:, 2, LAT], ACT.Sigmoid).then_inc(k.act.sem, 1)
            for b in range(4):
                act.wait_ge(k.stored[b], 16 * 6)
    k.mm.base += total
    k.act.base += 27
    k.dve.base += 48
    k.unit += 14


class Events:

    def __init__(self, signal, names, turns):
        self.s, self.names, self.turns = signal, {n: i + 1 for i, n in enumerate(names)}, turns
        assert len(self.names) == len(names)
        self.per = len(names)
        self.sent = 0

    def fire(self, ins, name):
        self.sent += 1
        assert self.names[name] == self.sent, (name, self.names[name], self.sent)
        ins.then_inc(self.s.sem, 1)

    def at(self, turn, name):
        n = 0 if name is None else self.names[name]
        return turn * self.per + (self.s.base + n)

    def close(self):
        assert self.sent == self.per
        self.s.base += self.per * self.turns


def rwkv_events():
    pe, dve, act, pool = [], [], [], []
    for ph in range(2):
        p = f"{ph}."
        pe += [p + n for n in ["low", "vt", "ss", "gram0", "gram1", "tok0", "tok1", "m1_0", "m1_1"]]
        dve += [p + n for n in ["kk0"]]
        act += [p + n for n in ["sg0", "sg1", "a"] + ["g"] * ph + ["vtok", "nrm"]]
        for z in "01":
            dve += [p + n + z for n in ("ref", "ie")]
            act += [p + n + z for n in ["io"] + ["e0"] * ph + ["e1", "e2"]]
        pool += [p + "zero0", p + "zero1"]
        act += [p + "mk0", p + "mk1"]
        for z in "01":
            dve += [p + "ab" + z]
        for z in "01":
            dve += [p + n + z for n in ("ge", "mt")]
        act += [p + "tokc0", p + "tokc1", p + "m1c0", p + "m1c1"]
        for l in range(1, 6):
            for z in "01":
                pe += [p + f"t{l}" + z]
                pool += [p + f"ot{l}" + z]
                act += [p + f"tc{l}" + z]
            for z in "01":
                pe += [p + f"n{l}" + z]
                dve += [p + f"mn{l}" + z]
        pe += [p + "rv0", p + "rv1"]
        act += [p + "rvc0", p + "rvc1"]
        for i in range(4):
            dve += [p + f"h{i}0", p + f"h{i}1", p + f"rh{i}0", p + f"rh{i}1"]
            pe += [p + f"{n}{i}{z}" for n in "rsu" for z in "01"]
            act += [p + f"sc{i}0", p + f"sc{i}1"]
        if ph == 0:
            dve += [p + "end"]
        else:
            pe += [p + "y", p + "bonus", p + "mean", p + "var"]
            act += [p + "yc", p + "ysq", p + "yrt"]
            dve += [p + n for n in ("rk", "yy", "yd", "yv", "end")]
    return pe, dve, act, pool


def stage_rwkv(k):
    nc = k.nc
    W, H, X = k.W, k.H, k.X
    at = [0]

    def take(n):
        at[0] += n
        assert at[0] <= 16384
        return W[:, at[0] - n:at[0]]
    rkv = take(1536).rearrange("p (i t) -> p i t", i=3)
    wj = take(520)
    VC = take(512).rearrange("p (a b v) -> p a b v", a=2, b=2)
    Vt = take(256).rearrange("p (b v) -> p b v", b=2)
    a_, kk, ka, k2, g_ = (take(256) for _ in range(5))
    reset = take(256)
    inc, exc, LT, KA, BR, KR, M, MT, T1, OT, tok, St, hatO, SA, RHS, masked = ([] for _ in range(16))
    for z in range(2):
        both_ = take(512)
        inc.append(both_[:, 0:256])
        exc.append(both_[:, 256:512])
        for lst in (LT, KA, BR, KR, M, MT):
            lst.append(take(512).rearrange("p (h b t) -> p h b t", h=2, b=2))
        mm_ = take(1024)
        masked.append(mm_.rearrange("p (i h t) -> p i h t", i=2, h=2))
        T1.append(mm_[:, 0:512].rearrange("p (h b t) -> p h b t", h=2, b=2))
        OT.append(mm_[:, 512:1024].rearrange("p (h b t) -> p h b t", h=2, b=2))
        tok.append(take(512).rearrange("p (i b v) -> p i b v", i=2, b=2))
        St.append(take(P))
        hatO.append(take(P))
        SA.append(take(256).rearrange("p (a v) -> p a v", a=2))
        RHS.append(take(P))
    RV = [inc[z] for z in range(2)]
    hat = [[k.hat[:, 2 * z + b, :] for b in range(2)] for z in range(2)]
    e = [[M[z].rearrange("p h b t -> p (h b t)")[:, 0:256], M[z].rearrange("p h b t -> p (h b t)")[:, 256:512],
          MT[z].rearrange("p h b t -> p (h b t)")[:, 0:256]] for z in range(2)]
    AR = [H[:, 2 * z:2 * z + 2, CTX] for z in range(2)]
    BK = [H[:, 4 + 2 * z:6 + 2 * z, CTX] for z in range(2)]
    TW, TA = (X[:, 2 * i:2 * i + 2, CTX] for i in range(2))
    TG = X[:, 5, CTX]
    IO = [k.sm[:, 16 * z:16 * z + 8] for z in range(2)]
    ru = [k.sm[:, 32 + 16 * z:40 + 16 * z] for z in range(2)]
    wa2, ww2, wg2 = wj[:, 0:128], [wj[:, 128:256], wj[:, 256:384]], wj[:, 384:512]
    col = lambda i: wj[:, 512 + i:513 + i]
    cols4 = lambda x: x.rearrange("p (c t) -> p c t", c=4)
    TURNS = 8
    pe_n, dve_n, act_n, pool_n = rwkv_events()
    E_pe, E_dve = Events(k.mm, pe_n, TURNS), Events(k.dve, dve_n, TURNS)
    E_act, E_pool = Events(k.act, act_n, TURNS), Events(k.pool, pool_n, TURNS)
    chunk = lambda z, i: i if z == 0 else 3 - i
    cm = k.cmask
    bc4 = lambda m: m.unsqueeze(1).unsqueeze(1).to_broadcast([P, 2, 2, P])
    psb = lambda b, i: k.ps[:, b:b + 2, :].rearrange("p h (b i t) -> p h b i t", b=2, i=2)[:, :, :, i, :]
    flat = lambda t: t.rearrange("p h b t -> p (h b t)")

    def update(dve, link, W_, p, i, z):
        ch = chunk(z, i)
        cout = 4 + ch if z == 0 else ch
        W_(E_pe, p + f"u{i}{z}")
        for h in range(2):
            q = slice(64 * h, 64 * h + 64)
            link(dve.scalar_tensor_tensor(St[z][q, q], k.ps[q, 4 + 2 * z, q], IO[z][q, cout:cout + 1], hatO[z][q, q],
                                          ALU.mult, ALU.add))

    with nc.Block() as block:
        @block.vector
        def _(dve):
            for z in range(2):
                dve.memset(SA[z], 0.0)
                dve.memset(RHS[z], 0.0)
            dve.memset(VC, 0.0)
            link = Link(k.dvel, dve)
            link(dve.memset(reset, 1.0))
            link(dve.memset(cols4(reset)[:, :, 0:1], 0.0))
            link.close()

        @block.sync
        def _(sp):
            sp.dma_start(cm[:, :], k.a["chunk_masks"]).then_inc(k.dma.sem, 16)
            sp.wait_ge(k.dma.sem, k.dma.at(16))
    k.dma.base += 16

    with nc.Block() as block:
        @block.sync
        def _(sp):
            tile = lambda name, j: k.a[name][bass.ds(j, 1)] if name == "rw_tiles" else \
                k.a[name][bass.ds(j, 1)].rearrange("a p i t -> (a p) i t")

            def early(j):
                sp.dma_start(rkv[:, 1:3, CTX], tile("rkv", j)[:, 1:3, CTX]).then_inc(k.ctx_in, 16)

            def weights(j):
                sp.dma_start(wj[:, 0:517], tile("rw_tiles", j).rearrange("a p n -> (a p) n")[:, 0:517]).then_inc(k.ctx_in, 16)

            def late(j):
                sp.wait_ge(k.dve.sem, E_dve.at(j, None))
                sp.dma_start(rkv[:, 1:3, LAT], tile("rkv", j)[:, 1:3, LAT]).then_inc(k.lat_in, 16)
                sp.dma_start(rkv[:, 0, LAT], tile("rkv", j)[:, 0, LAT]).then_inc(k.lat_in, 16)
                sp.dma_start(wj[:, 517:520], tile("rw_tiles", j).rearrange("a p n -> (a p) n")[:, 517:520]).then_inc(k.lat_in, 16)
            early(0)
            weights(0)
            with sp.Fori(0, TURNS - 1) as j:
                late(j)
                sp.wait_ge(k.dve.sem, E_dve.at(j, "0.end"))
                early(j + 1)
                sp.wait_ge(k.dve.sem, E_dve.at(j, "1.ab0"))
                weights(j + 1)
            late(TURNS - 1)

        @block.tensor
        def _(pe):
            with pe.Fori(0, TURNS) as j:
                W_ = lambda E, n: pe.wait_ge(E.s.sem, E.at(j, n))
                pe.wait_ge(k.ctx_in, j * 32 + 32)
                pe.wait_ge(k.dve.sem, E_dve.at(j, None) - 2)
                for ph in range(2):
                    p = f"{ph}."
                    if ph:
                        pe.wait_ge(k.lat_in, j * 48 + 48)
                        W_(E_dve, "0.end")
                    mm = pe.matmul(k.ps[:, 0, 0:256], lhsT=wa2, rhs=TA[:, ph, :], start=True, stop=True)
                    for z in range(2):
                        mm = pe.matmul(k.ps[:, z, 256 * (1 - z):256 * (2 - z)], lhsT=ww2[z], rhs=TW[:, ph, :], start=True, stop=True)
                    if ph:
                        mm = pe.matmul(k.ps[:, 1, 256:512], lhsT=wg2, rhs=TG, start=True, stop=True)
                    E_pe.fire(mm, p + "low")
                    if ph == 0:
                        pe.wait_ge(k.dve.sem, E_dve.at(j, None))
                    for b in range(2):
                        mm = pe.transpose(k.ps[:, 2, b * P:(b + 1) * P], rkv[:, 2, ph * S + b * P:ph * S + (b + 1) * P], k.ident)
                    E_pe.fire(mm, p + "vt")
                    W_(E_dve, p + "kk0")
                    mm = pe.matmul(k.ps[:, 3, 0:256], lhsT=k.hblock, rhs=flat(LT[1])[:, 0:256], start=True, stop=True)
                    E_pe.fire(mm, p + "ss")
                    for z in range(2):
                        W_(E_act, p + f"mk{z}")
                        if z:
                            W_(E_dve, p + "ge0")
                        for i in range(2):
                            for h in range(2):
                                for b in range(2):
                                    bc = slice(b * P, (b + 1) * P)
                                    n = 1 + ph
                                    mm = pe.matmul(k.ps[:, 4 + 2 * i + h, b * 256:b * 256 + n * P].rearrange("p (i t) -> p i t", i=n),
                                                   lhsT=masked[z][:, i, h, bc], rhs=AR[z][:, 0:n, bc], start=True, stop=True)
                        E_pe.fire(mm, p + f"gram{z}")
                    for z in range(2):
                        if z == 0:
                            W_(E_act, p + "vtok")
                        else:
                            W_(E_act, p + "nrm")
                        for i in range(2):
                            for b in range(2):
                                mm = pe.transpose(k.ps[:, 2 + z, (2 * i + b) * P:(2 * i + b + 1) * P],
                                                  BK[z][:, i, b * P:(b + 1) * P], k.ident)
                        E_pe.fire(mm, p + f"tok{z}")
                    for z in range(2):
                        W_(E_dve, p + f"mt{z}")
                        if z == 0:
                            W_(E_act, p + ("g" if ph else "a"))
                        for n in range(4):
                            mm = pe.transpose(k.ps[:, z, n * P:(n + 1) * P], MT[z][:, n // 2, n % 2, :], k.ident)
                        E_pe.fire(mm, p + f"m1_{z}")
                    for l in range(1, 6):
                        for z in range(2):
                            W_(E_pool, p + f"ot{l}{z}")
                            W_(E_act, p + f"m1c{z}") if l == 1 else W_(E_dve, p + f"mn{l - 1}{z}")
                            for n in range(4):
                                mm = pe.matmul(k.ps[:, z, n * P:(n + 1) * P], lhsT=OT[z][:, n // 2, n % 2, :],
                                               rhs=M[z][:, n // 2, n % 2, :], start=True, stop=True)
                            E_pe.fire(mm, p + f"t{l}{z}")
                        for z in range(2):
                            W_(E_act, p + f"tc{l}{z}")
                            if l == 1:
                                W_(E_dve, p + "ge1")
                            for n in range(4):
                                q = (n // 2, n % 2)
                                mm = pe.matmul(k.ps[:, 4 + 2 * z, n * P:(n + 1) * P], lhsT=T1[z][:, q[0], q[1], :],
                                               rhs=MT[z][:, q[0], q[1], :], start=True, stop=True)
                                if l < 5:
                                    mm = pe.matmul(k.ps[:, 5 + 2 * z, n * P:(n + 1) * P], lhsT=MT[z][:, q[0], q[1], :],
                                                   rhs=T1[z][:, q[0], q[1], :], start=True, stop=True)
                            E_pe.fire(mm, p + f"n{l}{z}")
                    for z in range(2):
                        W_(E_act, p + f"tokc{z}")
                        for b in range(2):
                            for h in range(2):
                                c = (2 * b + h) * P
                                mm = pe.matmul(k.ps[:, 2 + z, c:c + P], lhsT=KA[z][:, h, b, :], rhs=Vt[:, b, :],
                                               start=True, stop=True)
                        E_pe.fire(mm, p + f"rv{z}")
                    for i in range(4):
                        for z in range(2):
                            ch = chunk(z, i)
                            r = 64 * (ch % 2)
                            W_(E_dve, p + f"h{i}{z}")
                            mm = pe.matmul(k.ps[r:r + 64, z, 0:P], lhsT=AR[z][:, 0, ch * 64:ch * 64 + 64],
                                           rhs=hat[z][i % 2], start=True, stop=True)
                            E_pe.fire(mm, p + f"r{i}{z}")
                        for z in range(2):
                            ch = chunk(z, i)
                            b, r = ch // 2, 64 * (ch % 2)
                            W_(E_dve, p + f"rh{i}{z}")
                            if i == 0:
                                W_(E_dve, p + f"mn5{z}")
                            for h in range(2):
                                mm = pe.matmul(k.ps[r:r + 64, z, h * 64:h * 64 + 64], lhsT=MT[z][:, h, b, r:r + 64],
                                               rhs=RHS[z][:, h * 64:h * 64 + 64], start=True, stop=True)
                            E_pe.fire(mm, p + f"s{i}{z}")
                        for z in range(2):
                            ch = chunk(z, i)
                            b, par = ch // 2, ch % 2
                            r = 64 * par
                            W_(E_act, p + f"sc{i}{z}")
                            pe.matmul(k.ps[:, 4 + 2 * z, 0:P], lhsT=tok[z][:, 0, b, :], rhs=SA[z][:, par, :], start=True, stop=False)
                            mm = pe.matmul(k.ps[:, 4 + 2 * z, 0:P], lhsT=tok[z][:, 1, b, :], rhs=VC[:, par, b, :], start=False, stop=True)
                            E_pe.fire(mm, p + f"u{i}{z}")
                            if ph:
                                for h in range(2):
                                    yh = k.ps[64 * h:64 * h + 64, 5 + 2 * z, ch * 64:ch * 64 + 64]
                                    pe.matmul(yh, lhsT=hat[z][i % 2][:, 64 * h:64 * h + 64], rhs=AR[z][:, 1, ch * 64:ch * 64 + 64],
                                              start=True, stop=False, skip_group_check=True)
                                    pe.matmul(yh, lhsT=SA[z][:, par, h * 64:h * 64 + 64], rhs=BR[z][:, h, b, r:r + 64],
                                              start=False, stop=False, skip_group_check=True)
                                    mm = pe.matmul(yh, lhsT=VC[:, par, b, h * 64:h * 64 + 64], rhs=KR[z][:, h, b, r:r + 64],
                                                   start=False, stop=True, skip_group_check=True)
                    if ph:
                        E_pe.fire(mm, p + "y")
                        W_(E_dve, p + "rk")
                        E_pe.fire(pe.matmul(k.ps[:, 2, S:2 * S], lhsT=k.hblock, rhs=T1[0].rearrange("p h b t -> p (h b t)")[:, 0:256],
                                            start=True, stop=True), p + "bonus")
                        W_(E_dve, p + "yy")
                        E_pe.fire(pe.matmul(k.ps[:, 2, 0:S], lhsT=k.hblock, rhs=flat(M[0])[:, 0:256], start=True, stop=True), p + "mean")
                        W_(E_act, p + "ysq")
                        E_pe.fire(pe.matmul(k.ps[:, 3, 0:S], lhsT=k.hblock, rhs=flat(M[1])[:, 0:256], start=True, stop=True), p + "var")

        @block.scalar
        def _(act):
            with act.Fori(0, TURNS) as j:
                W_ = lambda E, n: act.wait_ge(E.s.sem, E.at(j, n))

                def go(name, *args, **kw):
                    E_act.fire(act.activation(*args, **kw), name)
                act.wait_ge(k.ctx_in, j * 32 + 32)
                for ph in range(2):
                    p = f"{ph}."
                    if ph:
                        W_(E_dve, "0.end")
                    W_(E_pe, p + "low")
                    for z in range(2):
                        go(p + f"sg{z}", inc[z], k.ps[:, z, 256 * (1 - z):256 * (2 - z)], ACT.Sigmoid, bias=col(z))
                    go(p + "a", a_, k.ps[:, 0, 0:256], ACT.Sigmoid, bias=col(2))
                    if ph:
                        go(p + "g", g_, k.ps[:, 1, 256:512], ACT.Copy)
                    W_(E_pe, p + "vt")
                    vt = k.ps[:, 2, 0:256].rearrange("p (b v) -> p b v", b=2)
                    act.activation(VC[0:64, 0, :, :], vt[0:64], ACT.Copy)
                    act.activation(VC[64:128, 1, :, :], vt[64:128], ACT.Copy)
                    go(p + "vtok", Vt, vt, ACT.Copy)
                    W_(E_pe, p + "ss")
                    go(p + "nrm", flat(LT[1])[:, 256:512], k.ps[:, 3, 0:256], ACT.Sqrt)
                    for z in range(2):
                        W_(E_dve, p + f"ref{z}")
                        go(p + f"io{z}", IO[z], ru[z], ACT.Exp)
                        W_(E_dve, p + f"ie{z}")
                        src = [(inc[z], 1.0), (exc[z], 1.0), (inc[z], -1.0)] if z == 0 else \
                              [(exc[z], -1.0), (inc[z], -1.0), (exc[z], 1.0)]
                        for n, (x, sc) in enumerate(src):
                            if n == 0 and ph == 0:
                                continue
                            go(p + f"e{n}{z}", e[z][n], x, ACT.Exp, scale=sc)
                    for z in range(2):
                        W_(E_pool, p + f"zero{z}")
                        W_(E_dve, p + f"ab{z}")
                        act.activation(masked[z][0:64, :, 0, :], BK[z][0:64], ACT.Copy)
                        go(p + f"mk{z}", masked[z][64:128, :, 1, :], BK[z][64:128], ACT.Copy)
                    for z in range(2):
                        W_(E_pe, p + f"tok{z}")
                        go(p + f"tokc{z}", tok[z].rearrange("p i b v -> p (i b v)"), k.ps[:, 2 + z, :], ACT.Copy)
                    for z in range(2):
                        W_(E_pe, p + f"m1_{z}")
                        go(p + f"m1c{z}", flat(M[z]), k.ps[:, z, :], ACT.Copy)
                    for l in range(1, 6):
                        for z in range(2):
                            W_(E_pe, p + f"t{l}{z}")
                            go(p + f"tc{l}{z}", flat(T1[z]), k.ps[:, z, :], ACT.Copy)
                    for z in range(2):
                        W_(E_pe, p + f"rv{z}")
                        own = [(RV[z].rearrange("p (b v) -> p b v", b=2)[:, :, 64 * h:64 * h + 64],
                                k.ps[:, 2 + z, :].rearrange("p (b v) -> p b v", b=2)[:, :, 192 * h:192 * h + 64]) for h in range(2)]
                        act.activation(*own[0], ACT.Copy)
                        go(p + f"rvc{z}", *own[1], ACT.Copy)
                    for i in range(4):
                        for z in range(2):
                            par = chunk(z, i) % 2
                            r = slice(64 * par, 64 * par + 64)
                            W_(E_pe, p + f"s{i}{z}")
                            go(p + f"sc{i}{z}", SA[z][r, par, :], k.ps[r, z, 0:P], ACT.Copy, scale=-1.0)
                    if ph:
                        W_(E_pe, p + "y")
                        go(p + "yc", flat(M[0])[:, 0:256], k.ps[:, 7, 0:256], ACT.Copy)
                        W_(E_dve, p + "yd")
                        go(p + "ysq", flat(M[1])[:, 0:256], flat(M[0])[:, 256:512], ACT.Square)
                        W_(E_dve, p + "yv")
                        go(p + "yrt", flat(M[1])[:, 256:512], flat(M[1])[:, 256:512], ACT.Sqrt)

        @block.gpsimd
        def _(pool):
            with pool.Fori(0, TURNS) as j:
                W_ = lambda E, n: pool.wait_ge(E.s.sem, E.at(j, n))
                for ph in range(2):
                    p = f"{ph}."
                    for z in range(2):
                        if ph == 0:
                            pool.wait_ge(k.dve.sem, E_dve.at(j, None))
                        else:
                            W_(E_pe, f"0.n5{z}")
                        E_pool.fire(pool.tensor_tensor(flat(masked[z]), k.v("hmask", 0).to_broadcast([P, 1024]),
                                                       k.v("hmask", 1).to_broadcast([P, 1024]), ALU.mult), p + f"zero{z}")
                    for l in range(1, 6):
                        for z in range(2):
                            if l == 1:
                                W_(E_dve, p + f"ge{z}")
                            else:
                                W_(E_pe, p + f"t{l - 1}{z}")
                            m = k.level[z][:, l * P:(l + 1) * P]
                            E_pool.fire(pool.tensor_tensor(OT[z], LT[z], bc4(m), ALU.mult), p + f"ot{l}{z}")

        @block.vector
        def _(dve):
            link = Link(k.dvel, dve)
            with dve.Fori(0, TURNS) as j:
                link.loop(j, RW_LINKS)
                W_ = lambda E, n: dve.wait_ge(E.s.sem, E.at(j, n))

                def fire(name, ins):
                    E_dve.fire(ins, name)
                    W_(E_dve, name)
                dve.wait_ge(k.ctx_in, j * 32 + 32)
                for z in range(2):
                    link(dve.memset(St[z], 0.0))
                    link(dve.memset(hat[z][0], 0.0))
                for ph in range(2):
                    p = f"{ph}."
                    cols = slice(ph * S, ph * S + S)
                    r_, kx, vx = (rkv[:, n, cols] for n in range(3))
                    if ph:
                        dve.wait_ge(k.lat_in, j * 48 + 48)
                    kk0, sq, nrm = kk, flat(LT[1])[:, 0:256], flat(LT[1])[:, 256:512]
                    link(dve.tensor_scalar(kk0, kx, col(3), None, ALU.mult))
                    fire(p + "kk0", dve.tensor_tensor(sq, kk0, kk0, ALU.mult))
                    for z in range(2):
                        W_(E_act, p + f"sg{z}")
                        link(dve.tensor_scalar(exc[z], inc[z], -float(np.exp(-0.5)), None, ALU.mult))
                        link(dve.tensor_tensor_scan(inc[z], reset, exc[z], 0.0, ALU.mult, ALU.add))
                        C4 = cols4(inc[z])
                        ref, rest = ru[z][:, 0:4], ru[z][:, 4:8]
                        link(dve.tensor_copy(ref.unsqueeze(2), C4[:, :, 31:32]))
                        fire(p + f"ref{z}", dve.tensor_tensor(rest.unsqueeze(2), C4[:, :, 63:64], ref.unsqueeze(2), ALU.subtract))
                        link(dve.tensor_tensor(C4, C4, ref.unsqueeze(2).to_broadcast([P, 4, 64]), ALU.subtract))
                        fire(p + f"ie{z}", dve.tensor_tensor(exc[z], inc[z], exc[z], ALU.subtract))
                    W_(E_act, p + "nrm")
                    link(dve.tensor_scalar(nrm, nrm, 1e-12, None, ALU.max))
                    link(dve.reciprocal(nrm, nrm))
                    link(dve.tensor_tensor(kk, kk0, nrm, ALU.mult))
                    link(dve.tensor_tensor(ka, kk, a_, ALU.mult))
                    link(dve.tensor_scalar(k2, a_, 1.0, col(4), ALU.subtract, ALU.mult))
                    link(dve.scalar_tensor_tensor(k2, k2, 1.0, kx, ALU.add, ALU.mult))
                    for z in range(2):
                        W_(E_act, p + f"e2{z}")
                        link(dve.tensor_tensor(AR[z][:, 0, :], kk, e[z][1], ALU.mult))
                        if ph:
                            link(dve.tensor_tensor(AR[z][:, 1, :], r_, e[z][0], ALU.mult))
                        link(dve.tensor_tensor(BK[z][:, 0, :], ka, e[z][2], ALU.mult))
                        fire(p + f"ab{z}", dve.tensor_tensor(BK[z][:, 1, :], k2, e[z][2], ALU.mult))
                    for z in range(2):
                        W_(E_pe, p + f"gram{z}")
                        s_, i_ = bc4(cm[:, (2 * z) * P:(2 * z + 1) * P]), bc4(cm[:, (2 * z + 1) * P:(2 * z + 2) * P])
                        link(dve.tensor_tensor(LT[z], psb(4, 0), s_, ALU.mult))
                        if ph:
                            link(dve.tensor_tensor(BR[z], psb(4, 1), i_, ALU.mult))
                            link(dve.tensor_tensor(KR[z], psb(6, 1), i_, ALU.mult))
                        fire(p + f"ge{z}", dve.tensor_tensor(KA[z], psb(6, 0), s_, ALU.mult))
                        link(dve.tensor_tensor(MT[z], LT[z], bc4(k.level[z][:, 0:P]), ALU.mult))
                        fire(p + f"mt{z}", dve.tensor_tensor(MT[z], bc4(k.ident), MT[z], ALU.subtract))
                    for l in range(1, 6):
                        for z in range(2):
                            W_(E_pe, p + f"n{l}{z}")
                            if l < 5:
                                link(dve.tensor_tensor(flat(M[z]), flat(M[z]), k.ps[:, 5 + 2 * z, :], ALU.subtract))
                            fire(p + f"mn{l}{z}", dve.tensor_tensor(flat(MT[z]), flat(MT[z]), k.ps[:, 4 + 2 * z, :], ALU.subtract))
                    for i in range(4):
                        for z in range(2):
                            ch = chunk(z, i)
                            cin, cout = (ch, 4 + ch) if z == 0 else (4 + ch, ch)
                            if i:
                                update(dve, link, W_, p, i - 1, z)
                            elif z == 0:
                                W_(E_act, p + "io1")
                            link(dve.tensor_scalar(hat[z][i % 2], St[z], IO[z][:, cin:cin + 1], None, ALU.mult))
                            fire(p + f"h{i}{z}", dve.tensor_scalar(hatO[z], hat[z][i % 2], IO[z][:, cout:cout + 1], None, ALU.mult))
                        for z in range(2):
                            ch = chunk(z, i)
                            b, r = ch // 2, slice(64 * (ch % 2), 64 * (ch % 2) + 64)
                            W_(E_pe, p + f"r{i}{z}")
                            if i == 0:
                                W_(E_act, p + f"rvc{z}")
                            fire(p + f"rh{i}{z}", dve.tensor_tensor(RHS[z][r, :], k.ps[r, z, 0:P], RV[z][r, b * P:(b + 1) * P], ALU.add))
                    for z in range(2):
                        update(dve, link, W_, p, 3, z)
                    if ph == 0:
                        fire(p + "end", dve.tensor_copy(k.sm[:, 80:81], St[1][:, 0:1]))
                        continue
                    f0, f1 = flat(M[0]), flat(M[1])
                    y, d, rs = f0[:, 0:256], f0[:, 256:512], f1[:, 256:512]
                    link(dve.tensor_tensor(k2, k2, r_, ALU.mult))
                    fire(p + "rk", dve.tensor_scalar(flat(T1[0])[:, 0:256], k2, col(5), None, ALU.mult))
                    W_(E_act, p + "yc")
                    fire(p + "yy", dve.tensor_tensor(y, y, k.ps[:, 5, 0:256], ALU.add))
                    W_(E_pe, p + "mean")
                    fire(p + "yd", dve.scalar_tensor_tensor(d, k.ps[:, 2, 0:256], -1.0 / 64, y, ALU.mult, ALU.add))
                    W_(E_pe, p + "var")
                    fire(p + "yv", dve.tensor_scalar(rs, k.ps[:, 3, 0:256], 1.0 / 64, 64e-5, ALU.mult, ALU.add))
                    W_(E_act, p + "yrt")
                    link(dve.reciprocal(rs, rs))
                    link(dve.scalar_tensor_tensor(d, d, col(6), rs, ALU.mult, ALU.mult))
                    link(dve.tensor_tensor(y, k.ps[:, 2, 256:512], vx, ALU.mult))
                    link(dve.scalar_tensor_tensor(d, d, col(7), y, ALU.add, ALU.add))
                    dst = H[:, bass.ds(j, 1), LAT].rearrange("p a t -> p (a t)")
                    fire(p + "end", dve.tensor_tensor(dst, d, g_, ALU.mult))
                link.end_loop(TURNS)
            link.close()

    for E in (E_pe, E_dve, E_act, E_pool):
        E.close()

def block2_rwkv(k):
    both = slice(0, T)
    stage_ada2(k, 1)
    stage_norm2(k, 1, 0, both)
    stage_rwkv_project(k)
    stage_rwkv(k)
    Y = k.W[:, 11264:15360].rearrange("p (o t) -> p o t", o=KD)
    stage_square(k, LAT, Y)
    stage_post_norm(k, 1, 0, LAT, Y)
    stage_norm2(k, 1, 1, LAT)
    stage_conv_ffn(k, 1, LAT, Y)
    stage_post_norm(k, 1, 1, LAT, Y)


def stage_store(k, name, src):
    with k.nc.Block() as block:
        @block.sync
        def _(sp):
            sp.dma_start(k.a[name], src).then_inc(k.dma.sem, 16)
            sp.wait_ge(k.dma.sem, k.dma.at(16))
    k.dma.base += 16


def block1(k):
    gate = lambda i: (lambda o: k.mod1[:, i, 16 + o:17 + o])
    stage_ada1(k, 0, 2)
    stage_norm1(k, 0)
    stage_conv_in(k)
    stage_out_residual(k, gate(0))
    stage_norm1(k, 1)
    stage_swiglu(k, 1)
    stage_ada1(k, 2, 2)
    stage_norm1(k, 2)
    stage_attention(k)
    stage_out_residual(k, gate(2))
    stage_norm1(k, 3)
    moe = Moe(k)
    stage_router(k, moe)
    unit0 = stage_experts(k, moe, gate(3))
    stage_second_slots(k, moe, gate(3), unit0)
    stage_norm(k, LAT, lambda t, h: k.v("final_g", t), None, dst=k.X)


def build(nc, aps):
    k = Kernel(nc, aps)
    k.a["rkv"] = nc.dram_tensor("rkv", (KD, P, 3, T), F32, kind="Internal").ap()
    stage_load(k)
    block1(k)
    block2_even(k)
    block2_rwkv(k)
    stage_store(k, "out", k.X[:, :, LAT])


def tiles(w):
    kk, n = w.shape
    kp, np_ = -(-kk // P) * P, -(-n // P) * P
    if (kp, np_) != (kk, n):
        w = np.pad(w, ((0, kp - kk), (0, np_ - n)))
    return w.reshape(kp // P, P, np_ // P, P).transpose(2, 0, 1, 3)


def units(t):
    t = t.reshape(-1, P, P)
    pad = -len(t) % UT
    if pad:
        t = np.concatenate([t, np.zeros((pad, P, P), t.dtype)])
    return t.reshape(-1, UT, P, P).transpose(0, 2, 1, 3).reshape(-1, P, UT * P)


def moving(w):
    n = w.shape[1]
    np_ = -(-n // 256) * 256
    w = np.pad(w, ((0, 0), (0, np_ - n)))
    return w.reshape(KD, P, np_ // 256, 256).transpose(2, 1, 0, 3).reshape(-1, P, KD * 256)


def cols(v):
    return np.ascontiguousarray(v).reshape(-1, P).T


def swiglu_units(g, u, d):
    gu = np.stack([tiles(g), tiles(u)], axis=1).reshape(-1, P, P)
    return units(np.concatenate([gu, tiles(d).reshape(-1, P, P)]))


def constants():
    i = np.arange(P)
    out = [np.eye(P), np.ones((P, P))]
    rot = np.zeros((P, P))
    for m in range(P):
        rot[m + 32 if m % 64 < 32 else m - 32, m] = -1.0 if m % 64 < 32 else 1.0
    out.append(rot)
    s, t = i[:, None], i[None, :]
    fwd = [((s >> l) % 2 == 0) & ((t >> l) % 2 == 1) & (s >> (l + 1) == t >> (l + 1)) for l in range(7)]
    out += fwd + [m.T for m in fwd]
    out.append(s // 64 == t // 64)
    return np.concatenate([np.asarray(o, np.float32) for o in out], axis=1)


def layout(i):
    q, kx, v = np.split(i["attn_w_qkv"][0], 3, axis=1)
    pad64 = lambda w: np.pad(w, ((0, 0), (0, 64)))
    parts = [units(tiles(i["mod_w"][0, 0])), units(tiles(i["mod_w"][0, 1])),
             units(tiles(i["conv_w_in"][0])), units(tiles(i["conv_w_out"][0])),
             swiglu_units(i["ffn_w_gate"][0], i["ffn_w_up"][0], i["ffn_w_down"][0]),
             units(tiles(i["mod_w"][1, 0])), units(tiles(i["mod_w"][1, 1])),
             units(tiles(np.concatenate([pad64(q), pad64(kx)], axis=1))), moving(v),
             units(tiles(i["attn_w_o"][0]))]
    for e in range(NE):
        gu = np.stack([tiles(i["moe_w_gate"][0, e]), tiles(i["moe_w_up"][0, e])], axis=1)
        parts += [units(gu), i["moe_w_down"][0, e].reshape(KF // 2, 2, P, D).transpose(0, 2, 1, 3).reshape(-1, P, 2 * D)]
    vectors = np.zeros((P, NVEC), np.float32)

    def put(name, a):
        vectors[:, VEC[name]] = a
    put("c", cols(i["c"]))
    put("c2", np.stack([cols(i["c_ctx_2"]), cols(i["c_2"])], axis=2).reshape(P, 16))
    put("norm_g", cols(i["norm_g"]))
    put("mod_b", cols(i["mod_b"]))
    put("final_g", cols(i["final_g"]))
    put("conv_w", cols(i["conv_w"]))
    put("router", i["router_w"][0].reshape(KD, P, NE).transpose(1, 0, 2).reshape(P, -1))
    put("hmask", np.repeat(np.eye(2, dtype=np.float32), 64, axis=0))
    inv = np.float32(10000.0) ** (-np.arange(0, 64, 2, dtype=np.float32) / np.float32(64))
    put("invf", np.tile(inv, 4)[:, None])
    put("mod_b2", cols(i["b_mod_2"]))
    put("norm_g2", cols(i["norm_g_2"]))
    tok = lambda x: x.T.reshape(KD, P, S).transpose(1, 0, 2)
    w = i["ev_w_in_2"][0]
    at = np.cumsum([0, 512, 512, 512, 512, 16, 256, 256, 512, 512, 32])
    mq, mk, mv, mo, mg, gq, gk, gv, gg, glr = (w[:, a:b] for a, b in zip(at[:-1], at[1:]))
    glr_t, in_t, f_t = (np.zeros((D, P), np.float32) for _ in range(3))
    glr_t[:, 0:16], glr_t[:, 32:48] = glr[:, 0:16], glr[:, 16:32]
    bias = np.zeros((P, 2), np.float32)
    bg = i["ev_b_gates_2"][0]
    for z in range(2):
        in_t[:, 32 * z:32 * z + 4], f_t[:, 32 * z:32 * z + 4] = mg[:, 8 * z:8 * z + 4], mg[:, 8 * z + 4:8 * z + 8]
        bias[32 * z:32 * z + 4, 0], bias[32 * z:32 * z + 4, 1] = bg[8 * z:8 * z + 4], bg[8 * z + 4:8 * z + 8]
    up = lambda l: np.split(i["ffn_w_up_2"][l], 2, axis=1)
    parts += [units(tiles(i["w_mod_2"][0])),
              units(tiles(np.concatenate([mq, mk, gq, gk, glr_t, in_t, f_t, mo, gg], axis=1))),
              moving(np.concatenate([mv, gv], axis=1)),
              units(tiles(i["ev_w_out_2"][0])),
              swiglu_units(*up(0), i["ffn_w_down_2"][0])]
    h64 = lambda w: np.pad(w, ((0, 0), (0, 64)))
    parts += [units(tiles(i["w_mod_2"][1])),
              units(tiles(np.concatenate([i["rw_w_rkv_2"][0, 0], i["rw_w_rkv_2"][0, 1], i["rw_w_rkv_2"][0, 2],
                                          i["rw_w1_2"][0, 0], i["rw_w1_2"][0, 1], h64(i["rw_a1_2"][0]),
                                          i["rw_g1_2"][0]], axis=1))),
              units(tiles(i["rw_w_o_2"][0])),
              swiglu_units(*up(1), i["ffn_w_down_2"][1])]
    put("mu", cols(i["rw_mu_2"][0]))
    rw = np.zeros((KD, P, 520), np.float32)
    by_tile = lambda w: w.reshape(w.shape[0], KD, P).transpose(1, 0, 2)
    rw[:, 0:64, 0:128] = by_tile(i["rw_a2_2"][0])
    rw[:, 0:64, 128:256] = by_tile(i["rw_w2_2"][0, 0])
    rw[:, 64:128, 256:384] = by_tile(i["rw_w2_2"][0, 1])
    rw[:, :, 384:512] = by_tile(i["rw_g2_2"][0])
    for n, v in enumerate([*i["rw_w0_2"][0], i["rw_a0_2"][0], *i["rw_kvec_2"][0], *i["rw_lnx_2"][0]]):
        rw[:, :, 512 + n] = v.reshape(KD, P)
    u, t = np.arange(P)[:, None], np.arange(P)[None, :]
    own = u // CH == t // CH
    chunk_masks = np.concatenate([own & (u < t), own & (u <= t), own & (u > t), own & (u >= t)], axis=1).astype(np.float32)
    put("fcw", cols(i["ffn_conv_w_2"]))
    put("fcb", cols(i["ffn_conv_b_2"]))
    put("ecw", cols(i["ev_conv_w_2"][0]))
    put("ecb", cols(i["ev_conv_b_2"][0]))
    put("ebg", bias)
    put("glab", cols(i["ev_gla_b_2"][0]))
    put("headg", cols(i["ev_head_g_2"][0]))
    gw2 = np.zeros((P, 2, 256), np.float32)
    gw2[0:16, 0], gw2[32:48, 1] = i["ev_gla_w2_2"][0]
    t, s = np.arange(S)[:, None], np.arange(S)[None, :]
    scan = np.stack([(t <= s), (t >= s)]).astype(np.float32).reshape(2, 2, P, S).transpose(2, 0, 1, 3)
    mask = [np.where((t >= s) & ((t - s) % dil == 0) & (t - s <= win), 0.0, -1e30).reshape(2, P, S)
            for win, dil in GROUPS]
    return parts, {
        "vectors": vectors,
        "tokens": np.ascontiguousarray(np.concatenate([tok(i["ctx_2"][0]), tok(i["x"][0])], axis=2)),
        "constants": constants(),
        "scan_mask": np.ascontiguousarray(scan.reshape(P, -1)),
        "chunk_masks": chunk_masks,
        "rw_tiles": rw,
        "gla_w2": gw2.reshape(P, -1),
        "positions": np.ascontiguousarray(np.broadcast_to(i["positions"], (P, S))),
        "attn_mask": np.ascontiguousarray(np.concatenate(mask).transpose(1, 0, 2).astype(np.float32)),
    }


def kernel(**inputs):
    import concourse.bacc as bacc
    from concourse.bass_utils import run_bass_kernel_spmd
    parts, arrays = layout({n: np.asarray(a) for n, a in inputs.items()})
    arrays["weights"] = np.concatenate(parts)
    nc = bacc.Bacc("TRN2", target_bir_lowering=False, num_devices=1)
    aps = {n: nc.dram_tensor(n, a.shape, mybir.dt.from_np(a.dtype), kind="ExternalInput").ap() for n, a in arrays.items()}
    aps["out"] = nc.dram_tensor("out", (P, KD, S), F32, kind="ExternalOutput").ap()
    build(nc, aps)
    r = run_bass_kernel_spmd(nc, [arrays], core_ids=[0])
    got = r.results[0]["out"]
    return np.ascontiguousarray(got.transpose(1, 0, 2).reshape(D, S).T)[None]
```
